# Optimizing a Trainium2 kernel written in Bass

```python
import math
import jax, jax.numpy as jnp
from jax import lax
import numpy as np

D_MODEL = 1024
BATCH = 1
SEQ = 512
DEPTH = 1

POOL_WIDTH = D_MODEL // 2
POOL_WINDOWS = (2, 4, 8, 16)
POOL_GROUPS = len(POOL_WINDOWS)
POOL_GROUP_DIM = POOL_WIDTH // POOL_GROUPS
SSM_WIDTH = D_MODEL // 2
SSM_GROUP_DIM = 16
SSM_GROUPS = SSM_WIDTH // SSM_GROUP_DIM
SSM_STATE = 64
N_BRANCHES = 2
IN_WIDTH = POOL_WIDTH + SSM_WIDTH + N_BRANCHES * D_MODEL
MEM_LEN = 256
X_HEADS = 4
X_HEAD_DIM = D_MODEL // X_HEADS
N_EXPERT_GROUPS = 4
EXPERTS_PER_GROUP = 4
N_EXPERTS = N_EXPERT_GROUPS * EXPERTS_PER_GROUP
TOP_K_IN_GROUP = 2
D_EXPERT = 512
RMS_EPS = 1e-6
DT_MIN = 1e-3
DT_MAX = 1e-1

kernel_name = "hybrid_pool_s5_xattn_hmoe"

def rms_norm(x, g):
    xf = x.astype(jnp.float32)
    y = xf * lax.rsqrt(jnp.mean(xf * xf, axis=-1, keepdims=True) + RMS_EPS)
    return (y * g.astype(jnp.float32)).astype(x.dtype)

def pool_mixer(z, pool_w, pool_scale):
    b, s, _ = z.shape
    zf = z.astype(jnp.float32).reshape(b, s, POOL_GROUPS, POOL_GROUP_DIM)
    cs = jnp.cumsum(zf, axis=1)
    pos = jnp.arange(1, s + 1, dtype=jnp.float32)
    pooled = []
    for gi, w in enumerate(POOL_WINDOWS):
        c = cs[:, :, gi]
        lag = jnp.pad(c, ((0, 0), (w, 0), (0, 0)))[:, :s]
        cnt = jnp.minimum(pos, float(w))[:, None]
        pooled.append((c - lag) / cnt)
    pooled = jnp.stack(pooled, axis=2)
    mixed = jnp.einsum('bsgc,gcd->bsgd', pooled - zf, pool_w.astype(jnp.float32))
    out = mixed.reshape(b, s, POOL_WIDTH) * pool_scale.astype(jnp.float32)
    return out.astype(z.dtype)

def s5_ssm(v, a_re, a_im, log_dt, b_re, b_im, c_re, c_im, d_skip):
    bsz, s, _ = v.shape
    f32 = jnp.float32
    vf = v.astype(f32).reshape(bsz, s, SSM_GROUPS, SSM_GROUP_DIM)
    ar, ai = a_re.astype(f32), a_im.astype(f32)
    dt = jnp.exp(log_dt.astype(f32))[:, None]
    mag = jnp.exp(ar * dt)
    lb_re, lb_im = mag * jnp.cos(ai * dt), mag * jnp.sin(ai * dt)
    den = ar * ar + ai * ai
    nr, ni = lb_re - 1.0, lb_im
    f_re = ((nr * ar + ni * ai) / den)[..., None]
    f_im = ((ni * ar - nr * ai) / den)[..., None]
    br, bi = b_re.astype(f32), b_im.astype(f32)
    bb_re = f_re * br - f_im * bi
    bb_im = f_re * bi + f_im * br
    u_re = jnp.einsum('bsgc,gnc->sbgn', vf, bb_re)
    u_im = jnp.einsum('bsgc,gnc->sbgn', vf, bb_im)
    a_re_s = jnp.broadcast_to(lb_re, (s, 1, SSM_GROUPS, SSM_STATE))
    a_im_s = jnp.broadcast_to(lb_im, (s, 1, SSM_GROUPS, SSM_STATE))

    def combine(e1, e2):
        a1r, a1i, b1r, b1i = e1
        a2r, a2i, b2r, b2i = e2
        return (a1r * a2r - a1i * a2i,
                a1r * a2i + a1i * a2r,
                a2r * b1r - a2i * b1i + b2r,
                a2r * b1i + a2i * b1r + b2i)

    _, _, h_re, h_im = lax.associative_scan(combine, (a_re_s, a_im_s, u_re, u_im), axis=0)
    y = (jnp.einsum('sbgn,gcn->bsgc', h_re, c_re.astype(f32))
         - jnp.einsum('sbgn,gcn->bsgc', h_im, c_im.astype(f32)))
    y = y + d_skip.astype(f32).reshape(SSM_GROUPS, SSM_GROUP_DIM) * vf
    return y.reshape(bsz, s, SSM_WIDTH)

def memory_cross_attention(hn, memn, w_q, w_kv, w_o):
    b, s, _ = hn.shape
    m = memn.shape[1]
    q = (hn @ w_q).reshape(b, s, X_HEADS, X_HEAD_DIM)
    kv = memn @ w_kv
    k = kv[..., :D_MODEL].reshape(b, m, X_HEADS, X_HEAD_DIM)
    v = kv[..., D_MODEL:].reshape(b, m, X_HEADS, X_HEAD_DIM)
    scores = jnp.einsum('bshd,bmhd->bhsm', q.astype(jnp.float32), k.astype(jnp.float32)) * (X_HEAD_DIM ** -0.5)
    p = jax.nn.softmax(scores, axis=-1).astype(v.dtype)
    o = jnp.einsum('bhsm,bmhd->bshd', p, v).reshape(b, s, D_MODEL)
    return o @ w_o

def hierarchical_moe(zn, rg_w, rg_b, re_w, re_b, w1, w3, w2):
    b, s, d = zn.shape
    z = zn.reshape(b * s, d)
    f32 = jnp.float32
    g_logits = (z @ rg_w).astype(f32) + rg_b.astype(f32)
    g_prob = jax.nn.softmax(g_logits, axis=-1)
    g_idx = jnp.argmax(g_logits, axis=-1)
    g_gate = jnp.take_along_axis(g_prob, g_idx[:, None], axis=1)
    e_logits = jnp.einsum('td,dge->tge', z, re_w).astype(f32) + re_b.astype(f32)
    e_sel = jnp.take_along_axis(e_logits, g_idx[:, None, None], axis=1)[:, 0]
    top_v, top_i = lax.top_k(e_sel, TOP_K_IN_GROUP)
    top_w = jax.nn.softmax(top_v, axis=-1)
    e_w = jnp.sum(jax.nn.one_hot(top_i, EXPERTS_PER_GROUP, dtype=f32) * top_w[..., None], axis=1)
    comb = (jax.nn.one_hot(g_idx, N_EXPERT_GROUPS, dtype=f32)[:, :, None]
            * e_w[:, None, :] * g_gate[:, :, None]).reshape(-1, N_EXPERTS).astype(z.dtype)
    out = jnp.zeros_like(z)
    for e in range(N_EXPERTS):
        hid = jax.nn.silu(z @ w1[e]) * (z @ w3[e])
        out = out + comb[:, e:e + 1] * (hid @ w2[e])
    return out.reshape(b, s, d)

def setup_inputs(seed: int = 0) -> dict:
    key = jax.random.key(seed)
    ks = jax.random.split(key, 32)
    f32 = jnp.float32
    L, D = DEPTH, D_MODEL

    def nrm(k, shape, scale):
        return jax.random.normal(k, shape, f32) * scale

    def gain(k, shape):
        return 1.0 + 0.05 * jax.random.normal(k, shape, f32)

    n_idx = jnp.arange(SSM_STATE, dtype=f32)
    return {
        "x": jax.random.normal(ks[0], (BATCH, SEQ, D), f32),
        "mem": jax.random.normal(ks[1], (BATCH, MEM_LEN, D), f32),
        "norm_mix": gain(ks[2], (L, D)),
        "w_in": nrm(ks[3], (L, D, IN_WIDTH), D ** -0.5),
        "pool_w": nrm(ks[4], (L, POOL_GROUPS, POOL_GROUP_DIM, POOL_GROUP_DIM), POOL_GROUP_DIM ** -0.5),
        "pool_scale": gain(ks[5], (L, POOL_WIDTH)),
        "ssm_a_re": -0.5 + 0.01 * jax.random.normal(ks[6], (L, SSM_GROUPS, SSM_STATE), f32),
        "ssm_a_im": math.pi * n_idx + 0.01 * jax.random.normal(ks[7], (L, SSM_GROUPS, SSM_STATE), f32),
        "ssm_log_dt": jax.random.uniform(ks[8], (L, SSM_GROUPS), f32, math.log(DT_MIN), math.log(DT_MAX)),
        "ssm_b_re": nrm(ks[9], (L, SSM_GROUPS, SSM_STATE, SSM_GROUP_DIM), (2 * SSM_GROUP_DIM) ** -0.5),
        "ssm_b_im": nrm(ks[10], (L, SSM_GROUPS, SSM_STATE, SSM_GROUP_DIM), (2 * SSM_GROUP_DIM) ** -0.5),
        "ssm_c_re": nrm(ks[11], (L, SSM_GROUPS, SSM_GROUP_DIM, SSM_STATE), SSM_STATE ** -0.5),
        "ssm_c_im": nrm(ks[12], (L, SSM_GROUPS, SSM_GROUP_DIM, SSM_STATE), SSM_STATE ** -0.5),
        "ssm_d": nrm(ks[13], (L, SSM_WIDTH), 1.0),
        "glu_w": nrm(ks[14], (L, SSM_WIDTH, SSM_WIDTH), SSM_WIDTH ** -0.5),
        "glu_b": nrm(ks[15], (L, SSM_WIDTH), 0.02),
        "br_pool": nrm(ks[16], (L, POOL_WIDTH, D), POOL_WIDTH ** -0.5),
        "br_ssm": nrm(ks[17], (L, SSM_WIDTH, D), SSM_WIDTH ** -0.5),
        "w_out": nrm(ks[18], (L, D, D), D ** -0.5),
        "norm_x": gain(ks[19], (L, D)),
        "norm_mem": gain(ks[20], (L, D)),
        "x_wq": nrm(ks[21], (L, D, D), D ** -0.5),
        "x_wkv": nrm(ks[22], (L, D, 2 * D), D ** -0.5),
        "x_wo": nrm(ks[23], (L, D, D), D ** -0.5),
        "norm_ffn": gain(ks[24], (L, D)),
        "router_g_w": nrm(ks[25], (L, D, N_EXPERT_GROUPS), D ** -0.5),
        "router_g_b": nrm(ks[26], (L, N_EXPERT_GROUPS), 0.01),
        "router_e_w": nrm(ks[27], (L, D, N_EXPERT_GROUPS, EXPERTS_PER_GROUP), D ** -0.5),
        "router_e_b": nrm(ks[28], (L, N_EXPERT_GROUPS, EXPERTS_PER_GROUP), 0.01),
        "exp_w1": nrm(ks[29], (L, N_EXPERTS, D, D_EXPERT), D ** -0.5),
        "exp_w3": nrm(ks[30], (L, N_EXPERTS, D, D_EXPERT), D ** -0.5),
        "exp_w2": nrm(ks[31], (L, N_EXPERTS, D_EXPERT, D), D_EXPERT ** -0.5),
        "norm_final": gain(jax.random.fold_in(key, 99), (D,)),
    }

def reference(x, mem, norm_mix, w_in, pool_w, pool_scale, ssm_a_re, ssm_a_im, ssm_log_dt,
              ssm_b_re, ssm_b_im, ssm_c_re, ssm_c_im, ssm_d, glu_w, glu_b, br_pool, br_ssm,
              w_out, norm_x, norm_mem, x_wq, x_wkv, x_wo, norm_ffn, router_g_w, router_g_b,
              router_e_w, router_e_b, exp_w1, exp_w3, exp_w2, norm_final):
    h = x
    for l in range(DEPTH):
        u = rms_norm(h, norm_mix[l])
        proj = u @ w_in[l]
        z_pool = proj[..., :POOL_WIDTH]
        v_ssm = proj[..., POOL_WIDTH:POOL_WIDTH + SSM_WIDTH]
        gate_logits = proj[..., POOL_WIDTH + SSM_WIDTH:]
        y_pool = pool_mixer(z_pool, pool_w[l], pool_scale[l])
        y_s = s5_ssm(v_ssm, ssm_a_re[l], ssm_a_im[l], ssm_log_dt[l], ssm_b_re[l], ssm_b_im[l],
                     ssm_c_re[l], ssm_c_im[l], ssm_d[l])
        y_s = jax.nn.gelu(y_s)
        y_s = (y_s * jax.nn.sigmoid(y_s @ glu_w[l].astype(jnp.float32) + glu_b[l].astype(jnp.float32))).astype(h.dtype)
        gates = jax.nn.sigmoid(gate_logits.astype(jnp.float32)).astype(h.dtype)
        merged = gates[..., :D_MODEL] * (y_pool @ br_pool[l]) + gates[..., D_MODEL:] * (y_s @ br_ssm[l])
        h = h + merged @ w_out[l]
        h = h + memory_cross_attention(rms_norm(h, norm_x[l]), rms_norm(mem, norm_mem[l]),
                                       x_wq[l], x_wkv[l], x_wo[l])
        h = h + hierarchical_moe(rms_norm(h, norm_ffn[l]), router_g_w[l], router_g_b[l],
                                 router_e_w[l], router_e_b[l], exp_w1[l], exp_w3[l], exp_w2[l])
    return rms_norm(h, norm_final)


_drawn_inputs = setup_inputs


def setup_inputs(seed=0):
    import zlib

    import numpy as np

    out = dict(_drawn_inputs(seed))
    spreads = {}
    factors = {'ssm_a_re': 64.0,
     'ssm_b_re': 3.097,
     'ssm_b_im': 3.251,
     'ssm_c_re': 2.995,
     'ssm_c_im': 3.758,
     'glu_b': 8.0,
     'norm_x': 4.036,
     'norm_mem': 4.536,
     'router_g_b': 36.159,
     'router_e_b': 49.747,
     'norm_ffn': 5.125}
    for name, (base, spread) in spreads.items():
        noise = np.random.default_rng([zlib.crc32(name.encode()), seed]).standard_normal(out[name].shape)
        drawn = base * np.exp(spread * noise) if base else spread * noise
        out[name] = __import__('jax').numpy.asarray(drawn.astype(out[name].dtype))
    for name, factor in factors.items():
        out[name] = (out[name] * factor).astype(out[name].dtype)
    return out
```

```python
import math
from contextlib import ExitStack

import concourse.bass as bass
from concourse import mybir
from concourse.alu_op_type import AluOpType as ALU

P = 128
SEQ, D, MEM = 512, 1024, 256
NT, KD, MT = SEQ // P, D // P, MEM // P
HALF = 512
POOL_G, SSM_G, SSM_C, SSM_N = 4, 32, 16, 64
LCH = 8
NCH = SEQ // LCH
SUP = 8
HEADS, HD = 4, 256
NE, F = 16, 512
CAP = 96
N_OVER = (2 * SEQ) // CAP
N_TILES = NE + N_OVER
SLOTS = N_TILES * CAP
RING = 6
PADT = 16
EPS = 1e-6
BANKS = 8


def bass_hybrid_decoder_layer(nc: bass.Bass, x, mem, norm_mix, w_in, pool_w, pool_scale, ssm_a_re, ssm_a_im,
                              ssm_log_dt, ssm_b_re, ssm_b_im, ssm_c_re, ssm_c_im, ssm_d, glu_w, glu_b,
                              br_pool, br_ssm, w_out, norm_x, norm_mem, x_wq, x_wkv, x_wo, norm_ffn,
                              router_g_w, router_g_b, router_e_w, router_e_b, exp_w1, exp_w3, exp_w2,
                              norm_final, out):
    f32, i32 = mybir.dt.float32, mybir.dt.int32
    ACT, AX = mybir.ActivationFunctionType, mybir.AxisListType

    ctx = ExitStack()
    with ctx:
        def sb(name, shape, dt=f32):
            return ctx.enter_context(nc.sbuf_tensor(name, shape, dt))

        def sem(name):
            return ctx.enter_context(nc.semaphore(name))

        ring = sb("ring", [P, RING, 4096])
        hreg = sb("hreg", [P, 4096])
        ureg = sb("ureg", [P, 4096])
        greg = sb("greg", [P, 8192])
        kvreg = sb("kvreg", [P, 4096])
        areg = sb("areg", [P, 2048 + POOL_G * (PADT + SEQ)])
        zeros = areg[:, 0:4 * 7 * SSM_C]
        memreg = sb("memreg", [P, 2048])
        ident = sb("ident", [P, P])
        before = sb("before", [P, P])
        ones = sb("ones", [P, P])
        poolw = sb("poolw", [P, POOL_G, P])
        lam8 = sb("lam8", [P, 8, 2, SSM_G])
        cols = sb("cols", [P, 3 * KD + 4 * 3])
        cntinv = sb("cntinv", [P, POOL_G, PADT])
        rstat = sb("rstat", [P, 32])
        newton = sb("newton", [P, 2])
        soft = sb("soft", [P, 4, 4 * HEADS])

        gain_mix, gain_x, gain_mem = (cols[:, KD * i:KD * (i + 1)] for i in range(3))
        pscale, dskip, glub = (cols[:, 3 * KD + 4 * i:3 * KD + 4 * (i + 1)] for i in range(3))
        rmax, nmax, esum, rsum = (soft[:, i, :] for i in range(4))
        ss_x, rs_x = rstat[:, 0:4], rstat[:, 4:8]
        ss_m, rs_m = rstat[:, 8:10], rstat[:, 10:12]
        ss_h, rs_h = rstat[:, 12:16], rstat[:, 16:20]
        ss_z, rs_z = rstat[:, 20:24], rstat[:, 24:28]
        ss_o = rstat[:, 28:32]

        h = hreg[:, :].rearrange("p (t d) -> p t d", t=NT)
        cpow = hreg[:, :].rearrange("p (g k c) -> p g k c", g=SSM_G, k=LCH)
        cpow_m = hreg[:, :].rearrange("p (g m) -> p g m", g=SSM_G)
        yj = hreg[0:NCH, :].rearrange("p (m l c) -> p m l c", m=4, l=LCH)
        yj_g = hreg[0:NCH, :].rearrange("p (m l g c) -> p m g l c", m=4, l=LCH, c=SSM_C)
        uT = ureg[:, :].rearrange("p (k t) -> p k t", k=KD)
        mgT, qT, zT = uT, uT, uT
        G_lo, G_hi = greg[:, 0:4096], greg[:, 4096:8192]
        bpow = G_lo.rearrange("p (g m c) -> p g m c", g=SSM_G, m=LCH)
        bpow_m = G_lo.rearrange("p (g m) -> p g m", g=SSM_G)
        W = G_lo.rearrange("p (g x s j) -> p g x s j", g=SSM_G, x=2, s=SUP)
        hin = G_lo.rearrange("p (g x q) -> p g x q", g=SSM_G, x=2)
        lamg = [greg[0:SSM_G, 64 * i:64 * (i + 1)] for i in range(24)]
        lamq = greg[0:SSM_G, 1536:2048].rearrange("p (q x n) -> p q x n", q=4, x=2)
        cload = greg[:, 2048:2560].rearrange("p (t n) -> p t n", t=4)
        gtmp = greg[:, 4096:6144]
        gtmp_k = gtmp.rearrange("p (g k c) -> p g k c", g=SSM_G, k=4)
        mem_tok = greg[:, 6144:8192].rearrange("p (t d) -> p t d", t=MT)
        kern_sb = greg[0:SSM_C, 4096:8192].rearrange("p (g x) -> p g x", g=SSM_G)
        vch = greg[:, 4096:6144].rearrange("p (g q) -> p g q", g=SSM_G)
        stmp = greg[:, 6144:8192]
        gT = greg[:, :].rearrange("p (k t) -> p k t", k=16)
        hnT = G_lo.rearrange("p (k t) -> p k t", k=KD)
        oT = hnT
        xn = G_hi.rearrange("p (t d) -> p t d", t=NT)
        prob = G_hi[:, 0:2048].rearrange("p (b t m) -> p b t m", b=2, t=NT)
        probT = G_hi[:, 2048:4096].rearrange("p (b m t) -> p b m t", b=2, m=MT)
        B_s, B_w = kvreg[:, 0:512], kvreg[:, 512:1024]
        ptmp = kvreg[:, 0:2 * (PADT + SEQ)].rearrange("p (b t) -> p b t", b=2)
        o = 1088
        Bb, Bbw, Cy, Cw = (kvreg[:, o + 512 * i:o + 512 * (i + 1)] for i in range(4))
        pw = kvreg[:, o + 2048:o + 2560].rearrange("p (k x g) -> p k x g", k=LCH, x=2)
        lamL = kvreg[:, o + 2560:o + 2688].rearrange("p (q g) -> p q g", q=4)
        gc = lambda a: a.rearrange("p (g c) -> p g c", g=SSM_G)
        vj = kvreg[0:NCH, :].rearrange("p (g m c) -> p g m c", g=SSM_G, m=LCH)
        vj_m = kvreg[0:NCH, :].rearrange("p (g m) -> p g m", g=SSM_G)
        kT = kvreg[:, 0:2048].rearrange("p (k m) -> p k m", k=KD)
        vm = kvreg[:, 2048:4096].rearrange("p (t d) -> p t d", t=MT)
        vT = areg[:, 0:2048].rearrange("p (k t) -> p k t", k=4)
        zp = areg[:, 2048:].rearrange("p (k t) -> p k t", k=POOL_G)
        ypT, ysT = zp[:, :, PADT:], vT
        memT = memreg[:, :].rearrange("p (k t) -> p k t", k=KD)
        ygT = memreg[:, :].rearrange("p (k t) -> p k t", k=4)
        gain_ffn, gain_fin = memreg[:, 0:D], memreg[:, D:2 * D]

        rw = poolw[:, :, :].rearrange("p g d -> p (g d)")[:, 0:KD * 20].rearrange("p (k n) -> p k n", k=KD)
        rb = areg[:, 0:20]
        AR = areg
        def ar(at, n):
            return AR[:, at:at + n]
        logits = ar(32, 80).rearrange("p (t n) -> p t n", t=NT)
        lg, le = logits[:, :, 0:4], logits[:, :, 4:20]
        desc = ar(112, 4)
        r4 = [ar(120 + 4 * i, 4) for i in range(16)]
        q4 = [ar(200 + 16 * i, 16).rearrange("p (t n) -> p t n", t=NT) for i in range(10)]
        e64 = [ar(400 + 64 * i, 64).rearrange("p (t n) -> p t n", t=NT) for i in range(8)]
        x64 = ar(912, 64).rearrange("p (t n) -> p t n", t=NT)
        n16 = [ar(1000 + 16 * i, 16) for i in range(14)]
        tile_row = ar(1290, N_OVER + 1)
        slot_f = ar(1260, 8).rearrange("p (s t) -> p s t", s=2)
        base_id = ar(1270, 16)
        tok_id = sb("tok_id", [P, NT], i32)
        slot_i = sb("slot_i", [P, 2, NT], i32)
        tile_i = sb("tile_i", [P, N_OVER + 1], i32)
        idx_all = sb("idx_all", [CAP, N_TILES], i32)
        idx_one = sb("idx_one", [CAP, 1], i32)
        gw = sb("gw", [P, 2, NT])
        o = 0
        xg = [greg[0:CAP, D * a:D * (a + 1)] for a in range(2)]
        zsT = [greg[:, 2048 + 768 * a:2048 + 768 * (a + 1)].rearrange("p (k t) -> p k t", k=KD) for a in range(2)]
        silu = [greg[:, 3584 + 384 * a:3968 + 384 * a] for a in range(2)]
        hid = [greg[:, 4352 + 384 * a:4736 + 384 * a].rearrange("p (k t) -> p k t", k=4) for a in range(2)]
        ysb = [greg[0:CAP, 5120 + D * a:5120 + D * (a + 1)] for a in range(2)]
        yg1 = [kvreg[:, 2048 * a:2048 * a + D] for a in range(2)]
        yg2 = [kvreg[:, 2048 * a + D:2048 * a + 2 * D] for a in range(2)]

        bank = [ctx.enter_context(nc.psum_tensor(f"bank{i}", [P, HALF], f32)) for i in range(BANKS)]

        kern_d = nc.dram_tensor("kern_d", [SSM_G, SSM_C, 15 * SSM_C], f32, kind="Internal").ap()
        z_d = nc.dram_tensor("z_d", [SEQ, D], f32, kind="Internal").ap()
        inv_d = nc.dram_tensor("inv_d", [SLOTS, 1], i32, kind="Internal").ap()
        y_d = nc.dram_tensor("y_d", [SLOTS, D], f32, kind="Internal").ap()

        x_loaded = [sem(f"x_loaded{t}") for t in range(NT)]
        mem_loaded, cols_loaded, ssm_loaded = sem("mem_loaded"), sem("cols_loaded"), sem("ssm_loaded")
        ssmb_loaded, poolw_loaded = sem("ssmb_loaded"), sem("poolw_loaded")
        slot_loaded = [sem(f"slot_loaded{s}") for s in range(RING)]
        toep_loaded, kern_stored, zero_stored = sem("toep_loaded"), sem("kern_stored"), sem("zero_stored")
        consts_ready, masks_ready, tok_ready, counts_ready, index_ready = (sem(n) for n in ("consts_ready", "masks_ready", "tok_ready", "counts_ready", "index_ready"))
        psum_filled, act_drained, dve_drained = sem("psum_filled"), sem("act_drained"), sem("dve_drained")
        dve_step, act_step, pool_step = sem("dve_step"), sem("act_step"), sem("pool_step")
        x_squared, mem_squared, x_normed, mem_normed = sem("x_squared"), sem("mem_squared"), sem("x_normed"), sem("mem_normed")
        dt_ready, decay_ready, lam_ready, sines_ready = sem("dt_ready"), sem("decay_ready"), sem("lam_ready"), sem("sines_ready")
        bc_ready, angle_ready, powers_ready = sem("bc_ready"), sem("angle_ready"), sem("powers_ready")
        pool_diff, states_ready = sem("pool_diff"), sem("states_ready")
        gelu_ready, ys_ready, merged_ready = sem("gelu_ready"), sem("ys_ready"), sem("merged_ready")
        h_loaded, h_squared, h_normed = sem("h_loaded"), sem("h_squared"), sem("h_normed")
        neg_max, exp_done, prob_ready = sem("neg_max"), sem("exp_done"), sem("prob_ready")
        gains_loaded, z_squared, z_normed, z_stored = sem("gains_loaded"), sem("z_squared"), sem("z_normed"), sem("z_stored")
        router_loaded, g_shift, g_exp, e_shift, e_exp = sem("router_loaded"), sem("g_shift"), sem("g_exp"), sem("e_shift"), sem("e_exp")
        mask_ready, slots_ready, inv_zeroed, inv_stored, inv_loaded = sem("mask_ready"), sem("slots_ready"), sem("inv_zeroed"), sem("inv_stored"), sem("inv_loaded")
        idx_ready, pool_tick, rows_filled = sem("idx_ready"), sem("pool_tick"), sem("rows_filled")
        gathered = [sem(f"gathered{a}") for a in range(2)]
        xg_used, zs_ready, up_done, gate_done = sem("xg_used"), sem("zs_ready"), sem("up_done"), sem("gate_done")
        silu_ready, hid_ready, down_done = sem("silu_ready"), sem("hid_ready"), sem("down_done")
        y_dve, y_act = sem("y_dve"), sem("y_act")
        y_stored = [sem(f"y_stored{a}") for a in range(2)]
        o_idx, o_gath, o_w, o_xT, o_zs, o_up, o_gate = (sem(n) for n in ("o_idx", "o_gath", "o_w", "o_xT", "o_zs", "o_up", "o_gate"))
        o_silu, o_hid, o_down, o_y, o_stored, all_stored = (sem(n) for n in ("o_silu", "o_hid", "o_down", "o_y", "o_stored", "all_stored"))
        back = [sem(f"back{t}") for t in range(NT)]
        combined, o_squared, out_ready = sem("combined"), sem("o_squared"), sem("out_ready")
        out_stored = [sem(f"out_stored{t}") for t in range(NT)]

        ORDER = []

        def jobs(name, n, engine):
            ORDER.extend((name, i, engine) for i in range(n))

        jobs("xT", 8, "dve")
        jobs("memT", 4, "dve")
        jobs("lam", 1, "dve")
        jobs("cT", 1, "act")
        jobs("v", 4, "act")
        jobs("zp", 4, "act")
        jobs("bT", 8, "act")
        jobs("kern", 8, "act")
        jobs("vl", 8, "act")
        jobs("vch", 4, "act")
        jobs("st", 4, "act")
        jobs("mix", 4, "act")
        jobs("kk", 4, "act")
        jobs("vv", 4, "act")
        jobs("y", 8, "dve")
        ORDER.extend(("gate", i, "act") for i in range(4))
        jobs("yT", 4, "dve")
        ORDER.extend(("gate", i, "act") for i in range(4, 8))
        jobs("glu", 4, "act")
        ORDER.extend(("gate", i, "act") for i in range(8, 16))
        for m in range(KD):
            ORDER.extend((("bp", m, "dve"), ("bs", m, "dve")))
        for t in range(NT):
            ORDER.extend(("wo1", 2 * t + n, "dve") for n in range(2))
            if t >= 1:
                ORDER.extend(("hT", 2 * (t - 1) + n, "dve") for n in range(2))
        ORDER.extend(("hT", 6 + n, "dve") for n in range(2))
        jobs("q", 8, "act")
        for hd in range(HEADS + 1):
            if hd < HEADS:
                ORDER.extend(("sc", 2 * hd + n, "act") for n in range(2))
            if hd >= 1:
                ORDER.extend(("pT", 2 * (hd - 1) + n, "act") for n in range(2))
                ORDER.extend(("pv", 2 * (hd - 1) + n, "dve") for n in range(2))
        for t in range(NT):
            ORDER.extend(("wo2", 2 * t + n, "dve") for n in range(2))
            if t >= 1:
                ORDER.extend(("zT", 2 * (t - 1) + n, "act") for n in range(2))
        ORDER.extend(("zT", 6 + n, "act") for n in range(2))
        jobs("route", 1, "dve")
        jobs("rank", 1, "dve")
        AT = {(n, i): k for k, (n, i, _) in enumerate(ORDER)}
        counts, at = {"act": 0, "dve": 0}, []
        for _, _, e in ORDER:
            counts[e] += 1
            at.append((e, counts[e]))

        def filled(name, i):
            return AT[name, i] + 1

        def drained(name, i):
            e, n = at[AT[name, i]]
            return (act_drained if e == "act" else dve_drained), n

        def bank_of(name, i):
            return bank[AT[name, i] % BANKS]

        wcol = lambda w, c: w[0, :, HALF * c:HALF * (c + 1)].rearrange("(k p) n -> p k n", p=P)
        FRONT = [("v", wcol(w_in, 1), ("v", 3)), ("z", wcol(w_in, 0), ("zp", 3)),
                 ("k0", wcol(x_wkv, 0), ("kk", 1)), ("k1", wcol(x_wkv, 1), ("kk", 3)),
                 ("v0", wcol(x_wkv, 2), ("vv", 1)), ("v1", wcol(x_wkv, 3), ("vv", 3)),
                 ("toep", None, ("y", 7)), ("g0", wcol(w_in, 2), ("gate", 3)), ("g1", wcol(w_in, 3), ("gate", 7)),
                 ("glu", glu_w[0].rearrange("(k p) n -> p k n", p=P), ("glu", 3)),
                 ("g2", wcol(w_in, 4), ("gate", 11)), ("g3", wcol(w_in, 5), ("gate", 15)),
                 ("bp", br_pool[0].rearrange("(k p) n -> p k n", p=P), ("bp", 7)),
                 ("bs", br_ssm[0].rearrange("(k p) n -> p k n", p=P), ("bs", 7)),
                 ("o0", wcol(w_out, 0), ("wo1", 6)), ("o1", wcol(w_out, 1), ("wo1", 7)),
                 ("q0", wcol(x_wq, 0), ("q", 3)), ("q1", wcol(x_wq, 1), ("q", 7)),
                 ("w0", wcol(x_wo, 0), ("wo2", 6)), ("w1", wcol(x_wo, 1), ("wo2", 7))]
        NF = len(FRONT)
        CH = {n: i for i, (n, _, _) in enumerate(FRONT)}
        front_loads = [16 * sum(1 for i in range(NF) if i % RING == s and FRONT[i][0] != "toep") for s in range(RING)]

        def loaded(name):
            c = CH[name]
            if name == "toep":
                return toep_loaded, 16 * LCH
            return slot_loaded[c % RING], 16 * sum(1 for i in range(c % RING, c + 1, RING) if FRONT[i][0] != "toep")

        def chunk(name, k):
            return ring[:, CH[name] % RING, 0:(k * D if k == 4 and name != "glu" else k * HALF)].rearrange("p (k n) -> p k n", k=k)

        def expert_slot(e, c):
            return (NF + 3 * e + c) % RING

        def expert_chunk(slot, k):
            return ring[:, slot, :].rearrange("p (k n) -> p k n", k=k)

        w13 = (exp_w1[0].rearrange("e (k p) f -> e p k f", p=P), exp_w3[0].rearrange("e (k p) f -> e p k f", p=P))
        w2v = exp_w2[0].rearrange("e (k p) n -> e p k n", p=P)
        block = ctx.enter_context(nc.Block())

        @block.sync
        def _(sp):
            for t in range(NT):
                sp.dma_start(h[:, t, :], x[0, P * t:P * (t + 1), :]).then_inc(x_loaded[t], 16)
            for c, (name, src, _) in enumerate(FRONT):
                if c >= RING:
                    sp.wait_ge(psum_filled, filled(*FRONT[c - RING][2]))
                if name == "toep":
                    sp.wait_ge(kern_stored, 16)
                    sp.wait_ge(zero_stored, 16)
                    dst = ring[:, c % RING, :].rearrange("p (g x) -> p g x", g=SSM_G)
                    for m in range(LCH):
                        sp.dma_start(dst[SSM_C * m:SSM_C * (m + 1), :, :],
                                     kern_d[:, :, SSM_C * m:SSM_C * m + P].rearrange("g c x -> c g x")).then_inc(toep_loaded, 16)
                    continue
                if name == "glu":
                    for lo in range(0, N_OVER * CAP, SEQ):
                        n = min(SEQ, N_OVER * CAP - lo)
                        sp.dma_start(y_d[NE * CAP + lo:NE * CAP + lo + n, :], x[0, 0:n, :]).then_inc(rows_filled, 16)
                k = src.shape[1]
                dst = ring[:, c % RING, 0:k * src.shape[2]].rearrange("p (k n) -> p k n", k=k)
                sp.dma_start(dst, src).then_inc(slot_loaded[c % RING], 16)

            def load_expert(e, a, used):
                for c in range(3):
                    if used:
                        sp.wait_ge(*used[c])
                    s = expert_slot(a, c)
                    src = (w13[c] if c < 2 else w2v)[bass.ds(e, 1)].rearrange("e p k n -> p (e k) n")
                    sp.dma_start(expert_chunk(s, 8 if c < 2 else 4), src).then_inc(slot_loaded[s], 16)

            for a in range(2):
                load_expert(a, a, [(psum_filled, filled(*FRONT[NF - RING + 3 * a + c][2])) for c in range(3)])
            with sp.Fori(1, NE // 2) as i:
                for a in range(2):
                    load_expert(2 * i + a, a, [(up_done, 2 * i + a - 1), (gate_done, 2 * i + a - 1),
                                               (down_done, 4 * i + 2 * a - 2)])
            sp.wait_ge(slots_ready, 1)
            n_over = sp.value_load(tile_i[0:1, N_OVER:N_OVER + 1], min_val=0, max_val=N_OVER)
            with sp.If(n_over > 0):
                with sp.Fori(0, n_over) as k:
                    ex = sp.value_load(tile_i[0:1, bass.ds(k, 1)], min_val=0, max_val=NE - 1)
                    sp.wait_ge(down_done, 2 * NE)
                    sp.wait_ge(o_down, k + 1)
                    for c in range(3):
                        src = (w13[c] if c < 2 else w2v)[bass.ds(ex, 1)].rearrange("e p k n -> p (e k) n")
                        sp.dma_start(expert_chunk(c, 8 if c < 2 else 4), src).then_inc(o_w, 16)
                sp.nop()
            with sp.Else():
                sp.nop()

            for t in range(NT):
                sp.wait_ge(out_ready, t + 1)
                sp.dma_start(out[0, P * t:P * (t + 1), :], yg1[t % 2]).then_inc(out_stored[t], 16)
            for t in range(NT):
                sp.wait_ge(out_stored[t], 16)

        @block.gpsimd
        def _(pool):
            pool.memset(ident[:, :], 0.0).then_inc(pool_step, 1)
            pool.memset(before[:, :], 1.0).then_inc(pool_step, 1)
            pool.memset(ones[:, :], 1.0).then_inc(pool_step, 1)
            pool.wait_ge(pool_step, 3)
            pool.affine_select(out=ident[:, :], in_=ident[:, :], compare_op=ALU.not_equal, fill=1.0, base=0,
                               pattern=[[-1, P]], channel_multiplier=1).then_inc(consts_ready, 1)
            column = lambda a: a.rearrange("a (k p) -> p (a k)", p=P)
            for dst, src in ((gain_mix, norm_mix), (gain_x, norm_x), (gain_mem, norm_mem), (pscale, pool_scale),
                             (dskip, ssm_d), (glub, glu_b)):
                pool.dma_start(dst, column(src), allow_slow_non_contiguous=True).then_inc(cols_loaded, 16)
            pool.affine_select(out=before[:, :], in_=before[:, :], compare_op=ALU.is_gt, fill=0.0, base=0,
                               pattern=[[1, P]], channel_multiplier=-1).then_inc(masks_ready, 1)
            pool.dma_start(poolw[:, :, :], pool_w[0].rearrange("g c d -> c g d")).then_inc(poolw_loaded, 16)
            pool.iota(tok_id[:, :], pattern=[[P, NT]], base=0, channel_multiplier=1).then_inc(tok_ready, 1)
            pool.memset(zeros, 0.0).then_inc(pool_step, 1)
            pool.wait_ge(pool_step, 4)
            pool.dma_start(kern_d.rearrange("g c x -> (g c) x")[:, 0:7 * SSM_C].rearrange("(p r) x -> p r x", p=P),
                           zeros.rearrange("p (r x) -> p r x", r=4)).then_inc(zero_stored, 16)
            pool.dma_start(inv_d.rearrange("(p r) o -> p (r o)", p=CAP), zeros[0:CAP, 0:N_TILES].bitcast(i32)).then_inc(inv_zeroed, 16)
            for gi in range(POOL_G):
                w = 2 << gi
                for c in range(w - 1):
                    pool.memset(cntinv[:, gi, c:c + 1], 1.0 / (c + 1))
                ins = pool.memset(cntinv[:, gi, w - 1:], 1.0 / w)
            ins.then_inc(counts_ready, 1)
            pool.wait_ge(psum_filled, filled("mix", 3))
            pool.dma_start(rw[:, :, 0:4], router_g_w[0].rearrange("(k p) n -> p k n", p=P)).then_inc(router_loaded, 16)
            pool.dma_start(rw[:, :, 4:20], router_e_w[0].rearrange("(k p) g n -> p k (g n)", p=P)).then_inc(router_loaded, 16)
            pool.wait_ge(psum_filled, filled("yT", 3))
            pool.dma_start(h, x[0].rearrange("(t p) d -> p t d", p=P)).then_inc(h_loaded, 16)
            pool.wait_ge(psum_filled, filled("bs", 7))
            pool.wait_ge(ys_ready, 4)
            pool.dma_start(gain_ffn, norm_ffn.partition_broadcast(P).rearrange("p a d -> p (a d)")).then_inc(gains_loaded, 16)
            pool.dma_start(gain_fin, norm_final.partition_broadcast(P)).then_inc(gains_loaded, 16)
            pool.dma_start(rb[:, 0:4], router_g_b.partition_broadcast(P).rearrange("p a n -> p (a n)")).then_inc(gains_loaded, 16)
            pool.dma_start(rb[:, 4:20], router_e_b.partition_broadcast(P).rearrange("p a g n -> p (a g n)")).then_inc(gains_loaded, 16)
            for c in range(4):
                pool.memset(desc[:, c:c + 1], 4.0 - c)
            for c in range(NE):
                ins = pool.memset(base_id[:, c:c + 1], float(CAP * c))
            ins.then_inc(index_ready, 1)
            for t in range(NT):
                pool.wait_ge(z_normed, t + 1)
                pool.dma_start(z_d[P * t:P * (t + 1), :], xn[:, t, :]).then_inc(z_stored, 16)
            pool.wait_ge(slots_ready, 1)
            pool.wait_ge(tok_ready, 1)
            pool.wait_ge(inv_zeroed, 16)
            for s in range(2):
                for t in range(NT):
                    pool.indirect_dma_start(out=inv_d, out_offset=bass.IndirectOffsetOnAxis(ap=slot_i[:, s, t:t + 1], axis=0),
                                            in_=tok_id[:, t:t + 1], in_offset=None).then_inc(inv_stored, 16)
            pool.wait_ge(inv_stored, 16 * 2 * NT)
            pool.dma_start(idx_all[:, :], inv_d.rearrange("(e p) o -> p (e o)", p=CAP), allow_slow_non_contiguous=True).then_inc(inv_loaded, 16)
            pool.wait_ge(inv_loaded, 16)
            pool.wait_ge(z_stored, 16 * NT)

            def gather(e, a):
                pool.tensor_copy(idx_one[:, :], idx_all[:, bass.ds(e, 1)] if not isinstance(e, int) else idx_all[:, e:e + 1]).then_inc(idx_ready, 1)
                pool.wait_ge(idx_ready, e + 1)
                pool.sem_inc(pool_tick, 1)
                pool.indirect_dma_start(out=xg[a], out_offset=None, in_=z_d,
                                        in_offset=bass.IndirectOffsetOnAxis(ap=idx_one[:, :], axis=0)).then_inc(gathered[a], 16)
            gather(0, 0)
            pool.wait_ge(gathered[0], 16)
            gather(1, 1)
            pool.wait_ge(gathered[1], 16)
            with pool.Fori(1, NE // 2) as i:
                for a in range(2):
                    pool.wait_ge(xg_used, 2 * i + a - 1)
                    gather(2 * i + a, a)
                    pool.wait_ge(gathered[a], 16 * i + 16)
            n_over = pool.value_load(tile_i[0:1, N_OVER:N_OVER + 1], min_val=0, max_val=N_OVER)
            with pool.If(n_over > 0):
                with pool.Fori(0, n_over) as k:
                    pool.wait_ge(xg_used, NE)
                    pool.wait_ge(o_down, k + 1)
                    pool.tensor_copy(idx_one[:, :], idx_all[:, bass.ds(k + NE, 1)]).then_inc(o_idx, 1)
                    pool.wait_ge(o_idx, k + 1)
                    pool.sem_inc(pool_tick, 1)
                    pool.indirect_dma_start(out=xg[0], out_offset=None, in_=z_d,
                                            in_offset=bass.IndirectOffsetOnAxis(ap=idx_one[:, :], axis=0)).then_inc(o_gath, 16)
                    pool.wait_ge(o_gath, 16 * k + 16)
                pool.nop()
            with pool.Else():
                pool.nop()
            pool.wait_ge(all_stored, 1)
            pool.wait_ge(rows_filled, 32)
            for t in range(NT):
                if t >= 2:
                    pool.wait_ge(out_stored[t - 2], 16)
                pool.indirect_dma_start(out=yg1[t % 2], out_offset=None, in_=y_d,
                                        in_offset=bass.IndirectOffsetOnAxis(ap=slot_i[:, 0, t:t + 1], axis=0)).then_inc(back[t], 16)
                pool.indirect_dma_start(out=yg2[t % 2], out_offset=None, in_=y_d,
                                        in_offset=bass.IndirectOffsetOnAxis(ap=slot_i[:, 1, t:t + 1], axis=0)).then_inc(back[t], 16)

        @block.scalar
        def _(act):
            g = lamg
            act.dma_start(g[0], ssm_a_re[0]).then_inc(ssm_loaded, 16)
            act.dma_start(g[1], ssm_a_im[0]).then_inc(ssm_loaded, 16)
            act.dma_start(g[2][:, 0:1], ssm_log_dt.rearrange("a g -> g a"), allow_slow_non_contiguous=True).then_inc(ssm_loaded, 16)
            act.dma_start(cload[:, :, 0:64], ssm_c_re[0].rearrange("(t g) c n -> (g c) t n", t=4)).then_inc(ssmb_loaded, 16)
            act.dma_start(cload[:, :, 64:128], ssm_c_im[0].rearrange("(t g) c n -> (g c) t n", t=4)).then_inc(ssmb_loaded, 16)
            act.dma_start(gc(B_s)[0:64], ssm_b_re[0].rearrange("g n c -> n g c")).then_inc(ssmb_loaded, 16)
            act.dma_start(gc(B_s)[64:128], ssm_b_im[0].rearrange("g n c -> n g c")).then_inc(ssmb_loaded, 16)
            act.dma_start(mem_tok, mem[0].rearrange("(t p) d -> p t d", p=P)).then_inc(mem_loaded, 16)
            steps = [0]

            def link(ins):
                steps[0] += 1
                ins.then_inc(act_step, 1)
                act.wait_ge(act_step, steps[0])

            act.wait_ge(ssm_loaded, 48)
            link(act.activation(g[2][:, 1:2], g[2][:, 0:1], ACT.Exp))
            act.activation(g[3], g[0], ACT.Exp, scale=g[2][:, 1:2]).then_inc(decay_ready, 1)
            for t in range(NT):
                act.wait_ge(x_loaded[t], 16)
                if t:
                    act.wait_ge(x_squared, t)
                act.activation(ureg[:, 0:D], h[:, t, :], ACT.Square, scale=1 / 32, accum_out=ss_x[:, t:t + 1]).then_inc(x_squared, 1)
            act.wait_ge(mem_loaded, 16)
            for t in range(MT):
                act.wait_ge(mem_squared, t) if t else act.wait_ge(x_squared, NT)
                act.activation(ureg[:, 0:D], mem_tok[:, t, :], ACT.Square, scale=1 / 32, accum_out=ss_m[:, t:t + 1]).then_inc(mem_squared, 1)
            act.wait_ge(angle_ready, 2)
            act.activation(g[6], g[4], ACT.Sin)
            act.activation(g[7], g[5], ACT.Sin, scale=0.5).then_inc(sines_ready, 1)

            act.wait_ge(psum_filled, filled("cT", 0))
            b = bank_of("cT", 0)
            act.activation(Cy[0:64], b[0:64, :], ACT.Copy)
            act.activation(Cy[64:128], b[64:128, :], ACT.Copy, scale=-1.0)
            act.activation(Cw[0:64], b[64:128, :], ACT.Copy, scale=-1.0)
            act.activation(Cw[64:128], b[0:64, :], ACT.Copy, scale=-1.0).then_inc(act_drained, 1)
            act.wait_ge(zero_stored, 16)
            act.wait_ge(inv_zeroed, 16)
            for m in range(4):
                act.wait_ge(psum_filled, filled("v", m))
                act.activation(vT[:, m, :], bank_of("v", m)[:, :], ACT.Copy).then_inc(act_drained, 1)
            for m in range(4):
                act.wait_ge(psum_filled, filled("zp", m))
                act.activation(zp[:, m, PADT:], bank_of("zp", m)[:, :], ACT.Copy).then_inc(act_drained, 1)
            for q in range(8):
                act.wait_ge(psum_filled, filled("bT", q))
                act.activation(bpow_m[:, 4 * q:4 * q + 4, :], bank_of("bT", q)[:, :].rearrange("p (g m) -> p g m", g=4),
                               ACT.Copy).then_inc(act_drained, 1)
            for q in range(8):
                act.wait_ge(psum_filled, filled("kern", q))
                act.activation(kern_sb[:, 4 * q:4 * q + 4, :], bank_of("kern", q)[0:SSM_C, :].rearrange("p (g m) -> p g m", g=4),
                               ACT.Copy).then_inc(act_drained, 1)
            act.wait_ge(*drained("kern", 7))
            act.dma_start(kern_d[:, :, 7 * SSM_C:].rearrange("g c x -> c g x"), kern_sb).then_inc(kern_stored, 16)
            act.wait_ge(pool_diff, POOL_G)
            for l in range(LCH):
                act.wait_ge(psum_filled, filled("vl", l))
                act.activation(vj[:, :, LCH - 1 - l, :], bank_of("vl", l)[0:NCH, :].rearrange("p (g c) -> p g c", g=SSM_G),
                               ACT.Copy).then_inc(act_drained, 1)
            act.wait_ge(kern_stored, 16)
            for q in range(4):
                act.wait_ge(psum_filled, filled("vch", q))
                act.activation(vch[:, 8 * q:8 * q + 8, :], bank_of("vch", q)[:, :].rearrange("p (g q) -> p g q", g=8),
                               ACT.Copy).then_inc(act_drained, 1)
            for q in range(4):
                act.wait_ge(psum_filled, filled("st", q))
                b = bank_of("st", q)[:, :].rearrange("p (g q) -> p g q", g=8)
                gs = slice(8 * q, 8 * q + 8)
                act.activation(hin[:, gs, 0, :], b, ACT.Copy)
                act.activation(hin[0:64, gs, 1, :], b[64:128], ACT.Copy, scale=-1.0)
                act.activation(hin[64:128, gs, 1, :], b[0:64], ACT.Copy).then_inc(act_drained, 1)
            act.wait_ge(cols_loaded, 96)
            for g_ in range(4):
                act.wait_ge(psum_filled, filled("mix", g_))
                act.activation(ypT[:, g_, :], bank_of("mix", g_)[:, :], ACT.Copy, scale=pscale[:, g_:g_ + 1]).then_inc(act_drained, 1)
            for m in range(4):
                act.wait_ge(psum_filled, filled("kk", m))
                act.activation(kT[:, 2 * m:2 * m + 2, :], bank_of("kk", m)[:, :].rearrange("p (k m) -> p k m", k=2),
                               ACT.Copy).then_inc(act_drained, 1)
            for n in range(4):
                act.wait_ge(psum_filled, filled("vv", n))
                act.activation(vm[:, n % 2, HALF * (n // 2):HALF * (n // 2 + 1)], bank_of("vv", n)[:, :],
                               ACT.Copy).then_inc(act_drained, 1)

            def gates(lo, hi):
                for m in range(lo, hi):
                    act.wait_ge(psum_filled, filled("gate", m))
                    act.activation(gT[:, m, :], bank_of("gate", m)[:, :], ACT.Sigmoid).then_inc(act_drained, 1)

            gates(0, 4)
            gates(4, 8)
            for m in range(4):
                act.wait_ge(*drained("yT", m))
                act.activation(ygT[:, m, :], vT[:, m, :], ACT.Gelu_apprx_tanh).then_inc(gelu_ready, 1)
            for m in range(4):
                act.wait_ge(psum_filled, filled("glu", m))
                act.activation(vT[:, m, :], bank_of("glu", m)[:, :], ACT.Sigmoid, bias=glub[:, m:m + 1]).then_inc(act_drained, 1)
            gates(8, 16)
            for t in range(NT):
                act.wait_ge(*drained("wo1", 2 * t + 1))
                act.activation(xn[:, t, :], h[:, t, :], ACT.Square, scale=1 / 32, accum_out=ss_h[:, t:t + 1]).then_inc(h_squared, 1)
            for m in range(8):
                act.wait_ge(psum_filled, filled("q", m))
                act.activation(qT[:, m, :], bank_of("q", m)[:, :], ACT.Copy).then_inc(act_drained, 1)

            def probs(hd):
                for n in range(2):
                    act.wait_ge(neg_max, 2 * hd + n + 1)
                    if hd >= 2 and n == 0:
                        act.wait_ge(psum_filled, filled("pT", 2 * hd - 3))
                    b = bank_of("sc", 2 * hd + n)[:, :].rearrange("p (t m) -> p t m", t=2)
                    for s in range(2):
                        t = 2 * n + s
                        ins = act.activation(prob[:, hd % 2, t, :], b[:, s, :], ACT.Exp, scale=HD ** -0.5,
                                             bias=nmax[:, 4 * hd + t:4 * hd + t + 1], accum_out=esum[:, 4 * hd + t:4 * hd + t + 1])
                    ins.then_inc(act_drained, 1)

            for hd in range(HEADS + 1):
                if hd < HEADS:
                    probs(hd)
                if hd >= 1:
                    for n in range(2):
                        act.wait_ge(psum_filled, filled("pT", 2 * (hd - 1) + n))
                        act.activation(probT[:, (hd - 1) % 2, n, :], bank_of("pT", 2 * (hd - 1) + n)[:, :], ACT.Copy).then_inc(act_drained, 1)

            def z_transposed(t):
                for n in range(2):
                    act.wait_ge(psum_filled, filled("zT", 2 * t + n))
                    act.activation(zT[:, 4 * n:4 * n + 4, P * t:P * (t + 1)],
                                   bank_of("zT", 2 * t + n)[:, :].rearrange("p (k t) -> p k t", k=4), ACT.Copy).then_inc(act_drained, 1)

            for t in range(NT):
                act.wait_ge(*drained("wo2", 2 * t + 1))
                if t == 0:
                    act.wait_ge(psum_filled, filled("pv", 7))
                act.activation(xn[:, t, :], h[:, t, :], ACT.Square, scale=1 / 32, accum_out=ss_z[:, t:t + 1]).then_inc(z_squared, 1)
                if t >= 1:
                    z_transposed(t - 1)
            z_transposed(NT - 1)
            act.wait_ge(g_shift, 1)
            act.activation(q4[0], q4[1], ACT.Exp).then_inc(g_exp, 1)
            act.wait_ge(e_shift, 1)
            act.activation(r4[1], r4[2], ACT.Exp).then_inc(e_exp, 1)

            act.sem_inc(silu_ready, 2)
            act.sem_inc(y_act, 1)

            def expert(e, a, n_st):
                act.wait_ge(up_done, e + 1)
                act.wait_ge(hid_ready, e + 1)
                act.activation(silu[a], bank[2 + 4 * a][:, 0:4 * CAP], ACT.Silu).then_inc(silu_ready, 1)
                act.wait_ge(down_done, 2 * e + 2)
                if n_st is not None:
                    act.wait_ge(y_stored[a], n_st)
                act.activation(ysb[a][:, HALF:D], bank[5][0:CAP, :], ACT.Copy).then_inc(y_act, 1)
                act.wait_ge(y_act, e + 2)
                act.wait_ge(y_dve, e + 2)
                act.dma_start(y_d[bass.ds(e * CAP, CAP), :], ysb[a]).then_inc(y_stored[a], 16)

            expert(0, 0, None)
            expert(1, 1, None)
            with act.Fori(1, NE // 2) as i:
                for a in range(2):
                    expert(2 * i + a, a, 16 * i)
            act.wait_ge(y_stored[0], 8 * NE)
            act.wait_ge(y_stored[1], 8 * NE)
            n_over = act.value_load(tile_i[0:1, N_OVER:N_OVER + 1], min_val=0, max_val=N_OVER)
            with act.If(n_over > 0):
                act.wait_ge(rows_filled, 32)
                with act.Fori(0, n_over) as k:
                    act.wait_ge(o_up, k + 1)
                    act.activation(silu[0], bank[2][:, 0:4 * CAP], ACT.Silu).then_inc(o_silu, 1)
                    act.wait_ge(o_y, k + 1)
                    act.dma_start(y_d[bass.ds((k + NE) * CAP, CAP), :], ysb[0]).then_inc(o_stored, 16)
                    act.wait_ge(o_stored, 16 * k + 16)
                act.nop()
            with act.Else():
                act.nop()
            act.sem_inc(all_stored, 1)
            for t in range(NT):
                act.wait_ge(combined, t + 1)
                if t:
                    act.wait_ge(o_squared, t)
                act.activation(ureg[:, 0:D], h[:, t, :], ACT.Square, scale=1 / 32, accum_out=ss_o[:, t:t + 1]).then_inc(o_squared, 1)

        @block.vector
        def _(dve):
            V = nc.vector
            steps = [0]

            def link(ins):
                steps[0] += 1
                ins.then_inc(dve_step, 1)
                dve.wait_ge(dve_step, steps[0])

            def tt(o_, a, b, op):
                return V.tensor_tensor(out=o_, in0=a, in1=b, op=op)

            def ts(o_, a, s1, op0, s2=None, op1=None):
                if op1 is None:
                    return V.tensor_scalar(o_, a, s1, None, op0)
                return V.tensor_scalar(o_, a, s1, s2, op0, op1)

            def rstd(o_, ss):
                v, t_ = newton[:, 0:1], newton[:, 1:2]
                link(ts(v, ss, EPS, ALU.add))
                link(ts(t_.bitcast(i32), v.bitcast(i32), 1, ALU.logical_shift_right))
                link(ts(o_.bitcast(i32), t_.bitcast(i32), -1.0, ALU.mult, float(0x5F3759DF), ALU.add))
                for _ in range(3):
                    link(tt(t_, o_, o_, ALU.mult))
                    link(V.scalar_tensor_tensor(out=t_, in0=t_, scalar=-0.5, in1=v, op0=ALU.mult, op1=ALU.mult))
                    link(V.scalar_tensor_tensor(out=o_, in0=t_, scalar=1.5, in1=o_, op0=ALU.add, op1=ALU.mult))

            for t in range(NT):
                dve.wait_ge(x_squared, t + 1)
                rstd(rs_x[:, t:t + 1], ss_x[:, t:t + 1])
                ts(h[:, t, :], h[:, t, :], rs_x[:, t:t + 1], ALU.mult).then_inc(x_normed, 1)
            for t in range(MT):
                dve.wait_ge(mem_squared, t + 1)
                rstd(rs_m[:, t:t + 1], ss_m[:, t:t + 1])
                ts(mem_tok[:, t, :], mem_tok[:, t, :], rs_m[:, t:t + 1], ALU.mult).then_inc(mem_normed, 1)

            g = lamg
            TWO_PI = 2 * math.pi
            c1 = 6.28125
            c2 = float(int((TWO_PI - c1) * 2 ** 22)) / 2 ** 22
            c3 = TWO_PI - c1 - c2
            MAGIC = 1.5 * 2.0 ** 23
            dve.wait_ge(decay_ready, 1)
            link(ts(g[8], g[1], g[2][:, 1:2], ALU.mult))
            link(ts(g[9], g[8], 1 / TWO_PI, ALU.mult, MAGIC, ALU.add))
            link(ts(g[9], g[9], MAGIC, ALU.subtract))
            for c in (c1, c2, c3):
                link(V.scalar_tensor_tensor(out=g[8], in0=g[9], scalar=-c, in1=g[8], op0=ALU.mult, op1=ALU.add))
            ts(g[4], g[8], 3.1415925, ALU.min, -3.1415925, ALU.max).then_inc(angle_ready, 1)
            ts(g[5], g[8], 3.1415925, ALU.min, -3.1415925, ALU.max).then_inc(angle_ready, 1)
            dve.wait_ge(sines_ready, 1)
            link(tt(g[10], g[7], g[7], ALU.mult))
            link(ts(g[10], g[10], -2.0, ALU.mult, 1.0, ALU.add))
            link(tt(g[11], g[3], g[10], ALU.mult))
            link(tt(g[12], g[3], g[6], ALU.mult))
            link(tt(g[13], g[0], g[0], ALU.mult))
            link(tt(g[14], g[1], g[1], ALU.mult))
            link(tt(g[13], g[13], g[14], ALU.add))
            link(V.reciprocal(g[13], g[13]))
            link(ts(g[15], g[11], 1.0, ALU.subtract))
            link(tt(g[16], g[15], g[0], ALU.mult))
            link(tt(g[17], g[12], g[1], ALU.mult))
            link(tt(g[16], g[16], g[17], ALU.add))
            link(tt(g[18], g[12], g[0], ALU.mult))
            link(tt(g[19], g[15], g[1], ALU.mult))
            link(tt(g[18], g[18], g[19], ALU.subtract))
            link(tt(g[16], g[16], g[13], ALU.mult))
            link(tt(g[18], g[18], g[13], ALU.mult))
            for n, s in enumerate((11, 12, 16, 18)):
                ins = V.tensor_copy(lamq[:, n, :, :], g[s].unsqueeze(1).to_broadcast([SSM_G, 2, SSM_N]))
            ins.then_inc(lam_ready, 1)

            dve.wait_ge(cols_loaded, 96)

            def transposed(name, i, dst, gain):
                dve.wait_ge(psum_filled, filled(name, i))
                tt(dst, bank_of(name, i)[:, :].rearrange("p (k t) -> p k t", k=4), gain.unsqueeze(2).to_broadcast([P, 4, P]),
                   ALU.mult).then_inc(dve_drained, 1)

            dve.wait_ge(mem_squared, MT)
            for i in range(8):
                t, n = i // 2, i % 2
                transposed("xT", i, uT[:, 4 * n:4 * n + 4, P * t:P * (t + 1)], gain_mix[:, 4 * n:4 * n + 4])
            for i in range(4):
                t, n = i // 2, i % 2
                transposed("memT", i, memT[:, 4 * n:4 * n + 4, P * t:P * (t + 1)], gain_mem[:, 4 * n:4 * n + 4])
            dve.wait_ge(psum_filled, filled("lam", 0))
            V.tensor_copy(lamL, bank_of("lam", 0)[:, 0:4 * SSM_G].rearrange("p (q g) -> p q g", q=4)).then_inc(dve_drained, 1)
            dve.wait_ge(*drained("lam", 0))
            LR, LI, FR, FI = (lamL[:, n, :] for n in range(4))
            over_c = lambda a: a.unsqueeze(2).to_broadcast([P, SSM_G, SSM_C])
            dve.wait_ge(ssmb_loaded, 64)

            def swapped(dst, src):
                link(ts(dst[0:64], src[64:128], -1.0, ALU.mult))
                link(V.tensor_copy(dst[64:128], src[0:64]))

            swapped(B_w, B_s)
            t1 = gtmp[:, 0:512]
            link(tt(gc(Bb), gc(B_s), over_c(FR), ALU.mult))
            link(tt(gc(t1), gc(B_w), over_c(FI), ALU.mult))
            link(tt(Bb, Bb, t1, ALU.add))
            swapped(Bbw, Bb)

            def powers(dst, base_r, base_i, tmp_at):
                link(V.tensor_copy(dst[:, 0, 0, :], base_r))
                link(V.tensor_copy(dst[:, 0, 1, :], base_i))
                n = 1
                while n < 8:
                    lo = dst[:, 0:n]
                    br = dst[:, n - 1, 0, :].unsqueeze(1).to_broadcast([P, n, SSM_G])
                    bi = dst[:, n - 1, 1, :].unsqueeze(1).to_broadcast([P, n, SSM_G])
                    tmp = tmp_at[:, 0:n * SSM_G].rearrange("p (k g) -> p k g", k=n)
                    hi = dst[:, n:2 * n]
                    link(tt(hi[:, :, 0, :], lo[:, :, 0, :], br, ALU.mult))
                    link(tt(tmp, lo[:, :, 1, :], bi, ALU.mult))
                    link(tt(hi[:, :, 0, :], hi[:, :, 0, :], tmp, ALU.subtract))
                    link(tt(hi[:, :, 1, :], lo[:, :, 0, :], bi, ALU.mult))
                    link(tt(tmp, lo[:, :, 1, :], br, ALU.mult))
                    link(tt(hi[:, :, 1, :], hi[:, :, 1, :], tmp, ALU.add))
                    n *= 2

            powers(pw, LR, LI, gtmp[:, 512:640])
            dve.wait_ge(*drained("cT", 0))
            link(V.tensor_copy(bpow[:, :, 0, :], gc(Bb)))

            def scaled(dst, a, b, lo, n):
                four = [P, SSM_G, n, SSM_C]
                bc = lambda v: gc(v).unsqueeze(2).to_broadcast(four)
                pr, pi = (pw[:, lo:lo + n, x_, :].rearrange("p k g -> p g k").unsqueeze(3).to_broadcast(four) for x_ in range(2))
                tmp = gtmp_k[:, :, 0:n, :]
                link(tt(dst, bc(a), pr, ALU.mult))
                link(tt(tmp, bc(b), pi, ALU.mult))
                return tt(dst, dst, tmp, ALU.add)

            link(scaled(bpow[:, :, 1:5, :], Bb, Bbw, 0, 4))
            link(scaled(bpow[:, :, 5:8, :], Bb, Bbw, 4, 3))
            link(scaled(cpow[:, :, 0:4, :], Cy, Cw, 0, 4))
            scaled(cpow[:, :, 4:8, :], Cy, Cw, 4, 4).then_inc(powers_ready, 1)
            powers(lam8, pw[:, 7, 0, :], pw[:, 7, 1, :], B_s)

            for b in range(2):
                link(V.memset(ptmp[:, b, 0:PADT], 0.0))
            link(V.memset(zp[:, :, 0:PADT], 0.0))
            dve.wait_ge(counts_ready, 1)
            for gi in range(POOL_G):
                dve.wait_ge(*drained("zp", gi))
                src, w = zp[:, gi, :], 1
                for s in range(gi + 1):
                    dst = ptmp[:, s % 2, :]
                    link(tt(dst[:, PADT:], src[:, PADT:], src[:, PADT - w:PADT + SEQ - w], ALU.add))
                    src, w = dst, 2 * w
                link(V.scalar_tensor_tensor(out=zp[:, gi, 2 * PADT:], in0=src[:, 2 * PADT:], scalar=1.0 / w,
                                            in1=zp[:, gi, 2 * PADT:], op0=ALU.mult, op1=ALU.subtract))
                link(tt(src[:, PADT:2 * PADT], src[:, PADT:2 * PADT], cntinv[:, gi, :], ALU.mult))
                ins = tt(zp[:, gi, PADT:2 * PADT], src[:, PADT:2 * PADT], zp[:, gi, PADT:2 * PADT], ALU.subtract)
                ins.then_inc(pool_diff, 1)
                dve.wait_ge(pool_diff, gi + 1)

            dve.wait_ge(*drained("st", 3))
            A1 = stmp[:, 0:512].rearrange("p (g x s) -> p g x s", g=SSM_G, x=2)
            A2 = stmp[:, 512:1024].rearrange("p (g x s) -> p g x s", g=SSM_G, x=2)
            S = stmp[:, 1024:1536].rearrange("p (g x s) -> p g x s", g=SSM_G, x=2)
            l8r, l8i = lam8[:, 0, 0, :], lam8[:, 0, 1, :]
            gxs = [P, SSM_G, 2, SUP]
            for j in range(1, SUP):
                old, new = W[:, :, :, :, j - 1], W[:, :, :, :, j]
                link(tt(A1, old, l8r.unsqueeze(2).unsqueeze(3).to_broadcast(gxs), ALU.mult))
                im = l8i.unsqueeze(2).to_broadcast([P, SSM_G, SUP])
                link(tt(A2[:, :, 0, :], old[:, :, 1, :], im, ALU.mult))
                link(V.scalar_tensor_tensor(out=A2[:, :, 1, :], in0=old[:, :, 0, :], scalar=-1.0, in1=im, op0=ALU.mult, op1=ALU.mult))
                link(tt(A1, A1, A2, ALU.add))
                link(tt(new, new, A1, ALU.add))
            link(V.memset(S[:, :, :, 0], 0.0))
            l64r, l64i = lam8[:, 7, 0, :], lam8[:, 7, 1, :]
            for s in range(SUP - 1):
                old, new = S[:, :, :, s], S[:, :, :, s + 1]
                link(tt(A1[:, :, :, 0], old, l64r.unsqueeze(2).to_broadcast([P, SSM_G, 2]), ALU.mult))
                link(tt(A2[:, :, 0, 0], old[:, :, 1], l64i, ALU.mult))
                link(V.scalar_tensor_tensor(out=A2[:, :, 1, 0], in0=old[:, :, 0], scalar=-1.0, in1=l64i, op0=ALU.mult, op1=ALU.mult))
                link(tt(A1[:, :, :, 0], A1[:, :, :, 0], A2[:, :, :, 0], ALU.add))
                link(tt(new, A1[:, :, :, 0], W[:, :, :, s, SUP - 1], ALU.add))
            Hn = W[:, :, 1, :, :]
            link(V.tensor_copy(Hn[:, :, :, 0], S[:, :, 0, :]))
            for j in range(1, SUP):
                pr, pi = (lam8[:, j - 1, x_, :].unsqueeze(2).to_broadcast([P, SSM_G, SUP]) for x_ in range(2))
                B1, B2 = A1[:, :, 0, :], A2[:, :, 0, :]
                link(tt(B1, S[:, :, 0, :], pr, ALU.mult))
                link(tt(B2, S[:, :, 1, :], pi, ALU.mult))
                link(tt(B1, B1, B2, ALU.add))
                ins = tt(Hn[:, :, :, j], B1, W[:, :, 0, :, j - 1], ALU.add)
                if j < SUP - 1:
                    link(ins)
            ins.then_inc(states_ready, 1)
            for q in range(8):
                dve.wait_ge(psum_filled, filled("y", q | 1))
                n = q % 2
                V.tensor_copy(yj_g[:, q // 2, 4 * n:4 * n + 4, :, :],
                              bank_of("y", q)[0:NCH, :].rearrange("p (g l c) -> p g l c", g=4, l=LCH)).then_inc(dve_drained, 1)
            jl = lambda a: a.rearrange("p (j l) -> p l j", l=LCH)
            for m in range(4):
                dve.wait_ge(psum_filled, filled("yT", m))
                V.scalar_tensor_tensor(out=jl(vT[:, m, :]), in0=jl(vT[:, m, :]), scalar=dskip[:, m:m + 1],
                                       in1=bank_of("yT", m)[:, :].rearrange("p (l j) -> p l j", l=LCH),
                                       op0=ALU.mult, op1=ALU.add).then_inc(dve_drained, 1)
            for m in range(4):
                dve.wait_ge(*drained("glu", m))
                tt(ysT[:, m, :], vT[:, m, :], ygT[:, m, :], ALU.mult).then_inc(ys_ready, 1)
            dve.wait_ge(*drained("gate", 15))
            for m in range(KD):
                dve.wait_ge(psum_filled, filled("bp", m))
                tt(mgT[:, m, :], gT[:, m, :], bank_of("bp", m)[:, :], ALU.mult).then_inc(dve_drained, 1)
                dve.wait_ge(psum_filled, filled("bs", m))
                tt(gT[:, KD + m, :], gT[:, KD + m, :], bank_of("bs", m)[:, :], ALU.mult).then_inc(dve_drained, 1)
                dve.wait_ge(*drained("bs", m))
                tt(mgT[:, m, :], mgT[:, m, :], gT[:, KD + m, :], ALU.add).then_inc(merged_ready, 1)
            dve.wait_ge(h_loaded, 16)

            def normed(t):
                dve.wait_ge(h_squared, t + 1)
                rstd(rs_h[:, t:t + 1], ss_h[:, t:t + 1])
                ts(xn[:, t, :], h[:, t, :], rs_h[:, t:t + 1], ALU.mult).then_inc(h_normed, 1)

            def h_transposed(t):
                for n in range(2):
                    transposed("hT", 2 * t + n, hnT[:, 4 * n:4 * n + 4, P * t:P * (t + 1)], gain_x[:, 4 * n:4 * n + 4])

            def residual(name, t):
                for n in range(2):
                    dve.wait_ge(psum_filled, filled(name, 2 * t + n))
                    hs = h[:, t, HALF * n:HALF * (n + 1)]
                    tt(hs, hs, bank_of(name, 2 * t + n)[:, :], ALU.add).then_inc(dve_drained, 1)

            for t in range(NT):
                residual("wo1", t)
                normed(t)
                if t >= 1:
                    h_transposed(t - 1)
            h_transposed(NT - 1)
            def maxima(hd):
                for n in range(2):
                    dve.wait_ge(psum_filled, filled("sc", 2 * hd + n))
                    at_ = 4 * hd + 2 * n
                    link(V.tensor_reduce(out=rmax[:, at_:at_ + 2], in_=bank_of("sc", 2 * hd + n)[:, :].rearrange("p (t m) -> p t m", t=2),
                                         axis=AX.X, op=ALU.max))
                    ts(nmax[:, at_:at_ + 2], rmax[:, at_:at_ + 2], -HD ** -0.5, ALU.mult).then_inc(neg_max, 1)

            def divide(hd):
                for n in range(2):
                    dve.wait_ge(*drained("sc", 2 * hd + n))
                    at_ = 4 * hd + 2 * n
                    link(V.reciprocal(rsum[:, at_:at_ + 2], esum[:, at_:at_ + 2]))
                    for s in range(2):
                        t = 2 * n + s
                        ins = ts(prob[:, hd % 2, t, :], prob[:, hd % 2, t, :], rsum[:, at_ + s:at_ + s + 1], ALU.mult)
                    ins.then_inc(prob_ready, 1)

            maxima(0)
            for hd in range(HEADS + 1):
                if hd < HEADS:
                    divide(hd)
                if hd + 1 < HEADS:
                    maxima(hd + 1)
                if hd >= 1:
                    for n in range(2):
                        dve.wait_ge(psum_filled, filled("pv", 2 * (hd - 1) + n))
                        V.tensor_copy(oT[:, 2 * (hd - 1) + n, :], bank_of("pv", 2 * (hd - 1) + n)[:, :]).then_inc(dve_drained, 1)
            dve.wait_ge(gains_loaded, 64)
            for t in range(NT):
                residual("wo2", t)
                dve.wait_ge(z_squared, t + 1)
                rstd(rs_z[:, t:t + 1], ss_z[:, t:t + 1])
                V.scalar_tensor_tensor(out=xn[:, t, :], in0=h[:, t, :], scalar=rs_z[:, t:t + 1], in1=gain_ffn,
                                       op0=ALU.mult, op1=ALU.mult).then_inc(z_normed, 1)

            t4 = lambda a: a.unsqueeze(2).to_broadcast([P, NT, 4])
            n4 = lambda a: a.unsqueeze(1).to_broadcast([P, NT, 4])
            ts4 = lambda a: a.unsqueeze(1).to_broadcast([P, NT, 16])
            dve.wait_ge(index_ready, 1)
            dve.wait_ge(psum_filled, filled("route", 0))
            tt(logits, bank_of("route", 0)[:, 0:80].rearrange("p (t n) -> p t n", t=NT),
               rb.unsqueeze(1).to_broadcast([P, NT, 20]), ALU.add).then_inc(dve_drained, 1)
            dve.wait_ge(*drained("route", 0))

            def first_max(mask, top, src, t_a, t_b):
                link(V.tensor_reduce(out=top, in_=src, axis=AX.X, op=ALU.max))
                link(tt(t_a, src, t4(top), ALU.is_equal))
                link(tt(t_a, t_a, n4(desc), ALU.mult))
                link(V.tensor_reduce(out=t_b, in_=t_a, axis=AX.X, op=ALU.max))
                link(tt(mask, t_a, t4(t_b), ALU.is_equal))

            gmask, esel, top1, top2, e2 = q4[2], q4[3], q4[4], q4[5], q4[6]
            first_max(gmask, r4[3], lg, q4[7], r4[4])
            tt(q4[1], lg, t4(r4[3]), ALU.subtract).then_inc(g_shift, 1)
            le4 = le.rearrange("p t (g e) -> p t g e", g=4)
            link(tt(e64[0].rearrange("p t (g e) -> p t g e", g=4), le4, gmask.unsqueeze(3).to_broadcast([P, NT, 4, 4]), ALU.mult))
            link(V.tensor_reduce(out=esel, in_=e64[0].rearrange("p t (g e) -> p t e g", g=4), axis=AX.X, op=ALU.add))
            first_max(top1, r4[5], esel, q4[7], r4[4])
            link(ts(q4[8], top1, -1.0, ALU.mult, 1.0, ALU.add))
            link(tt(e2, esel, q4[8], ALU.mult))
            link(ts(q4[9], top1, -3.0e38, ALU.mult))
            link(tt(e2, e2, q4[9], ALU.add))
            first_max(top2, r4[6], e2, q4[7], r4[4])
            tt(r4[2], r4[6], r4[5], ALU.subtract).then_inc(e_shift, 1)
            for n, tm in ((1, top1), (2, top2)):
                link(tt(e64[n].rearrange("p t (g e) -> p t g e", g=4), gmask.unsqueeze(3).to_broadcast([P, NT, 4, 4]),
                        tm.unsqueeze(2).to_broadcast([P, NT, 4, 4]), ALU.mult))
            tt(e64[3], e64[1], e64[2], ALU.add).then_inc(mask_ready, 1)
            dve.wait_ge(g_exp, 1)
            link(V.tensor_reduce(out=r4[7], in_=q4[0], axis=AX.X, op=ALU.add))
            link(V.reciprocal(r4[7], r4[7]))
            dve.wait_ge(e_exp, 1)
            link(ts(r4[8], r4[1], 1.0, ALU.add))
            link(V.reciprocal(r4[8], r4[8]))
            link(tt(gw[:, 0, :], r4[8], r4[7], ALU.mult))
            link(tt(gw[:, 1, :], gw[:, 0, :], r4[1], ALU.mult))
            dve.wait_ge(psum_filled, filled("rank", 0))
            rk = bank_of("rank", 0)
            V.tensor_copy(x64, rk[:, 0:64].rearrange("p (t n) -> p t n", t=NT))
            V.tensor_copy(n16[0], rk[:, 64:80]).then_inc(dve_drained, 1)
            dve.wait_ge(*drained("rank", 0))
            link(ts(n16[1], n16[0], CAP + 0.5, ALU.is_gt))
            for k in range(2, -(-SEQ // CAP)):
                link(V.scalar_tensor_tensor(out=n16[1], in0=n16[0], scalar=CAP * k + 0.5, in1=n16[1], op0=ALU.is_gt, op1=ALU.add))
            src = n16[1]
            for s, sh in enumerate((1, 2, 4, 8)):
                dst = n16[2 + s]
                link(V.tensor_copy(dst[:, 0:sh], src[:, 0:sh]))
                link(tt(dst[:, sh:], src[:, sh:], src[:, 0:NE - sh], ALU.add))
                src = dst
            incl = src
            link(tt(n16[7], incl, n16[1], ALU.subtract))
            link(ts(n16[7], n16[7], NE - 1.0, ALU.add, float(CAP), ALU.mult))
            link(tt(n16[7], n16[7], base_id, ALU.subtract))
            link(ts(e64[4], x64, CAP - 0.5, ALU.is_gt))
            link(tt(e64[4], e64[4], ts4(n16[7]), ALU.mult))
            link(tt(e64[4], e64[4], ts4(base_id), ALU.add))
            link(tt(e64[4], e64[4], x64, ALU.add))
            for n in range(2):
                link(tt(e64[5], e64[4], e64[1 + n], ALU.mult))
                link(V.tensor_reduce(out=slot_f[:, n, :], in_=e64[5], axis=AX.X, op=ALU.add))
            link(V.tensor_copy(slot_i[:, :, :], slot_f))
            for k in range(N_OVER):
                link(ts(n16[8], incl, k + 0.5, ALU.is_lt))
                link(V.tensor_reduce(out=tile_row[:, k:k + 1], in_=n16[8], axis=AX.X, op=ALU.add))
            link(V.tensor_copy(tile_row[:, N_OVER:N_OVER + 1], incl[:, NE - 1:NE]))
            link(ts(tile_row[:, 0:N_OVER], tile_row[:, 0:N_OVER], NE - 1.0, ALU.min))
            V.tensor_copy(tile_i[:, 0:N_OVER + 1], tile_row[:, 0:N_OVER + 1]).then_inc(slots_ready, 1)

            dve.sem_inc(hid_ready, 2)
            dve.sem_inc(zs_ready, 1)
            dve.sem_inc(y_dve, 1)
            dve.wait_ge(z_stored, 16 * NT)

            def rows_transposed(e, a):
                dve.wait_ge(xg_used, e + 1)
                V.tensor_copy(zsT[a][:, 0:4, :], bank[0][:, 0:4 * CAP].rearrange("p (k t) -> p k t", k=4))
                V.tensor_copy(zsT[a][:, 4:8, :], bank[1][:, 0:4 * CAP].rearrange("p (k t) -> p k t", k=4)).then_inc(zs_ready, 1)

            def expert(e, a):
                dve.wait_ge(silu_ready, e + 3)
                dve.wait_ge(gate_done, e + 1)
                tt(hid[a].rearrange("p k t -> p (k t)"), silu[a], bank[3 + 4 * a][:, 0:4 * CAP], ALU.mult).then_inc(hid_ready, 1)

            def left(e, a, n_st):
                dve.wait_ge(down_done, 2 * e + 1)
                if n_st is not None:
                    dve.wait_ge(y_stored[a], n_st)
                V.tensor_copy(ysb[a][:, 0:HALF], bank[4][0:CAP, :]).then_inc(y_dve, 1)

            rows_transposed(0, 0)
            expert(0, 0)
            rows_transposed(1, 1)
            left(0, 0, None)
            expert(1, 1)
            rows_transposed(2, 0)
            left(1, 1, None)
            with dve.Fori(1, NE // 2 - 1) as i:
                for a in range(2):
                    expert(2 * i + a, a)
                    rows_transposed(2 * i + a + 1, 1 - a)
                    left(2 * i + a, a, 16 * i)
            expert(NE - 2, 0)
            rows_transposed(NE - 1, 1)
            left(NE - 2, 0, 8 * (NE - 2))
            expert(NE - 1, 1)
            left(NE - 1, 1, 8 * (NE - 2))
            n_over = dve.value_load(tile_i[0:1, N_OVER:N_OVER + 1], min_val=0, max_val=N_OVER)
            with dve.If(n_over > 0):
                with dve.Fori(0, n_over) as k:
                    dve.wait_ge(o_xT, k + 1)
                    V.tensor_copy(zsT[0][:, 0:4, :], bank[0][:, 0:4 * CAP].rearrange("p (k t) -> p k t", k=4))
                    V.tensor_copy(zsT[0][:, 4:8, :], bank[1][:, 0:4 * CAP].rearrange("p (k t) -> p k t", k=4)).then_inc(o_zs, 1)
                    dve.wait_ge(o_silu, k + 1)
                    dve.wait_ge(o_gate, k + 1)
                    tt(hid[0].rearrange("p k t -> p (k t)"), silu[0], bank[3][:, 0:4 * CAP], ALU.mult).then_inc(o_hid, 1)
                    dve.wait_ge(o_down, k + 2)
                    dve.wait_ge(y_stored[0], 8 * NE)
                    V.tensor_copy(ysb[0][:, 0:HALF], bank[4][0:CAP, :])
                    V.tensor_copy(ysb[0][:, HALF:D], bank[5][0:CAP, :]).then_inc(o_y, 1)
                dve.nop()
            with dve.Else():
                dve.nop()
            for t in range(NT):
                dve.wait_ge(back[t], 32)
                link(V.scalar_tensor_tensor(out=h[:, t, :], in0=yg1[t % 2], scalar=gw[:, 0, t:t + 1], in1=h[:, t, :], op0=ALU.mult, op1=ALU.add))
                V.scalar_tensor_tensor(out=h[:, t, :], in0=yg2[t % 2], scalar=gw[:, 1, t:t + 1], in1=h[:, t, :], op0=ALU.mult, op1=ALU.add).then_inc(combined, 1)
                dve.wait_ge(o_squared, t + 1)
                rstd(rs_z[:, t:t + 1], ss_o[:, t:t + 1])
                V.scalar_tensor_tensor(out=yg1[t % 2], in0=h[:, t, :], scalar=rs_z[:, t:t + 1], in1=gain_fin, op0=ALU.mult, op1=ALU.mult).then_inc(out_ready, 1)

        @block.tensor
        def _(pe):
            def claim(name, i):
                n = AT[name, i]
                assert ORDER[n][:2] == (name, i) and n == claimed[0]
                claimed[0] += 1
                if n >= BANKS:
                    pe.wait_ge(*drained(*ORDER[n - BANKS][:2]))
                return bank[n % BANKS]

            claimed = [0]

            def mm(o_, l_, r_, first, last):
                return nc.tensor.matmul(o_, lhsT=l_, rhs=r_, start=first, stop=last)

            def tr(o_, i_, p=P):
                return nc.tensor.transpose(o_, i_, ident[0:p, 0:p])

            def rows_to_columns(name, src, t):
                for n in range(2):
                    b = claim(name, 2 * t + n)
                    for k in range(4):
                        ins = tr(b[:, P * k:P * (k + 1)], src[:, t, P * (4 * n + k):P * (4 * n + k + 1)])
                    ins.then_inc(psum_filled, 1)

            def project(name, i, w, m, act_in, nk=KD):
                b = claim(name, i)
                for k in range(nk):
                    ins = mm(b[:, :], w[:, k, P * m:P * (m + 1)], act_in[:, k, :], k == 0, k == nk - 1)
                ins.then_inc(psum_filled, 1)

            pe.wait_ge(consts_ready, 1)
            for t in range(NT):
                pe.wait_ge(x_normed, t + 1)
                rows_to_columns("xT", h, t)
            for t in range(MT):
                pe.wait_ge(mem_normed, t + 1)
                rows_to_columns("memT", mem_tok, t)
            pe.wait_ge(lam_ready, 1)
            b = claim("lam", 0)
            for n in range(4):
                ins = tr(b[:, SSM_G * n:SSM_G * (n + 1)], lamq[:, n, :, :].rearrange("p x n -> p (x n)"), SSM_G)
            ins.then_inc(psum_filled, 1)
            pe.wait_ge(ssmb_loaded, 64)
            b = claim("cT", 0)
            for n in range(4):
                ins = tr(b[:, P * n:P * (n + 1)], cload[:, n, :])
            ins.then_inc(psum_filled, 1)
            pe.wait_ge(*loaded("v"))
            pe.wait_ge(*drained("xT", 7))
            for m in range(4):
                project("v", m, chunk("v", 8), m, uT)
            pe.wait_ge(*loaded("z"))
            for m in range(4):
                project("zp", m, chunk("z", 8), m, uT)
            pe.wait_ge(powers_ready, 1)
            for q in range(8):
                b = claim("bT", q)
                for n in range(4):
                    ins = tr(b[:, P * n:P * (n + 1)], bpow_m[:, 4 * q + n, :])
                ins.then_inc(psum_filled, 1)
            for q in range(8):
                b = claim("kern", q)
                for n in range(4):
                    gg = 4 * q + n
                    Bg, o_ = gc(Bb)[:, gg, :], b[0:SSM_C, P * n:P * (n + 1)]
                    mm(o_[:, 0:SSM_C], Bg, gc(Cy)[:, gg, :], True, True)
                    ins = mm(o_[:, SSM_C:P], Bg, cpow_m[:, gg, 0:P - SSM_C], True, True)
                ins.then_inc(psum_filled, 1)
            pe.wait_ge(*drained("v", 3))
            for l in range(LCH):
                b = claim("vl", l)
                for m in range(4):
                    ins = tr(b[0:NCH, P * m:P * (m + 1)], vT[:, m, :].rearrange("p (j l) -> p l j", l=LCH)[:, l, :])
                ins.then_inc(psum_filled, 1)
            pe.wait_ge(*drained("vl", 7))
            for q in range(4):
                b = claim("vch", q)
                for n in range(8):
                    ins = tr(b[:, NCH * n:NCH * (n + 1)], vj_m[:, 8 * q + n, :], NCH)
                ins.then_inc(psum_filled, 1)
            for q in range(4):
                b = claim("st", q)
                pe.wait_ge(*drained("vch", q))
                for n in range(8):
                    ins = mm(b[:, NCH * n:NCH * (n + 1)], bpow_m[:, 8 * q + n, :], vch[:, 8 * q + n, :], True, True)
                ins.then_inc(psum_filled, 1)
            pe.wait_ge(poolw_loaded, 16)
            for g_ in range(POOL_G):
                pe.wait_ge(pool_diff, g_ + 1)
                b = claim("mix", g_)
                mm(b[:, :], poolw[:, g_, :], zp[:, g_, PADT:], True, True).then_inc(psum_filled, 1)
            pe.wait_ge(*drained("memT", 3))
            for m in range(4):
                if m % 2 == 0:
                    pe.wait_ge(*loaded(f"k{m // 2}"))
                w = chunk(f"k{m // 2}", 8)
                b = claim("kk", m)
                for s in range(2):
                    c = 2 * (m % 2) + s
                    for k in range(KD):
                        ins = mm(b[:, MEM * s:MEM * (s + 1)], w[:, k, P * c:P * (c + 1)], memT[:, k, :], k == 0, k == KD - 1)
                ins.then_inc(psum_filled, 1)
            for n in range(4):
                if n % 2 == 0:
                    pe.wait_ge(*loaded(f"v{n // 2}"))
                w = chunk(f"v{n // 2}", 8)
                b = claim("vv", n)
                for k in range(KD):
                    ins = mm(b[:, :], memT[:, k, P * (n % 2):P * (n % 2 + 1)], w[:, k, :], k == 0, k == KD - 1)
                ins.then_inc(psum_filled, 1)
            pe.wait_ge(*loaded("toep"))
            pe.wait_ge(states_ready, 1)
            toep = ring[:, CH["toep"] % RING, :].rearrange("p (g x) -> p g x", g=SSM_G)
            for q in range(8):
                b = claim("y", q)
                for n in range(4):
                    gg = 4 * q + n
                    mm(b[0:NCH, P * n:P * (n + 1)], vch[:, gg, :], toep[:, gg, :], True, False)
                    ins = mm(b[0:NCH, P * n:P * (n + 1)], hin[:, gg, 1, :], cpow_m[:, gg, :], False, True)
                ins.then_inc(psum_filled, 1)

            def gates(lo, hi):
                for m in range(lo, hi):
                    if m % 4 == 0:
                        pe.wait_ge(*loaded(f"g{m // 4}"))
                    project("gate", m, chunk(f"g{m // 4}", 8), m % 4, uT)

            gates(0, 4)
            pe.wait_ge(*drained("y", 7))
            for m in range(4):
                b = claim("yT", m)
                for l in range(LCH):
                    ins = tr(b[:, NCH * l:NCH * (l + 1)], yj[:, m, l, :], NCH)
                ins.then_inc(psum_filled, 1)
            gates(4, 8)
            pe.wait_ge(*loaded("glu"))
            pe.wait_ge(gelu_ready, 4)
            for m in range(4):
                project("glu", m, chunk("glu", 4), m, ygT, 4)
            gates(8, 16)
            pe.wait_ge(*loaded("bp"))
            pe.wait_ge(*loaded("bs"))
            pe.wait_ge(*drained("mix", 3))
            pe.wait_ge(ys_ready, 4)
            for m in range(KD):
                project("bp", m, chunk("bp", 4), m, ypT, 4)
                project("bs", m, chunk("bs", 4), m, ysT, 4)
            pe.wait_ge(*loaded("o0"))
            pe.wait_ge(*loaded("o1"))
            pe.wait_ge(merged_ready, KD)

            def by_rows(name, t, src, w):
                for n in range(2):
                    b = claim(name, 2 * t + n)
                    for k in range(KD):
                        ins = mm(b[:, :], src[:, k, P * t:P * (t + 1)], w[n][:, k, :], k == 0, k == KD - 1)
                    ins.then_inc(psum_filled, 1)

            w = [chunk("o0", 8), chunk("o1", 8)]
            for t in range(NT):
                by_rows("wo1", t, mgT, w)
                if t >= 1:
                    pe.wait_ge(h_normed, t)
                    rows_to_columns("hT", xn, t - 1)
            pe.wait_ge(h_normed, NT)
            rows_to_columns("hT", xn, NT - 1)
            pe.wait_ge(*drained("hT", 7))
            for m in range(8):
                if m % 4 == 0:
                    pe.wait_ge(*loaded(f"q{m // 4}"))
                project("q", m, chunk(f"q{m // 4}", 8), m % 4, hnT)
            pe.wait_ge(*drained("vv", 3))
            for hd in range(HEADS + 1):
                if hd < HEADS:
                    pe.wait_ge(*drained("q", 2 * hd + 1))
                    for n in range(2):
                        b = claim("sc", 2 * hd + n)
                        for s in range(2):
                            t = 2 * n + s
                            for k in range(2):
                                ins = mm(b[:, MEM * s:MEM * (s + 1)], qT[:, 2 * hd + k, P * t:P * (t + 1)], kT[:, 2 * hd + k, :], k == 0, k == 1)
                        ins.then_inc(psum_filled, 1)
                if hd >= 1:
                    o_ = hd - 1
                    pe.wait_ge(prob_ready, 2 * o_ + 2)
                    for n in range(2):
                        b = claim("pT", 2 * o_ + n)
                        for t in range(NT):
                            ins = tr(b[:, P * t:P * (t + 1)], prob[:, o_ % 2, t, P * n:P * (n + 1)])
                        ins.then_inc(psum_filled, 1)
                    pe.wait_ge(*drained("pT", 2 * o_ + 1))
                    for n in range(2):
                        b = claim("pv", 2 * o_ + n)
                        for k in range(MT):
                            ins = mm(b[:, :], vm[:, k, HD * o_ + P * n:HD * o_ + P * (n + 1)], probT[:, o_ % 2, k, :], k == 0, k == MT - 1)
                        ins.then_inc(psum_filled, 1)
            pe.wait_ge(*loaded("w0"))
            pe.wait_ge(*loaded("w1"))
            pe.wait_ge(*drained("pv", 7))
            w = [chunk("w0", 8), chunk("w1", 8)]
            for t in range(NT):
                by_rows("wo2", t, oT, w)
                if t >= 1:
                    pe.wait_ge(z_normed, t)
                    rows_to_columns("zT", xn, t - 1)
            pe.wait_ge(z_normed, NT)
            rows_to_columns("zT", xn, NT - 1)
            pe.wait_ge(router_loaded, 32)
            pe.wait_ge(*drained("zT", 7))
            b = claim("route", 0)
            for t in range(NT):
                for k in range(KD):
                    ins = mm(b[:, 20 * t:20 * (t + 1)], zT[:, k, P * t:P * (t + 1)], rw[:, k, :], k == 0, k == KD - 1)
            ins.then_inc(psum_filled, 1)
            pe.wait_ge(mask_ready, 1)
            pe.wait_ge(masks_ready, 1)
            b = claim("rank", 0)
            for t in range(NT):
                for s in range(t):
                    mm(b[:, 16 * t:16 * (t + 1)], ones[:, :], e64[3][:, s, :], s == 0, False)
                mm(b[:, 16 * t:16 * (t + 1)], before[:, :], e64[3][:, t, :], t == 0, True)
            for t in range(NT):
                ins = mm(b[:, 64:80], ones[:, :], e64[3][:, t, :], t == 0, t == NT - 1)
            ins.then_inc(psum_filled, 1)
            pe.wait_ge(*drained("rank", 0))

            def transposes(e, a, n_g):
                pe.wait_ge(gathered[a], n_g)
                pe.wait_ge(zs_ready, e + 1)
                for k in range(KD):
                    ins = tr(bank[k // 4][:, CAP * (k % 4):CAP * (k % 4 + 1)], xg[a][:, P * k:P * (k + 1)], CAP)
                ins.then_inc(xg_used, 1)

            def up(a, s, b_, n_w, done):
                pe.wait_ge(slot_loaded[s], n_w)
                w = expert_chunk(s, 8)
                for m in range(4):
                    for k in range(KD):
                        ins = mm(b_[:, CAP * m:CAP * (m + 1)], w[:, k, P * m:P * (m + 1)], zsT[a][:, k, :], k == 0, k == KD - 1)
                ins.then_inc(done, 1)

            def expert(e, a, i, n_next):
                s0, s1, s2 = (expert_slot(a, c) for c in range(3))
                pe.wait_ge(zs_ready, e + 2)
                pe.wait_ge(silu_ready, e + 1)
                up(a, s0, bank[2 + 4 * a], front_loads[s0] + 16 * i + 16, up_done)
                pe.wait_ge(hid_ready, e + 1)
                up(a, s1, bank[3 + 4 * a], front_loads[s1] + 16 * i + 16, gate_done)
                if n_next is not None:
                    transposes(e + 1, 1 - a, n_next)
                pe.wait_ge(slot_loaded[s2], front_loads[s2] + 16 * i + 16)
                pe.wait_ge(hid_ready, e + 3)
                w = expert_chunk(s2, 4)
                for n, drained_by in ((0, y_dve), (1, y_act)):
                    pe.wait_ge(drained_by, e + 1)
                    for k in range(4):
                        ins = mm(bank[4 + n][0:CAP, :], hid[a][:, k, :], w[:, k, HALF * n:HALF * (n + 1)], k == 0, k == 3)
                    ins.then_inc(down_done, 1)

            transposes(0, 0, 16)
            with pe.Fori(0, NE // 2 - 1) as i:
                expert(2 * i, 0, i, 16 * i + 16)
                expert(2 * i + 1, 1, i, 16 * i + 32)
            last = NE // 2 - 1
            expert(NE - 2, 0, last, 16 * last + 16)
            expert(NE - 1, 1, last, None)
            pe.sem_inc(o_down, 1)
            pe.wait_ge(y_dve, NE + 1)
            pe.wait_ge(y_act, NE + 1)
            n_over = pe.value_load(tile_i[0:1, N_OVER:N_OVER + 1], min_val=0, max_val=N_OVER)
            with pe.If(n_over > 0):
                with pe.Fori(0, n_over) as k:
                    pe.wait_ge(o_gath, 16 * k + 16)
                    for kk in range(KD):
                        ins = tr(bank[kk // 4][:, CAP * (kk % 4):CAP * (kk % 4 + 1)], xg[0][:, P * kk:P * (kk + 1)], CAP)
                    ins.then_inc(o_xT, 1)
                    pe.wait_ge(o_zs, k + 1)
                    pe.wait_ge(o_w, 48 * k + 48)
                    for c, done in ((0, o_up), (1, o_gate)):
                        w = expert_chunk(c, 8)
                        for m in range(4):
                            for kk in range(KD):
                                ins = mm(bank[2 + c][:, CAP * m:CAP * (m + 1)], w[:, kk, P * m:P * (m + 1)], zsT[0][:, kk, :], kk == 0, kk == KD - 1)
                        ins.then_inc(done, 1)
                    pe.wait_ge(o_hid, k + 1)
                    w = expert_chunk(2, 4)
                    for n in range(2):
                        for kk in range(4):
                            ins = mm(bank[4 + n][0:CAP, :], hid[0][:, kk, :], w[:, kk, HALF * n:HALF * (n + 1)], kk == 0, kk == 3)
                    ins.then_inc(o_down, 1)
                    pe.wait_ge(o_y, k + 1)
                pe.nop()
            with pe.Else():
                pe.nop()


_INS = ['x', 'mem', 'norm_mix', 'w_in', 'pool_w', 'pool_scale', 'ssm_a_re', 'ssm_a_im', 'ssm_log_dt', 'ssm_b_re', 'ssm_b_im', 'ssm_c_re', 'ssm_c_im', 'ssm_d', 'glu_w', 'glu_b', 'br_pool', 'br_ssm', 'w_out', 'norm_x', 'norm_mem', 'x_wq', 'x_wkv', 'x_wo', 'norm_ffn', 'router_g_w', 'router_g_b', 'router_e_w', 'router_e_b', 'exp_w1', 'exp_w3', 'exp_w2', 'norm_final']
_OUTS = [((1, SEQ, D), 'float32')]


def kernel(**inputs):
    import numpy as _np
    import concourse.bacc as _bacc
    from concourse import mybir as _mybir
    from concourse.bass_utils import run_bass_kernel_spmd as _run

    nc = _bacc.Bacc("TRN2", target_bir_lowering=False, num_devices=1)
    arrays, args = {}, []
    for name in _INS:
        a = _np.ascontiguousarray(inputs[name])
        arrays[f"in_{name}_dram"] = a
        args.append(nc.dram_tensor(f"in_{name}_dram", a.shape, _mybir.dt.from_np(a.dtype), kind="ExternalInput").ap())
    for i, (shape, dtype) in enumerate(_OUTS):
        dt = _mybir.dt.from_np(_np.dtype(dtype))
        args.append(nc.dram_tensor(f"out_{i}_dram", shape, dt, kind="ExternalOutput").ap())
    bass_hybrid_decoder_layer(nc, *args)
    r = _run(nc, [arrays], core_ids=[0])
    return r.results[0]["out_0_dram"]
```

```python
import math
from contextlib import ExitStack

import concourse.bass as bass
from concourse import mybir
from concourse.alu_op_type import AluOpType as ALU

P = 128
SEQ, D, MEM = 512, 1024, 256
NT, KD, MT = SEQ // P, D // P, MEM // P
HALF = 512
POOL_G, SSM_G, SSM_C, SSM_N = 4, 32, 16, 64
LCH = 8
NCH = SEQ // LCH
SUP = 8
HEADS, HD = 4, 256
NE, F = 16, 512
CAP = 96
N_OVER = (2 * SEQ) // CAP
N_TILES = NE + N_OVER
SLOTS = N_TILES * CAP
RING = 6
RAW = 3
PADT = 16
EPS = 1e-6
BANKS = 8


def bass_hybrid_decoder_layer(nc: bass.Bass, x, mem, norm_mix, w_in, pool_w, pool_scale, ssm_a_re, ssm_a_im,
                              ssm_log_dt, ssm_b_re, ssm_b_im, ssm_c_re, ssm_c_im, ssm_d, glu_w, glu_b,
                              br_pool, br_ssm, w_out, norm_x, norm_mem, x_wq, x_wkv, x_wo, norm_ffn,
                              router_g_w, router_g_b, router_e_w, router_e_b, exp_w1, exp_w3, exp_w2,
                              norm_final, out):
    f32, i32 = mybir.dt.float32, mybir.dt.int32
    ACT, AX = mybir.ActivationFunctionType, mybir.AxisListType

    ctx = ExitStack()
    with ctx:
        places = {}

        def sb(name, shape, dt=f32):
            places[name] = -(-nc.sbuf_base // 32) * 32
            return ctx.enter_context(nc.sbuf_tensor(name, shape, dt))

        def sem(name):
            return ctx.enter_context(nc.semaphore(name))

        ring = [sb(f"slot{i}", [P, 4096]) for i in range(RING)]
        hreg = sb("hreg", [P, 4096])
        ureg = sb("ureg", [P, 4096])
        greg = sb("greg", [P, 8192])
        kvreg = sb("kvreg", [P, 4096])
        areg = sb("areg", [P, 2048 + POOL_G * (PADT + SEQ)])
        zeros = areg[:, 0:4 * 7 * SSM_C]
        memreg = sb("memreg", [P, 2048])
        ident = sb("ident", [P, P])
        before = sb("before", [P, P])
        ones = sb("ones", [P, P])
        poolw = sb("poolw", [P, POOL_G, P])
        lam8 = sb("lam8", [P, 8, 2, SSM_G])
        cols = sb("cols", [P, 3 * KD + 4 * 3])
        cntinv = sb("cntinv", [P, POOL_G, PADT])
        rstat = sb("rstat", [P, 32])
        newton = sb("newton", [P, 8])
        soft = sb("soft", [P, 4, 4 * HEADS])

        f32r = mybir.dt.float32r

        def rounded(name, shape):
            return nc.alloc_sbuf_tensor_at(name + "_r", shape, f32r, offset=places[name])

        ring_r = [rounded(f"slot{i}", [P, 4096]) for i in range(RING)]
        hreg_r = rounded("hreg", [P, 4096])
        ureg_r = rounded("ureg", [P, 4096])
        greg_r = rounded("greg", [P, 8192])
        areg_r = rounded("areg", [P, 2048 + POOL_G * (PADT + SEQ)])

        gain_mix, gain_x, gain_mem = (cols[:, KD * i:KD * (i + 1)] for i in range(3))
        pscale, dskip, glub = (cols[:, 3 * KD + 4 * i:3 * KD + 4 * (i + 1)] for i in range(3))
        rmax, nmax, esum, rsum = (soft[:, i, :] for i in range(4))
        ss_x, rs_x = rstat[:, 0:4], rstat[:, 4:8]
        ss_m, rs_m = rstat[:, 8:10], rstat[:, 10:12]
        ss_h, rs_h = rstat[:, 12:16], rstat[:, 16:20]
        ss_z, rs_z = rstat[:, 20:24], rstat[:, 24:28]
        ss_o = rstat[:, 28:32]

        h = hreg[:, :].rearrange("p (t d) -> p t d", t=NT)
        cpow = hreg[:, :].rearrange("p (g k c) -> p g k c", g=SSM_G, k=LCH)
        cpow_m = hreg[:, :].rearrange("p (g m) -> p g m", g=SSM_G)
        msq = areg[:, 2048:4096].rearrange("p (t d) -> p t d", t=MT)
        yj = hreg[0:NCH, :].rearrange("p (m l c) -> p m l c", m=4, l=LCH)
        yj_g = hreg[0:NCH, :].rearrange("p (m l g c) -> p m g l c", m=4, l=LCH, c=SSM_C)
        uT = ureg[:, :].rearrange("p (k t) -> p k t", k=KD)
        qT, zT = uT, uT
        by_k = lambda a: a.rearrange("p (k t) -> p k t", t=SEQ)
        u_hi, u_lo = by_k(ring_r[5][:, :]), by_k(ureg_r[:, :])
        mg_hi, mg_lo = by_k(ureg_r[:, :]), by_k(ring_r[5][:, :])
        G_lo, G_hi = greg[:, 0:4096], greg[:, 4096:8192]
        bpow = G_lo.rearrange("p (g m c) -> p g m c", g=SSM_G, m=LCH)
        bpow_m = G_lo.rearrange("p (g m) -> p g m", g=SSM_G)
        W = G_lo.rearrange("p (g x s j) -> p g x s j", g=SSM_G, x=2, s=SUP)
        hin = G_lo.rearrange("p (g x q) -> p g x q", g=SSM_G, x=2)
        lamg = [greg[0:SSM_G, 64 * i:64 * (i + 1)] for i in range(24)]
        lamq = greg[0:SSM_G, 1536:2048].rearrange("p (q x n) -> p q x n", q=4, x=2)
        cload = greg[:, 2048:2560].rearrange("p (t n) -> p t n", t=4)
        gtmp = greg[:, 4096:6144]
        gtmp_k = gtmp.rearrange("p (g k c) -> p g k c", g=SSM_G, k=4)
        mem_tok = greg[:, 6144:8192].rearrange("p (t d) -> p t d", t=MT)
        kern_sb = greg[0:SSM_C, 4096:8192].rearrange("p (g x) -> p g x", g=SSM_G)
        vch = greg[:, 4096:6144].rearrange("p (g q) -> p g q", g=SSM_G)
        stmp = greg[:, 6144:8192]
        gT = greg[:, :].rearrange("p (k t) -> p k t", k=16)
        hnT, hn_hi, hn_lo = by_k(areg[:, 64:4160]), by_k(greg_r[:, 0:4096]), by_k(areg_r[:, 64:4160])
        oT, o_hi, o_lo = by_k(ring[5][:, :]), by_k(greg_r[:, 0:4096]), by_k(ring_r[5][:, :])
        xn = G_hi.rearrange("p (t d) -> p t d", t=NT)
        prob = G_hi[:, 0:2048].rearrange("p (b t m) -> p b t m", b=2, t=NT)
        probT = G_hi[:, 2048:4096].rearrange("p (b m t) -> p b m t", b=2, m=MT)
        B_s, B_w = kvreg[:, 0:512], kvreg[:, 512:1024]
        ptmp = kvreg[:, 0:2 * (PADT + SEQ)].rearrange("p (b t) -> p b t", b=2)
        o = 1088
        Bb, Bbw, Cy, Cw = (kvreg[:, o + 512 * i:o + 512 * (i + 1)] for i in range(4))
        pw = kvreg[:, o + 2048:o + 2560].rearrange("p (k x g) -> p k x g", k=LCH, x=2)
        lamL = kvreg[:, o + 2560:o + 2688].rearrange("p (q g) -> p q g", q=4)
        gc = lambda a: a.rearrange("p (g c) -> p g c", g=SSM_G)
        vj = kvreg[0:NCH, :].rearrange("p (g m c) -> p g m c", g=SSM_G, m=LCH)
        vj_m = kvreg[0:NCH, :].rearrange("p (g m) -> p g m", g=SSM_G)
        kT = kvreg[:, 0:2048].rearrange("p (k m) -> p k m", k=KD)
        vm = kvreg[:, 2048:4096].rearrange("p (t d) -> p t d", t=MT)
        vT = areg[:, 0:2048].rearrange("p (k t) -> p k t", k=4)
        zp = areg[:, 2048:].rearrange("p (k t) -> p k t", k=POOL_G)
        ypT, ysT = zp[:, :, PADT:], vT
        yp_hi, ys_hi = by_k(hreg_r[:, 0:2048]), by_k(hreg_r[:, 2048:4096])
        yp_lo, ys_lo = areg_r[:, 2048:].rearrange("p (k t) -> p k t", k=POOL_G)[:, :, PADT:], by_k(areg_r[:, 0:2048])
        memT = memreg[:, :].rearrange("p (k t) -> p k t", k=KD)
        ygT = memreg[:, :].rearrange("p (k t) -> p k t", k=4)
        gain_ffn, gain_fin = memreg[:, 0:D], memreg[:, D:2 * D]

        rw = poolw[:, :, :].rearrange("p g d -> p (g d)")[:, 0:KD * 20].rearrange("p (k n) -> p k n", k=KD)
        rb = areg[:, 0:20]
        AR = areg
        def ar(at, n):
            return AR[:, at:at + n]
        logits = ar(32, 80).rearrange("p (t n) -> p t n", t=NT)
        lg, le = logits[:, :, 0:4], logits[:, :, 4:20]
        desc = ar(112, 4)
        r4 = [ar(120 + 4 * i, 4) for i in range(16)]
        q4 = [ar(200 + 16 * i, 16).rearrange("p (t n) -> p t n", t=NT) for i in range(10)]
        e64 = [ar(400 + 64 * i, 64).rearrange("p (t n) -> p t n", t=NT) for i in range(8)]
        x64 = ar(912, 64).rearrange("p (t n) -> p t n", t=NT)
        n16 = [ar(1000 + 16 * i, 16) for i in range(14)]
        m_cum = ar(1312, 80)
        o_k = ar(1400, N_OVER * NE).rearrange("p (k n) -> p k n", k=N_OVER)
        o_lt = ar(1600, N_OVER * NE).rearrange("p (k n) -> p k n", k=N_OVER)
        pre = [ar(1800 + 32 * i, 32) for i in range(5)]
        tile_row = ar(1290, N_OVER + 1)
        slot_f = ar(1260, 8).rearrange("p (s t) -> p s t", s=2)
        base_id = ar(1270, 16)
        tok_id = sb("tok_id", [P, NT], i32)
        slot_i = sb("slot_i", [P, 2, NT], i32)
        tile_i = sb("tile_i", [P, N_OVER + 1], i32)
        idx_all = sb("idx_all", [CAP, N_TILES], i32)
        idx_one = sb("idx_one", [CAP, 1], i32)
        gw = sb("gw", [P, 2, NT])
        o = 0
        xg = [greg[0:CAP, D * a:D * (a + 1)] for a in range(2)]
        zsT = [greg[:, 2048 + 768 * a:2048 + 768 * a + KD * CAP].rearrange("p (k t) -> p k t", k=KD) for a in range(2)]
        silu = [greg[:, 3584 + 384 * a:3584 + 384 * a + 4 * CAP] for a in range(2)]
        hid = [greg[:, 4352 + 384 * a:4352 + 384 * a + 4 * CAP].rearrange("p (k t) -> p k t", k=4) for a in range(2)]
        ysb = [greg[0:CAP, 5120 + D * a:5120 + D * (a + 1)] for a in range(2)]
        yg1 = [kvreg[:, 2048 * a:2048 * a + D] for a in range(2)]
        yg2 = [kvreg[:, 2048 * a + D:2048 * a + 2 * D] for a in range(2)]

        bank = [ctx.enter_context(nc.psum_tensor(f"bank{i}", [P, HALF], f32)) for i in range(BANKS)]

        kern_d = nc.dram_tensor("kern_d", [SSM_G, SSM_C, 15 * SSM_C], f32, kind="Internal").ap()
        z_d = nc.dram_tensor("z_d", [SEQ, D], f32, kind="Internal").ap()
        inv_d = nc.dram_tensor("inv_d", [SLOTS, 1], i32, kind="Internal").ap()
        y_d = nc.dram_tensor("y_d", [SLOTS, D], f32, kind="Internal").ap()

        x_loaded = [sem(f"x_loaded{t}") for t in range(NT)]
        mem_loaded, cols_loaded, ssm_loaded = sem("mem_loaded"), sem("cols_loaded"), sem("ssm_loaded")
        ssmb_loaded, poolw_loaded = sem("ssmb_loaded"), sem("poolw_loaded")
        slot_loaded = [sem(f"slot_loaded{s}") for s in range(RING)]
        toep_loaded, kern_stored, zero_stored = sem("toep_loaded"), sem("kern_stored"), sem("zero_stored")
        consts_ready, masks_ready, tok_ready, counts_ready, index_ready = (sem(n) for n in ("consts_ready", "masks_ready", "tok_ready", "counts_ready", "index_ready"))
        psum_filled, act_drained, dve_drained = sem("psum_filled"), sem("act_drained"), sem("dve_drained")
        dve_step, act_step, pool_step = sem("dve_step"), sem("act_step"), sem("pool_step")
        x_squared, mem_squared, x_normed, mem_normed = sem("x_squared"), sem("mem_squared"), sem("x_normed"), sem("mem_normed")
        decay_ready, lam_ready, sines_ready = sem("decay_ready"), sem("lam_ready"), sem("sines_ready")
        x_rstd, mem_rstd = sem("x_rstd"), sem("mem_rstd")
        angle_ready, powers_ready = sem("angle_ready"), sem("powers_ready")
        pool_diff, states_ready = sem("pool_diff"), sem("states_ready")
        weight_hi, weight_lo = sem("weight_hi"), sem("weight_lo")
        u_rounded, u_split, yp_rounded, yp_split, ys_rounded, ys_split = (sem(n) for n in ("u_rounded", "u_split", "yp_rounded", "yp_split", "ys_rounded", "ys_split"))
        mg_exact, mg_rounded, hn_rounded, hn_split, o_rounded, o_split = (sem(n) for n in ("mg_exact", "mg_rounded", "hn_rounded", "hn_split", "o_rounded", "o_split"))
        gain_loaded = sem("gain_loaded")
        gelu_ready, ys_ready, merged_ready = sem("gelu_ready"), sem("ys_ready"), sem("merged_ready")
        h_loaded, h_squared, h_normed = sem("h_loaded"), sem("h_squared"), sem("h_normed")
        neg_max, exp_done, prob_ready = sem("neg_max"), sem("exp_done"), sem("prob_ready")
        gains_loaded, z_squared, z_normed, z_stored = sem("gains_loaded"), sem("z_squared"), sem("z_normed"), sem("z_stored")
        router_loaded, g_shift, g_exp, e_shift, e_exp = sem("router_loaded"), sem("g_shift"), sem("g_exp"), sem("e_shift"), sem("e_exp")
        mask_ready, slots_ready, tiles_ready, inv_zeroed, inv_stored, inv_loaded = sem("mask_ready"), sem("slots_ready"), sem("tiles_ready"), sem("inv_zeroed"), sem("inv_stored"), sem("inv_loaded")
        idx_ready, pool_tick, rows_filled = sem("idx_ready"), sem("pool_tick"), sem("rows_filled")
        gathered = [sem(f"gathered{a}") for a in range(2)]
        xg_used, zs_ready, up_done, gate_done = sem("xg_used"), sem("zs_ready"), sem("up_done"), sem("gate_done")
        silu_ready, hid_ready, down_done = sem("silu_ready"), sem("hid_ready"), sem("down_done")
        y_dve, y_act = sem("y_dve"), sem("y_act")
        y_stored = [sem(f"y_stored{a}") for a in range(2)]
        o_idx, o_gath, o_w, o_xT, o_zs, o_up, o_gate = (sem(n) for n in ("o_idx", "o_gath", "o_w", "o_xT", "o_zs", "o_up", "o_gate"))
        o_silu, o_hid, o_down, o_y, o_stored, all_stored = (sem(n) for n in ("o_silu", "o_hid", "o_down", "o_y", "o_stored", "all_stored"))
        back = [sem(f"back{t}") for t in range(NT)]
        combined, o_squared, out_ready = sem("combined"), sem("o_squared"), sem("out_ready")
        out_stored = [sem(f"out_stored{t}") for t in range(NT)]

        ORDER = []

        def jobs(name, n, engine):
            ORDER.extend((name, i, engine) for i in range(n))

        jobs("xT", 8, "dve")
        ORDER.extend(("v", i, "act") for i in range(2))
        jobs("lam", 1, "dve")
        jobs("cT", 1, "act")
        ORDER.extend(("v", i, "act") for i in range(2, 4))
        jobs("zp", 4, "act")
        jobs("memT", 4, "dve")
        jobs("bT", 8, "act")
        jobs("kern", 8, "act")
        jobs("vl", 8, "act")
        jobs("vch", 4, "act")
        jobs("st", 4, "act")
        jobs("mix", 4, "act")
        jobs("kk", 4, "act")
        jobs("vv", 4, "act")
        jobs("y", 8, "dve")
        ORDER.extend(("gate", i, "act") for i in range(4))
        jobs("yT", 4, "dve")
        ORDER.extend(("gate", i, "act") for i in range(4, 8))
        jobs("glu", 4, "act")
        ORDER.extend(("gate", i, "act") for i in range(8, 16))
        jobs("bp", 8, "dve")
        jobs("bs", 8, "dve")
        for t in range(NT):
            ORDER.extend(("wo1", 2 * t + n, "dve") for n in range(2))
            if t >= 1:
                ORDER.extend(("hT", 2 * (t - 1) + n, "dve") for n in range(2))
        ORDER.extend(("hT", 6 + n, "dve") for n in range(2))
        jobs("q", 8, "act")
        for hd in range(HEADS + 1):
            if hd < HEADS:
                ORDER.extend(("sc", 2 * hd + n, "act") for n in range(2))
            if hd >= 1:
                ORDER.extend(("pT", 2 * (hd - 1) + n, "act") for n in range(2))
                ORDER.extend(("pv", 2 * (hd - 1) + n, "dve") for n in range(2))
        for t in range(NT):
            ORDER.extend(("wo2", 2 * t + n, "dve") for n in range(2))
            if t >= 2:
                ORDER.append(("route", t - 2, "dve"))
            if t >= 1:
                ORDER.extend(("zT", 2 * (t - 1) + n, "act") for n in range(2))
        ORDER.append(("route", NT - 2, "dve"))
        ORDER.extend(("zT", 6 + n, "act") for n in range(2))
        ORDER.append(("route", NT - 1, "dve"))
        jobs("rank", 1, "dve")
        AT = {(n, i): k for k, (n, i, _) in enumerate(ORDER)}
        counts, at = {"act": 0, "dve": 0}, []
        for _, _, e in ORDER:
            counts[e] += 1
            at.append((e, counts[e]))

        def filled(name, i):
            return AT[name, i] + 1

        def drained(name, i):
            e, n = at[AT[name, i]]
            return (act_drained if e == "act" else dve_drained), n

        def bank_of(name, i):
            return bank[AT[name, i] % BANKS]

        wcol = lambda w, c: w[0, :, HALF * c:HALF * (c + 1)].rearrange("(k p) n -> p k n", p=P)
        FRONT = [("v", wcol(w_in, 1), ("v", 3)), ("z", wcol(w_in, 0), ("zp", 3)),
                 ("k0", wcol(x_wkv, 0), ("kk", 1)), ("k1", wcol(x_wkv, 1), ("kk", 3)),
                 ("v0", wcol(x_wkv, 2), ("vv", 1)), ("v1", wcol(x_wkv, 3), ("vv", 3)),
                 ("toep", None, ("y", 7)), ("g0", wcol(w_in, 2), ("gate", 3)), ("g1", wcol(w_in, 3), ("gate", 7)),
                 ("glu", glu_w[0].rearrange("(k p) n -> p k n", p=P), ("glu", 3)),
                 ("g2", wcol(w_in, 4), ("gate", 11)), ("g3", wcol(w_in, 5), ("gate", 15)),
                 ("bp", br_pool[0].rearrange("(k p) n -> p k n", p=P), ("bp", 7)),
                 ("bs", br_ssm[0].rearrange("(k p) n -> p k n", p=P), ("bs", 7)),
                 ("o0", wcol(w_out, 0), ("wo1", 6)), ("o1", wcol(w_out, 1), ("wo1", 7)),
                 ("q0", wcol(x_wq, 0), ("q", 3)), ("q1", wcol(x_wq, 1), ("q", 7)),
                 ("w0", wcol(x_wo, 0), ("wo2", 6)), ("w1", wcol(x_wo, 1), ("wo2", 7))]
        NF = len(FRONT)
        CH = {n: i for i, (n, _, _) in enumerate(FRONT)}
        front_loads = [16 * sum(1 for i in range(NF) if i % RAW == s and FRONT[i][0] != "toep") for s in range(RING)]

        def loaded(name):
            c = CH[name]
            if name == "toep":
                return toep_loaded, 16 * LCH
            return slot_loaded[c % RAW], 16 * sum(1 for i in range(c % RAW, c + 1, RAW) if FRONT[i][0] != "toep")

        def chunk(name, k, of=ring):
            return of[CH[name] % RAW][:, 0:(k * D if k == 4 and name != "glu" else k * HALF)].rearrange("p (k n) -> p k n", k=k)

        SPLIT = ["g0", "g1", "g2", "g3", "bp", "bs", "o0", "o1", "q0", "q1", "w0", "w1"]

        def hi_slot(name):
            return RAW + SPLIT.index(name) % 2

        def parts(name, k):
            return ring_r[hi_slot(name)][:, :].rearrange("p (k n) -> p k n", k=k), chunk(name, k, ring_r)

        def expert_slot(e, c):
            return 3 * e + c

        def expert_chunk(slot, k):
            return ring[slot][:, :].rearrange("p (k n) -> p k n", k=k)

        w13 = (exp_w1[0].rearrange("e (k p) f -> e p k f", p=P), exp_w3[0].rearrange("e (k p) f -> e p k f", p=P))
        w2v = exp_w2[0].rearrange("e (k p) n -> e p k n", p=P)
        block = ctx.enter_context(nc.Block())

        @block.sync
        def _(sp):
            for t in range(NT):
                sp.dma_start(h[:, t, :], x[0, P * t:P * (t + 1), :]).then_inc(x_loaded[t], 16)
            for c, (name, src, _) in enumerate(FRONT):
                if name == "k0":
                    sp.wait_ge(cols_loaded, 80)
                    sp.wait_ge(ssmb_loaded, 64)
                if name == "z":
                    sp.dma_start(mem_tok, mem[0].rearrange("(t p) d -> p t d", p=P)).then_inc(mem_loaded, 16)
                if c >= RAW:
                    sp.wait_ge(psum_filled, filled(*FRONT[c - RAW][2]))
                if name == "toep":
                    sp.wait_ge(kern_stored, 16)
                    sp.wait_ge(zero_stored, 16)
                    dst = ring[c % RAW][:, :].rearrange("p (g x) -> p g x", g=SSM_G)
                    for m in range(LCH):
                        sp.dma_start(dst[SSM_C * m:SSM_C * (m + 1), :, :],
                                     kern_d[:, :, SSM_C * m:SSM_C * m + P].rearrange("g c x -> c g x")).then_inc(toep_loaded, 16)
                    continue
                if name == "glu":
                    for lo in range(0, N_OVER * CAP, SEQ):
                        n = min(SEQ, N_OVER * CAP - lo)
                        sp.dma_start(y_d[NE * CAP + lo:NE * CAP + lo + n, :], x[0, 0:n, :]).then_inc(rows_filled, 16)
                k = src.shape[1]
                dst = ring[c % RAW][:, 0:k * src.shape[2]].rearrange("p (k n) -> p k n", k=k)
                sp.dma_start(dst, src).then_inc(slot_loaded[c % RAW], 16)

            def load_expert(e, a, used, order=(0, 1, 2)):
                for c in order:
                    if used:
                        sp.wait_ge(*used[c])
                    s = expert_slot(a, c)
                    src = (w13[c] if c < 2 else w2v)[bass.ds(e, 1)].rearrange("e p k n -> p (e k) n")
                    sp.dma_start(expert_chunk(s, 8 if c < 2 else 4), src).then_inc(slot_loaded[s], 16)

            load_expert(0, 0, [(psum_filled, filled(*job)) for job in (("wo2", 6), ("wo2", 7), ("q", 7))], (2, 0, 1))
            load_expert(1, 1, [(psum_filled, filled("wo2", 7))] * 3)
            with sp.Fori(1, NE // 2) as i:
                for a in range(2):
                    load_expert(2 * i + a, a, [(up_done, 2 * i + a - 1), (gate_done, 2 * i + a - 1),
                                               (down_done, 4 * i + 2 * a - 2)])
            sp.wait_ge(tiles_ready, 1)
            n_over = sp.value_load(tile_i[0:1, N_OVER:N_OVER + 1], min_val=0, max_val=N_OVER)
            with sp.If(n_over > 0):
                with sp.Fori(0, n_over) as k:
                    ex = sp.value_load(tile_i[0:1, bass.ds(k, 1)], min_val=0, max_val=NE - 1)
                    sp.wait_ge(down_done, 2 * NE)
                    sp.wait_ge(o_down, k + 1)
                    for c in range(3):
                        src = (w13[c] if c < 2 else w2v)[bass.ds(ex, 1)].rearrange("e p k n -> p (e k) n")
                        sp.dma_start(expert_chunk(c, 8 if c < 2 else 4), src).then_inc(o_w, 16)
                sp.nop()
            with sp.Else():
                sp.nop()

            for t in range(NT):
                sp.wait_ge(out_ready, t + 1)
                sp.dma_start(out[0, P * t:P * (t + 1), :], yg1[t % 2]).then_inc(out_stored[t], 16)
            for t in range(NT):
                sp.wait_ge(out_stored[t], 16)

        @block.gpsimd
        def _(pool):
            pool.memset(ident[:, :], 0.0).then_inc(pool_step, 1)
            pool.memset(before[:, :], 1.0).then_inc(pool_step, 1)
            pool.memset(ones[:, :], 1.0).then_inc(pool_step, 1)
            pool.wait_ge(pool_step, 3)
            pool.affine_select(out=ident[:, :], in_=ident[:, :], compare_op=ALU.not_equal, fill=1.0, base=0,
                               pattern=[[-1, P]], channel_multiplier=1).then_inc(consts_ready, 1)
            column = lambda a: a.rearrange("a (k p) -> p (a k)", p=P)
            pool.dma_start(gain_mix, column(norm_mix), allow_slow_non_contiguous=True).then_inc(gain_loaded, 16)
            for dst, src in ((gain_x, norm_x), (gain_mem, norm_mem), (pscale, pool_scale),
                             (dskip, ssm_d), (glub, glu_b)):
                pool.dma_start(dst, column(src), allow_slow_non_contiguous=True).then_inc(cols_loaded, 16)
            pool.affine_select(out=before[:, :], in_=before[:, :], compare_op=ALU.is_gt, fill=0.0, base=0,
                               pattern=[[1, P]], channel_multiplier=-1).then_inc(masks_ready, 1)
            pool.dma_start(poolw[:, :, :], pool_w[0].rearrange("g c d -> c g d")).then_inc(poolw_loaded, 16)
            pool.iota(tok_id[:, :], pattern=[[P, NT]], base=0, channel_multiplier=1).then_inc(tok_ready, 1)
            pool.memset(zeros, 0.0).then_inc(pool_step, 1)
            pool.wait_ge(pool_step, 4)
            pool.dma_start(kern_d.rearrange("g c x -> (g c) x")[:, 0:7 * SSM_C].rearrange("(p r) x -> p r x", p=P),
                           zeros.rearrange("p (r x) -> p r x", r=4)).then_inc(zero_stored, 16)
            pool.dma_start(inv_d.rearrange("(p r) o -> p (r o)", p=CAP), zeros[0:CAP, 0:N_TILES].bitcast(i32)).then_inc(inv_zeroed, 16)
            for gi in range(POOL_G):
                w = 2 << gi
                for c in range(w - 1):
                    pool.memset(cntinv[:, gi, c:c + 1], 1.0 / (c + 1))
                ins = pool.memset(cntinv[:, gi, w - 1:], 1.0 / w)
            ins.then_inc(counts_ready, 1)
            pool.wait_ge(psum_filled, filled("mix", 3))
            pool.dma_start(rw[:, :, 0:4], router_g_w[0].rearrange("(k p) n -> p k n", p=P)).then_inc(router_loaded, 16)
            pool.dma_start(rw[:, :, 4:20], router_e_w[0].rearrange("(k p) g n -> p k (g n)", p=P)).then_inc(router_loaded, 16)
            pool.wait_ge(psum_filled, filled("bs", 7))
            pool.dma_start(h, x[0].rearrange("(t p) d -> p t d", p=P)).then_inc(h_loaded, 16)
            pool.wait_ge(ys_ready, 4)
            pool.dma_start(gain_ffn, norm_ffn.partition_broadcast(P).rearrange("p a d -> p (a d)")).then_inc(gains_loaded, 16)
            pool.dma_start(gain_fin, norm_final.partition_broadcast(P)).then_inc(gains_loaded, 16)
            pool.wait_ge(psum_filled, filled("q", 7))
            pool.dma_start(rb[:, 0:4], router_g_b.partition_broadcast(P).rearrange("p a n -> p (a n)")).then_inc(gains_loaded, 16)
            pool.dma_start(rb[:, 4:20], router_e_b.partition_broadcast(P).rearrange("p a g n -> p (a g n)")).then_inc(gains_loaded, 16)
            for c in range(4):
                pool.memset(desc[:, c:c + 1], 4.0 - c)
            for c in range(NE):
                ins = pool.memset(base_id[:, c:c + 1], float(CAP * c))
            pool.memset(m_cum[:, 0:16], 0.0)
            for k in range(N_OVER):
                pool.memset(o_k[:, k, :], k + 0.5)
            for q in range(5):
                ins = pool.memset(pre[q][:, 0:16], 0.0)
            ins.then_inc(index_ready, 1)
            for t in range(NT):
                pool.wait_ge(z_normed, t + 1)
                pool.dma_start(z_d[P * t:P * (t + 1), :], xn[:, t, :]).then_inc(z_stored, 16)
            pool.wait_ge(slots_ready, 1)
            pool.wait_ge(tok_ready, 1)
            pool.wait_ge(inv_zeroed, 16)
            for s in range(2):
                for t in range(NT):
                    pool.indirect_dma_start(out=inv_d, out_offset=bass.IndirectOffsetOnAxis(ap=slot_i[:, s, t:t + 1], axis=0),
                                            in_=tok_id[:, t:t + 1], in_offset=None).then_inc(inv_stored, 16)
            pool.wait_ge(inv_stored, 16 * 2 * NT)
            pool.dma_start(idx_all[:, :], inv_d.rearrange("(e p) o -> p (e o)", p=CAP), allow_slow_non_contiguous=True).then_inc(inv_loaded, 16)
            pool.wait_ge(inv_loaded, 16)
            pool.wait_ge(z_stored, 16 * NT)

            def gather(e, a):
                pool.tensor_copy(idx_one[:, :], idx_all[:, bass.ds(e, 1)] if not isinstance(e, int) else idx_all[:, e:e + 1]).then_inc(idx_ready, 1)
                pool.wait_ge(idx_ready, e + 1)
                pool.sem_inc(pool_tick, 1)
                pool.indirect_dma_start(out=xg[a], out_offset=None, in_=z_d,
                                        in_offset=bass.IndirectOffsetOnAxis(ap=idx_one[:, :], axis=0)).then_inc(gathered[a], 16)
            gather(0, 0)
            pool.wait_ge(gathered[0], 16)
            gather(1, 1)
            pool.wait_ge(gathered[1], 16)
            with pool.Fori(1, NE // 2) as i:
                for a in range(2):
                    pool.wait_ge(xg_used, 2 * i + a - 1)
                    gather(2 * i + a, a)
                    pool.wait_ge(gathered[a], 16 * i + 16)
            pool.wait_ge(tiles_ready, 1)
            n_over = pool.value_load(tile_i[0:1, N_OVER:N_OVER + 1], min_val=0, max_val=N_OVER)
            with pool.If(n_over > 0):
                with pool.Fori(0, n_over) as k:
                    pool.wait_ge(xg_used, NE)
                    pool.wait_ge(o_down, k + 1)
                    pool.tensor_copy(idx_one[:, :], idx_all[:, bass.ds(k + NE, 1)]).then_inc(o_idx, 1)
                    pool.wait_ge(o_idx, k + 1)
                    pool.sem_inc(pool_tick, 1)
                    pool.indirect_dma_start(out=xg[0], out_offset=None, in_=z_d,
                                            in_offset=bass.IndirectOffsetOnAxis(ap=idx_one[:, :], axis=0)).then_inc(o_gath, 16)
                    pool.wait_ge(o_gath, 16 * k + 16)
                pool.nop()
            with pool.Else():
                pool.nop()
            pool.wait_ge(all_stored, 1)
            pool.wait_ge(rows_filled, 32)
            for t in range(NT):
                if t >= 2:
                    pool.wait_ge(out_stored[t - 2], 16)
                pool.indirect_dma_start(out=yg1[t % 2], out_offset=None, in_=y_d,
                                        in_offset=bass.IndirectOffsetOnAxis(ap=slot_i[:, 0, t:t + 1], axis=0)).then_inc(back[t], 16)
                pool.indirect_dma_start(out=yg2[t % 2], out_offset=None, in_=y_d,
                                        in_offset=bass.IndirectOffsetOnAxis(ap=slot_i[:, 1, t:t + 1], axis=0)).then_inc(back[t], 16)

        @block.scalar
        def _(act):
            g = lamg
            act.dma_start(g[0], ssm_a_re[0]).then_inc(ssm_loaded, 16)
            act.dma_start(g[1], ssm_a_im[0]).then_inc(ssm_loaded, 16)
            act.dma_start(g[2][:, 0:1], ssm_log_dt.rearrange("a g -> g a"), allow_slow_non_contiguous=True).then_inc(ssm_loaded, 16)
            act.dma_start(cload[:, :, 0:64], ssm_c_re[0].rearrange("(t g) c n -> (g c) t n", t=4)).then_inc(ssmb_loaded, 16)
            act.dma_start(cload[:, :, 64:128], ssm_c_im[0].rearrange("(t g) c n -> (g c) t n", t=4)).then_inc(ssmb_loaded, 16)
            act.dma_start(gc(B_s)[0:64], ssm_b_re[0].rearrange("g n c -> n g c")).then_inc(ssmb_loaded, 16)
            act.dma_start(gc(B_s)[64:128], ssm_b_im[0].rearrange("g n c -> n g c")).then_inc(ssmb_loaded, 16)
            steps = [0]

            def link(ins):
                steps[0] += 1
                ins.then_inc(act_step, 1)
                act.wait_ge(act_step, steps[0])

            for t in range(NT):
                act.wait_ge(x_loaded[t], 16)
                if t:
                    act.wait_ge(x_squared, t)
                act.activation(ureg[:, 0:D], h[:, t, :], ACT.Square, scale=1 / 32, accum_out=ss_x[:, t:t + 1]).then_inc(x_squared, 1)
            act.wait_ge(ssm_loaded, 48)
            link(act.activation(g[2][:, 1:2], g[2][:, 0:1], ACT.Exp))
            act.activation(g[3], g[0], ACT.Exp, scale=g[2][:, 1:2]).then_inc(decay_ready, 1)
            for t in range(NT):
                act.wait_ge(x_rstd, t // 2 + 1)
                act.activation(h[:, t, :], h[:, t, :], ACT.Copy, scale=rs_x[:, t:t + 1]).then_inc(x_normed, 1)
            act.wait_ge(angle_ready, 2)
            act.activation(g[6], g[4], ACT.Sin)
            act.activation(g[7], g[5], ACT.Sin, scale=0.5).then_inc(sines_ready, 1)

            act.wait_ge(zero_stored, 16)
            act.wait_ge(inv_zeroed, 16)
            def v_drained(lo, hi):
                for m in range(lo, hi):
                    act.wait_ge(psum_filled, filled("v", m))
                    act.activation(vT[:, m, :], bank_of("v", m)[:, :], ACT.Copy).then_inc(act_drained, 1)

            v_drained(0, 2)
            act.wait_ge(psum_filled, filled("cT", 0))
            b = bank_of("cT", 0)
            act.activation(Cy[0:64], b[0:64, :], ACT.Copy)
            act.activation(Cy[64:128], b[64:128, :], ACT.Copy, scale=-1.0)
            act.activation(Cw[0:64], b[64:128, :], ACT.Copy, scale=-1.0)
            act.activation(Cw[64:128], b[0:64, :], ACT.Copy, scale=-1.0).then_inc(act_drained, 1)
            v_drained(2, 4)
            act.wait_ge(mem_loaded, 16)
            for t in range(MT):
                act.activation(msq[:, t, :], mem_tok[:, t, :], ACT.Square, scale=1 / 32, accum_out=ss_m[:, t:t + 1]).then_inc(mem_squared, 1)
            act.wait_ge(mem_squared, MT)
            for m in range(4):
                act.wait_ge(psum_filled, filled("zp", m))
                act.activation(zp[:, m, PADT:], bank_of("zp", m)[:, :], ACT.Copy).then_inc(act_drained, 1)
            for k in range(KD):
                act.activation(u_hi[:, k, :], uT[:, k, :], ACT.Copy).then_inc(u_rounded, 1)
            for q in range(8):
                act.wait_ge(psum_filled, filled("bT", q))
                act.activation(bpow_m[:, 4 * q:4 * q + 4, :], bank_of("bT", q)[:, :].rearrange("p (g m) -> p g m", g=4),
                               ACT.Copy).then_inc(act_drained, 1)
            for q in range(8):
                act.wait_ge(psum_filled, filled("kern", q))
                act.activation(kern_sb[:, 4 * q:4 * q + 4, :], bank_of("kern", q)[0:SSM_C, :].rearrange("p (g m) -> p g m", g=4),
                               ACT.Copy).then_inc(act_drained, 1)
            act.wait_ge(*drained("kern", 7))
            act.dma_start(kern_d[:, :, 7 * SSM_C:].rearrange("g c x -> c g x"), kern_sb).then_inc(kern_stored, 16)
            act.wait_ge(pool_diff, POOL_G)
            for l in range(LCH):
                act.wait_ge(psum_filled, filled("vl", l))
                act.activation(vj[:, :, LCH - 1 - l, :], bank_of("vl", l)[0:NCH, :].rearrange("p (g c) -> p g c", g=SSM_G),
                               ACT.Copy).then_inc(act_drained, 1)
            act.wait_ge(kern_stored, 16)
            for q in range(4):
                act.wait_ge(psum_filled, filled("vch", q))
                act.activation(vch[:, 8 * q:8 * q + 8, :], bank_of("vch", q)[:, :].rearrange("p (g q) -> p g q", g=8),
                               ACT.Copy).then_inc(act_drained, 1)
            for q in range(4):
                act.wait_ge(psum_filled, filled("st", q))
                b = bank_of("st", q)[:, :].rearrange("p (g q) -> p g q", g=8)
                gs = slice(8 * q, 8 * q + 8)
                act.activation(hin[:, gs, 0, :], b, ACT.Copy)
                act.activation(hin[0:64, gs, 1, :], b[64:128], ACT.Copy, scale=-1.0)
                act.activation(hin[64:128, gs, 1, :], b[0:64], ACT.Copy).then_inc(act_drained, 1)
            act.wait_ge(cols_loaded, 80)
            for g_ in range(4):
                act.wait_ge(psum_filled, filled("mix", g_))
                act.activation(ypT[:, g_, :], bank_of("mix", g_)[:, :], ACT.Copy, scale=pscale[:, g_:g_ + 1]).then_inc(act_drained, 1)
            for m in range(4):
                act.wait_ge(psum_filled, filled("kk", m))
                act.activation(kT[:, 2 * m:2 * m + 2, :], bank_of("kk", m)[:, :].rearrange("p (k m) -> p k m", k=2),
                               ACT.Copy).then_inc(act_drained, 1)
            for n in range(4):
                act.wait_ge(psum_filled, filled("vv", n))
                act.activation(vm[:, n % 2, HALF * (n // 2):HALF * (n // 2 + 1)], bank_of("vv", n)[:, :],
                               ACT.Copy).then_inc(act_drained, 1)

            def round_weights(name):
                j = SPLIT.index(name)
                act.wait_ge(*loaded(name))
                if j >= 2:
                    act.wait_ge(psum_filled, filled(*FRONT[CH[SPLIT[j - 2]]][2]))
                for c in range(2):
                    half = slice(2048 * c, 2048 * (c + 1))
                    act.activation(ring_r[hi_slot(name)][:, half], ring[CH[name] % RAW][:, half], ACT.Copy).then_inc(weight_hi, 1)

            round_weights("g0")
            round_weights("g1")

            def gates(lo, hi):
                for m in range(lo, hi):
                    act.wait_ge(psum_filled, filled("gate", m))
                    act.activation(gT[:, m, :], bank_of("gate", m)[:, :], ACT.Sigmoid).then_inc(act_drained, 1)

            gates(0, 6)
            round_weights("g2")
            gates(6, 8)
            for m in range(4):
                act.wait_ge(*drained("yT", m))
                act.activation(ygT[:, m, :], vT[:, m, :], ACT.Gelu_apprx_tanh).then_inc(gelu_ready, 1)
            for m in range(4):
                act.activation(yp_hi[:, m, :], ypT[:, m, :], ACT.Copy).then_inc(yp_rounded, 1)
            for m in range(4):
                act.wait_ge(psum_filled, filled("glu", m))
                act.activation(vT[:, m, :], bank_of("glu", m)[:, :], ACT.Sigmoid, bias=glub[:, m:m + 1]).then_inc(act_drained, 1)
            for m in range(4):
                act.wait_ge(ys_ready, m + 1)
                act.activation(ys_hi[:, m, :], ysT[:, m, :], ACT.Copy).then_inc(ys_rounded, 1)
            gates(8, 10)
            round_weights("g3")
            gates(10, 13)
            round_weights("bp")
            gates(13, 16)
            round_weights("bs")
            round_weights("o0")
            for m in range(KD):
                act.wait_ge(mg_exact, m + 1)
                act.activation(mg_hi[:, m, :], gT[:, m, :], ACT.Copy).then_inc(mg_rounded, 1)
            round_weights("o1")

            def round_hn(t):
                for n in range(2):
                    act.wait_ge(*drained("hT", 2 * t + n))
                    act.activation(hn_hi[:, 4 * n:4 * n + 4, P * t:P * (t + 1)], hnT[:, 4 * n:4 * n + 4, P * t:P * (t + 1)],
                                   ACT.Copy).then_inc(hn_rounded, 1)

            for t in range(NT):
                act.wait_ge(*drained("wo1", 2 * t + 1))
                act.activation(xn[:, t, :], h[:, t, :], ACT.Square, scale=1 / 32, accum_out=ss_h[:, t:t + 1]).then_inc(h_squared, 1)
                if t >= 1:
                    round_hn(t - 1)
            round_weights("q0")
            round_hn(NT - 1)
            round_weights("q1")
            for m in range(8):
                act.wait_ge(psum_filled, filled("q", m))
                act.activation(qT[:, m, :], bank_of("q", m)[:, :], ACT.Copy).then_inc(act_drained, 1)
                if m == 5:
                    round_weights("w0")

            def probs(hd):
                for n in range(2):
                    act.wait_ge(neg_max, 2 * hd + n + 1)
                    if hd >= 2 and n == 0:
                        act.wait_ge(psum_filled, filled("pT", 2 * hd - 3))
                    b = bank_of("sc", 2 * hd + n)[:, :].rearrange("p (t m) -> p t m", t=2)
                    for s in range(2):
                        t = 2 * n + s
                        ins = act.activation(prob[:, hd % 2, t, :], b[:, s, :], ACT.Exp, scale=HD ** -0.5,
                                             bias=nmax[:, 4 * hd + t:4 * hd + t + 1], accum_out=esum[:, 4 * hd + t:4 * hd + t + 1])
                    ins.then_inc(act_drained, 1)

            def round_o(hd):
                for n in range(2):
                    act.wait_ge(*drained("pv", 2 * hd + n))
                    act.activation(o_hi[:, 2 * hd + n, :], oT[:, 2 * hd + n, :], ACT.Copy).then_inc(o_rounded, 1)

            for hd in range(HEADS + 1):
                if hd < HEADS:
                    probs(hd)
                if hd >= 1:
                    for n in range(2):
                        act.wait_ge(psum_filled, filled("pT", 2 * (hd - 1) + n))
                        act.activation(probT[:, (hd - 1) % 2, n, :], bank_of("pT", 2 * (hd - 1) + n)[:, :], ACT.Copy).then_inc(act_drained, 1)
                if hd == 0:
                    round_weights("w1")
                if hd >= 2:
                    round_o(hd - 2)
            round_o(HEADS - 1)

            def z_transposed(t):
                for n in range(2):
                    act.wait_ge(psum_filled, filled("zT", 2 * t + n))
                    act.activation(zT[:, 4 * n:4 * n + 4, P * t:P * (t + 1)],
                                   bank_of("zT", 2 * t + n)[:, :].rearrange("p (k t) -> p k t", k=4), ACT.Copy).then_inc(act_drained, 1)

            for t in range(NT):
                act.wait_ge(*drained("wo2", 2 * t + 1))
                if t == 0:
                    act.wait_ge(psum_filled, filled("pv", 7))
                act.activation(xn[:, t, :], h[:, t, :], ACT.Square, scale=1 / 32, accum_out=ss_z[:, t:t + 1]).then_inc(z_squared, 1)
                if t >= 1:
                    z_transposed(t - 1)
            z_transposed(NT - 1)
            act.wait_ge(g_shift, 1)
            act.activation(q4[0], q4[1], ACT.Exp).then_inc(g_exp, 1)
            act.wait_ge(e_shift, 1)
            act.activation(r4[1], r4[2], ACT.Exp).then_inc(e_exp, 1)

            act.sem_inc(silu_ready, 2)
            act.sem_inc(y_act, 1)

            def expert(e, a, n_st):
                act.wait_ge(up_done, e + 1)
                act.wait_ge(hid_ready, e + 1)
                act.activation(silu[a], bank[2 + 4 * a][:, 0:4 * CAP], ACT.Silu).then_inc(silu_ready, 1)
                act.wait_ge(down_done, 2 * e + 2)
                if n_st is not None:
                    act.wait_ge(y_stored[a], n_st)
                act.activation(ysb[a][:, HALF:D], bank[5][0:CAP, :], ACT.Copy).then_inc(y_act, 1)
                act.wait_ge(y_act, e + 2)
                act.wait_ge(y_dve, e + 2)
                act.dma_start(y_d[bass.ds(e * CAP, CAP), :], ysb[a]).then_inc(y_stored[a], 16)

            expert(0, 0, None)
            expert(1, 1, None)
            with act.Fori(1, NE // 2) as i:
                for a in range(2):
                    expert(2 * i + a, a, 16 * i)
            act.wait_ge(y_stored[0], 8 * NE)
            act.wait_ge(y_stored[1], 8 * NE)
            act.wait_ge(tiles_ready, 1)
            n_over = act.value_load(tile_i[0:1, N_OVER:N_OVER + 1], min_val=0, max_val=N_OVER)
            with act.If(n_over > 0):
                act.wait_ge(rows_filled, 32)
                with act.Fori(0, n_over) as k:
                    act.wait_ge(o_up, k + 1)
                    act.activation(silu[0], bank[2][:, 0:4 * CAP], ACT.Silu).then_inc(o_silu, 1)
                    act.wait_ge(o_y, k + 1)
                    act.dma_start(y_d[bass.ds((k + NE) * CAP, CAP), :], ysb[0]).then_inc(o_stored, 16)
                    act.wait_ge(o_stored, 16 * k + 16)
                act.nop()
            with act.Else():
                act.nop()
            act.sem_inc(all_stored, 1)
            for t in range(NT):
                act.wait_ge(combined, t + 1)
                if t:
                    act.wait_ge(o_squared, t)
                act.activation(ureg[:, 0:D], h[:, t, :], ACT.Square, scale=1 / 32, accum_out=ss_o[:, t:t + 1]).then_inc(o_squared, 1)

        @block.vector
        def _(dve):
            V = nc.vector
            steps = [0]

            def link(ins):
                steps[0] += 1
                ins.then_inc(dve_step, 1)
                dve.wait_ge(dve_step, steps[0])

            def tt(o_, a, b, op):
                return V.tensor_tensor(out=o_, in0=a, in1=b, op=op)

            def ts(o_, a, s1, op0, s2=None, op1=None):
                if op1 is None:
                    return V.tensor_scalar(o_, a, s1, None, op0)
                return V.tensor_scalar(o_, a, s1, s2, op0, op1)

            def rstd(o_, ss, done=None):
                n = ss.shape[1]
                v, t_ = newton[:, 0:n], newton[:, 4:4 + n]
                link(ts(v, ss, EPS, ALU.add))
                link(ts(t_.bitcast(i32), v.bitcast(i32), 1, ALU.logical_shift_right))
                link(ts(o_.bitcast(i32), t_.bitcast(i32), -1.0, ALU.mult, float(0x5F3759DF), ALU.add))
                for r in range(3):
                    link(tt(t_, o_, o_, ALU.mult))
                    link(V.scalar_tensor_tensor(out=t_, in0=t_, scalar=-0.5, in1=v, op0=ALU.mult, op1=ALU.mult))
                    ins = V.scalar_tensor_tensor(out=o_, in0=t_, scalar=1.5, in1=o_, op0=ALU.add, op1=ALU.mult)
                    if r == 2 and done is not None:
                        ins.then_inc(done, 1)
                    else:
                        link(ins)

            for q in range(2):
                dve.wait_ge(x_squared, 2 * q + 2)
                rstd(rs_x[:, 2 * q:2 * q + 2], ss_x[:, 2 * q:2 * q + 2], x_rstd)
            dve.wait_ge(gain_loaded, 16)

            def transposed(name, i, dst, gain):
                dve.wait_ge(psum_filled, filled(name, i))
                tt(dst, bank_of(name, i)[:, :].rearrange("p (k t) -> p k t", k=4), gain.unsqueeze(2).to_broadcast([P, 4, P]),
                   ALU.mult).then_inc(dve_drained, 1)

            for i in range(8):
                t, n = i // 2, i % 2
                transposed("xT", i, uT[:, 4 * n:4 * n + 4, P * t:P * (t + 1)], gain_mix[:, 4 * n:4 * n + 4])
            g = lamg
            TWO_PI = 2 * math.pi
            c1 = 6.28125
            c2 = float(int((TWO_PI - c1) * 2 ** 22)) / 2 ** 22
            c3 = TWO_PI - c1 - c2
            MAGIC = 1.5 * 2.0 ** 23
            dve.wait_ge(decay_ready, 1)
            link(ts(g[8], g[1], g[2][:, 1:2], ALU.mult))
            link(ts(g[9], g[8], 1 / TWO_PI, ALU.mult, MAGIC, ALU.add))
            link(ts(g[9], g[9], MAGIC, ALU.subtract))
            for c in (c1, c2, c3):
                link(V.scalar_tensor_tensor(out=g[8], in0=g[9], scalar=-c, in1=g[8], op0=ALU.mult, op1=ALU.add))
            ts(g[4], g[8], 3.1415925, ALU.min, -3.1415925, ALU.max).then_inc(angle_ready, 1)
            ts(g[5], g[8], 3.1415925, ALU.min, -3.1415925, ALU.max).then_inc(angle_ready, 1)
            dve.wait_ge(sines_ready, 1)
            link(tt(g[10], g[7], g[7], ALU.mult))
            link(ts(g[10], g[10], -2.0, ALU.mult, 1.0, ALU.add))
            link(tt(g[11], g[3], g[10], ALU.mult))
            link(tt(g[12], g[3], g[6], ALU.mult))
            link(tt(g[13], g[0], g[0], ALU.mult))
            link(tt(g[14], g[1], g[1], ALU.mult))
            link(tt(g[13], g[13], g[14], ALU.add))
            link(V.reciprocal(g[13], g[13]))
            link(ts(g[15], g[11], 1.0, ALU.subtract))
            link(tt(g[16], g[15], g[0], ALU.mult))
            link(tt(g[17], g[12], g[1], ALU.mult))
            link(tt(g[16], g[16], g[17], ALU.add))
            link(tt(g[18], g[12], g[0], ALU.mult))
            link(tt(g[19], g[15], g[1], ALU.mult))
            link(tt(g[18], g[18], g[19], ALU.subtract))
            link(tt(g[16], g[16], g[13], ALU.mult))
            link(tt(g[18], g[18], g[13], ALU.mult))
            for n, s in enumerate((11, 12, 16, 18)):
                ins = V.tensor_copy(lamq[:, n, :, :], g[s].unsqueeze(1).to_broadcast([SSM_G, 2, SSM_N]))
            ins.then_inc(lam_ready, 1)

            dve.wait_ge(psum_filled, filled("lam", 0))
            V.tensor_copy(lamL, bank_of("lam", 0)[:, 0:4 * SSM_G].rearrange("p (q g) -> p q g", q=4)).then_inc(dve_drained, 1)
            dve.wait_ge(*drained("lam", 0))
            LR, LI, FR, FI = (lamL[:, n, :] for n in range(4))
            over_c = lambda a: a.unsqueeze(2).to_broadcast([P, SSM_G, SSM_C])
            dve.wait_ge(ssmb_loaded, 64)

            def swapped(dst, src):
                link(ts(dst[0:64], src[64:128], -1.0, ALU.mult))
                link(V.tensor_copy(dst[64:128], src[0:64]))

            swapped(B_w, B_s)
            t1 = gtmp[:, 0:512]
            link(tt(gc(Bb), gc(B_s), over_c(FR), ALU.mult))
            link(tt(gc(t1), gc(B_w), over_c(FI), ALU.mult))
            link(tt(Bb, Bb, t1, ALU.add))
            swapped(Bbw, Bb)

            def powers(dst, base_r, base_i, tmp_at):
                link(V.tensor_copy(dst[:, 0, 0, :], base_r))
                link(V.tensor_copy(dst[:, 0, 1, :], base_i))
                n = 1
                while n < 8:
                    lo = dst[:, 0:n]
                    br = dst[:, n - 1, 0, :].unsqueeze(1).to_broadcast([P, n, SSM_G])
                    bi = dst[:, n - 1, 1, :].unsqueeze(1).to_broadcast([P, n, SSM_G])
                    tmp = tmp_at[:, 0:n * SSM_G].rearrange("p (k g) -> p k g", k=n)
                    hi = dst[:, n:2 * n]
                    link(tt(hi[:, :, 0, :], lo[:, :, 0, :], br, ALU.mult))
                    link(tt(tmp, lo[:, :, 1, :], bi, ALU.mult))
                    link(tt(hi[:, :, 0, :], hi[:, :, 0, :], tmp, ALU.subtract))
                    link(tt(hi[:, :, 1, :], lo[:, :, 0, :], bi, ALU.mult))
                    link(tt(tmp, lo[:, :, 1, :], br, ALU.mult))
                    link(tt(hi[:, :, 1, :], hi[:, :, 1, :], tmp, ALU.add))
                    n *= 2

            powers(pw, LR, LI, gtmp[:, 512:640])
            dve.wait_ge(*drained("cT", 0))
            link(V.tensor_copy(bpow[:, :, 0, :], gc(Bb)))

            def scaled(dst, a, b, lo, n):
                four = [P, SSM_G, n, SSM_C]
                bc = lambda v: gc(v).unsqueeze(2).to_broadcast(four)
                pr, pi = (pw[:, lo:lo + n, x_, :].rearrange("p k g -> p g k").unsqueeze(3).to_broadcast(four) for x_ in range(2))
                tmp = gtmp_k[:, :, 0:n, :]
                link(tt(dst, bc(a), pr, ALU.mult))
                link(tt(tmp, bc(b), pi, ALU.mult))
                return tt(dst, dst, tmp, ALU.add)

            link(scaled(bpow[:, :, 1:5, :], Bb, Bbw, 0, 4))
            link(scaled(bpow[:, :, 5:8, :], Bb, Bbw, 4, 3))
            link(scaled(cpow[:, :, 0:4, :], Cy, Cw, 0, 4))
            scaled(cpow[:, :, 4:8, :], Cy, Cw, 4, 4).then_inc(powers_ready, 1)
            powers(lam8, pw[:, 7, 0, :], pw[:, 7, 1, :], B_s)

            dve.wait_ge(mem_squared, MT)
            rstd(rs_m, ss_m, mem_rstd)
            dve.wait_ge(mem_rstd, 1)
            for t in range(MT):
                ts(mem_tok[:, t, :], mem_tok[:, t, :], rs_m[:, t:t + 1], ALU.mult).then_inc(mem_normed, 1)
            for i in range(4):
                t, n = i // 2, i % 2
                transposed("memT", i, memT[:, 4 * n:4 * n + 4, P * t:P * (t + 1)], gain_mem[:, 4 * n:4 * n + 4])

            for b in range(2):
                link(V.memset(ptmp[:, b, 0:PADT], 0.0))
            link(V.memset(zp[:, :, 0:PADT], 0.0))
            dve.wait_ge(counts_ready, 1)
            for gi in range(POOL_G):
                dve.wait_ge(*drained("zp", gi))
                src, w = zp[:, gi, :], 1
                for s in range(gi + 1):
                    dst = ptmp[:, s % 2, :]
                    link(tt(dst[:, PADT:], src[:, PADT:], src[:, PADT - w:PADT + SEQ - w], ALU.add))
                    src, w = dst, 2 * w
                link(V.scalar_tensor_tensor(out=zp[:, gi, 2 * PADT:], in0=src[:, 2 * PADT:], scalar=1.0 / w,
                                            in1=zp[:, gi, 2 * PADT:], op0=ALU.mult, op1=ALU.subtract))
                link(tt(src[:, PADT:2 * PADT], src[:, PADT:2 * PADT], cntinv[:, gi, :], ALU.mult))
                ins = tt(zp[:, gi, PADT:2 * PADT], src[:, PADT:2 * PADT], zp[:, gi, PADT:2 * PADT], ALU.subtract)
                ins.then_inc(pool_diff, 1)
                dve.wait_ge(pool_diff, gi + 1)

            def lo_of(lo, exact, hi):
                return tt(lo, exact, hi, ALU.subtract)

            def weights_lo(name):
                j = SPLIT.index(name)
                for c in range(2):
                    half = slice(2048 * c, 2048 * (c + 1))
                    s_ = CH[name] % RAW
                    dve.wait_ge(weight_hi, 2 * j + c + 1)
                    lo_of(ring_r[s_][:, half], ring[s_][:, half], ring_r[hi_slot(name)][:, half]).then_inc(weight_lo, 1)

            dve.wait_ge(psum_filled, filled("zp", 3))
            for k in range(KD):
                dve.wait_ge(u_rounded, k + 1)
                lo_of(u_lo[:, k, :], uT[:, k, :], u_hi[:, k, :]).then_inc(u_split, 1)

            dve.wait_ge(*drained("st", 3))
            A1 = stmp[:, 0:512].rearrange("p (g x s) -> p g x s", g=SSM_G, x=2)
            A2 = stmp[:, 512:1024].rearrange("p (g x s) -> p g x s", g=SSM_G, x=2)
            S = stmp[:, 1024:1536].rearrange("p (g x s) -> p g x s", g=SSM_G, x=2)
            l8r, l8i = lam8[:, 0, 0, :], lam8[:, 0, 1, :]
            gxs = [P, SSM_G, 2, SUP]
            for j in range(1, SUP):
                old, new = W[:, :, :, :, j - 1], W[:, :, :, :, j]
                link(tt(A1, old, l8r.unsqueeze(2).unsqueeze(3).to_broadcast(gxs), ALU.mult))
                im = l8i.unsqueeze(2).to_broadcast([P, SSM_G, SUP])
                link(tt(A2[:, :, 0, :], old[:, :, 1, :], im, ALU.mult))
                link(V.scalar_tensor_tensor(out=A2[:, :, 1, :], in0=old[:, :, 0, :], scalar=-1.0, in1=im, op0=ALU.mult, op1=ALU.mult))
                link(tt(A1, A1, A2, ALU.add))
                link(tt(new, new, A1, ALU.add))
            link(V.memset(S[:, :, :, 0], 0.0))
            l64r, l64i = lam8[:, 7, 0, :], lam8[:, 7, 1, :]
            for s in range(SUP - 1):
                old, new = S[:, :, :, s], S[:, :, :, s + 1]
                link(tt(A1[:, :, :, 0], old, l64r.unsqueeze(2).to_broadcast([P, SSM_G, 2]), ALU.mult))
                link(tt(A2[:, :, 0, 0], old[:, :, 1], l64i, ALU.mult))
                link(V.scalar_tensor_tensor(out=A2[:, :, 1, 0], in0=old[:, :, 0], scalar=-1.0, in1=l64i, op0=ALU.mult, op1=ALU.mult))
                link(tt(A1[:, :, :, 0], A1[:, :, :, 0], A2[:, :, :, 0], ALU.add))
                link(tt(new, A1[:, :, :, 0], W[:, :, :, s, SUP - 1], ALU.add))
            Hn = W[:, :, 1, :, :]
            link(V.tensor_copy(Hn[:, :, :, 0], S[:, :, 0, :]))
            for j in range(1, SUP):
                pr, pi = (lam8[:, j - 1, x_, :].unsqueeze(2).to_broadcast([P, SSM_G, SUP]) for x_ in range(2))
                B1, B2 = A1[:, :, 0, :], A2[:, :, 0, :]
                link(tt(B1, S[:, :, 0, :], pr, ALU.mult))
                link(tt(B2, S[:, :, 1, :], pi, ALU.mult))
                link(tt(B1, B1, B2, ALU.add))
                ins = tt(Hn[:, :, :, j], B1, W[:, :, 0, :, j - 1], ALU.add)
                if j < SUP - 1:
                    link(ins)
            ins.then_inc(states_ready, 1)
            weights_lo("g0")
            for q in range(8):
                dve.wait_ge(psum_filled, filled("y", q | 1))
                n = q % 2
                V.tensor_copy(yj_g[:, q // 2, 4 * n:4 * n + 4, :, :],
                              bank_of("y", q)[0:NCH, :].rearrange("p (g l c) -> p g l c", g=4, l=LCH)).then_inc(dve_drained, 1)
            weights_lo("g1")
            jl = lambda a: a.rearrange("p (j l) -> p l j", l=LCH)
            for m in range(4):
                dve.wait_ge(psum_filled, filled("yT", m))
                V.scalar_tensor_tensor(out=jl(vT[:, m, :]), in0=jl(vT[:, m, :]), scalar=dskip[:, m:m + 1],
                                       in1=bank_of("yT", m)[:, :].rearrange("p (l j) -> p l j", l=LCH),
                                       op0=ALU.mult, op1=ALU.add).then_inc(dve_drained, 1)
            weights_lo("g2")
            for m in range(4):
                dve.wait_ge(yp_rounded, m + 1)
                lo_of(yp_lo[:, m, :], ypT[:, m, :], yp_hi[:, m, :]).then_inc(yp_split, 1)
            for m in range(4):
                dve.wait_ge(*drained("glu", m))
                tt(ysT[:, m, :], vT[:, m, :], ygT[:, m, :], ALU.mult).then_inc(ys_ready, 1)
            for m in range(4):
                dve.wait_ge(ys_rounded, m + 1)
                lo_of(ys_lo[:, m, :], ysT[:, m, :], ys_hi[:, m, :]).then_inc(ys_split, 1)
            weights_lo("g3")
            weights_lo("bp")
            dve.wait_ge(*drained("gate", 15))
            for m in range(KD):
                dve.wait_ge(psum_filled, filled("bp", m))
                tt(gT[:, m, :], gT[:, m, :], bank_of("bp", m)[:, :], ALU.mult).then_inc(dve_drained, 1)
                if m == 1:
                    weights_lo("bs")
            for m in range(KD + 1):
                if m < KD:
                    dve.wait_ge(psum_filled, filled("bs", m))
                    tt(gT[:, KD + m, :], gT[:, KD + m, :], bank_of("bs", m)[:, :], ALU.mult).then_inc(dve_drained, 1)
                    dve.wait_ge(*drained("bs", m))
                    tt(gT[:, m, :], gT[:, m, :], gT[:, KD + m, :], ALU.add).then_inc(mg_exact, 1)
                    if m == 1:
                        weights_lo("o0")
                if m >= 1:
                    dve.wait_ge(mg_rounded, m)
                    lo_of(mg_lo[:, m - 1, :], gT[:, m - 1, :], mg_hi[:, m - 1, :]).then_inc(merged_ready, 1)
            weights_lo("o1")
            dve.wait_ge(h_loaded, 16)

            def normed(t):
                dve.wait_ge(h_squared, t + 1)
                rstd(rs_h[:, t:t + 1], ss_h[:, t:t + 1])
                ts(xn[:, t, :], h[:, t, :], rs_h[:, t:t + 1], ALU.mult).then_inc(h_normed, 1)

            def h_transposed(t):
                for n in range(2):
                    transposed("hT", 2 * t + n, hnT[:, 4 * n:4 * n + 4, P * t:P * (t + 1)], gain_x[:, 4 * n:4 * n + 4])

            def residual(name, t):
                for n in range(2):
                    dve.wait_ge(psum_filled, filled(name, 2 * t + n))
                    hs = h[:, t, HALF * n:HALF * (n + 1)]
                    tt(hs, hs, bank_of(name, 2 * t + n)[:, :], ALU.add).then_inc(dve_drained, 1)

            def hn_remainder(t):
                for n in range(2):
                    at_ = (slice(None), slice(4 * n, 4 * n + 4), slice(P * t, P * (t + 1)))
                    dve.wait_ge(hn_rounded, 2 * t + n + 1)
                    lo_of(hn_lo[at_], hnT[at_], hn_hi[at_]).then_inc(hn_split, 1)

            for t in range(NT):
                residual("wo1", t)
                normed(t)
                if t >= 1:
                    h_transposed(t - 1)
                if t >= 2:
                    hn_remainder(t - 2)
            h_transposed(NT - 1)
            hn_remainder(NT - 2)
            weights_lo("q0")
            hn_remainder(NT - 1)
            weights_lo("q1")
            weights_lo("w0")
            def maxima(hd):
                for n in range(2):
                    dve.wait_ge(psum_filled, filled("sc", 2 * hd + n))
                    at_ = 4 * hd + 2 * n
                    link(V.tensor_reduce(out=rmax[:, at_:at_ + 2], in_=bank_of("sc", 2 * hd + n)[:, :].rearrange("p (t m) -> p t m", t=2),
                                         axis=AX.X, op=ALU.max))
                    ts(nmax[:, at_:at_ + 2], rmax[:, at_:at_ + 2], -HD ** -0.5, ALU.mult).then_inc(neg_max, 1)

            def divide(hd):
                for n in range(2):
                    dve.wait_ge(*drained("sc", 2 * hd + n))
                    at_ = 4 * hd + 2 * n
                    link(V.reciprocal(rsum[:, at_:at_ + 2], esum[:, at_:at_ + 2]))
                    for s in range(2):
                        t = 2 * n + s
                        ins = ts(prob[:, hd % 2, t, :], prob[:, hd % 2, t, :], rsum[:, at_ + s:at_ + s + 1], ALU.mult)
                    ins.then_inc(prob_ready, 1)

            maxima(0)
            def o_remainder(hd):
                for n in range(2):
                    dve.wait_ge(o_rounded, 2 * hd + n + 1)
                    lo_of(o_lo[:, 2 * hd + n, :], oT[:, 2 * hd + n, :], o_hi[:, 2 * hd + n, :]).then_inc(o_split, 1)

            for hd in range(HEADS + 1):
                if hd < HEADS:
                    divide(hd)
                if hd + 1 < HEADS:
                    maxima(hd + 1)
                if hd == 1:
                    weights_lo("w1")
                if hd >= 3:
                    o_remainder(hd - 3)
                if hd >= 1:
                    for n in range(2):
                        dve.wait_ge(psum_filled, filled("pv", 2 * (hd - 1) + n))
                        V.tensor_copy(oT[:, 2 * (hd - 1) + n, :], bank_of("pv", 2 * (hd - 1) + n)[:, :]).then_inc(dve_drained, 1)
            o_remainder(HEADS - 2)
            o_remainder(HEADS - 1)
            dve.wait_ge(gains_loaded, 64)

            def logits_of(t):
                dve.wait_ge(psum_filled, filled("route", t))
                tt(logits[:, t, :], bank_of("route", t)[:, 0:20], rb, ALU.add).then_inc(dve_drained, 1)

            for t in range(NT):
                residual("wo2", t)
                dve.wait_ge(z_squared, t + 1)
                rstd(rs_z[:, t:t + 1], ss_z[:, t:t + 1])
                V.scalar_tensor_tensor(out=xn[:, t, :], in0=h[:, t, :], scalar=rs_z[:, t:t + 1], in1=gain_ffn,
                                       op0=ALU.mult, op1=ALU.mult).then_inc(z_normed, 1)
                if t >= 2:
                    logits_of(t - 2)
            logits_of(NT - 2)

            t4 = lambda a: a.unsqueeze(2).to_broadcast([P, NT, 4])
            n4 = lambda a: a.unsqueeze(1).to_broadcast([P, NT, 4])
            ts4 = lambda a: a.unsqueeze(1).to_broadcast([P, NT, 16])
            dve.wait_ge(index_ready, 1)
            logits_of(NT - 1)
            dve.wait_ge(*drained("route", NT - 1))

            def first_max(mask, top, src, t_a, t_b):
                link(V.tensor_reduce(out=top, in_=src, axis=AX.X, op=ALU.max))
                link(tt(t_a, src, t4(top), ALU.is_equal))
                link(tt(t_a, t_a, n4(desc), ALU.mult))
                link(V.tensor_reduce(out=t_b, in_=t_a, axis=AX.X, op=ALU.max))
                link(tt(mask, t_a, t4(t_b), ALU.is_equal))

            gmask, esel, top1, top2, e2 = q4[2], q4[3], q4[4], q4[5], q4[6]
            first_max(gmask, r4[3], lg, q4[7], r4[4])
            tt(q4[1], lg, t4(r4[3]), ALU.subtract).then_inc(g_shift, 1)
            le4 = le.rearrange("p t (g e) -> p t g e", g=4)
            link(tt(e64[0].rearrange("p t (g e) -> p t g e", g=4), le4, gmask.unsqueeze(3).to_broadcast([P, NT, 4, 4]), ALU.mult))
            link(V.tensor_reduce(out=esel, in_=e64[0].rearrange("p t (g e) -> p t e g", g=4), axis=AX.X, op=ALU.add))
            first_max(top1, r4[5], esel, q4[7], r4[4])
            link(ts(q4[8], top1, -1.0, ALU.mult, 1.0, ALU.add))
            link(tt(e2, esel, q4[8], ALU.mult))
            link(ts(q4[9], top1, -3.0e38, ALU.mult))
            link(tt(e2, e2, q4[9], ALU.add))
            first_max(top2, r4[6], e2, q4[7], r4[4])
            tt(r4[2], r4[6], r4[5], ALU.subtract).then_inc(e_shift, 1)
            for n, tm in ((1, top1), (2, top2)):
                link(tt(e64[n].rearrange("p t (g e) -> p t g e", g=4), gmask.unsqueeze(3).to_broadcast([P, NT, 4, 4]),
                        tm.unsqueeze(2).to_broadcast([P, NT, 4, 4]), ALU.mult))
            link(tt(e64[3], e64[1], e64[2], ALU.add))
            mc = m_cum.rearrange("p (t n) -> p t n", t=5)
            link(V.tensor_copy(mc[:, 1, :], e64[3][:, 0, :]))
            for t in range(1, NT):
                ins = tt(mc[:, t + 1, :], mc[:, t, :], e64[3][:, t, :], ALU.add)
                if t < NT - 1:
                    link(ins)
            ins.then_inc(mask_ready, 1)
            dve.wait_ge(g_exp, 1)
            link(V.tensor_reduce(out=r4[7], in_=q4[0], axis=AX.X, op=ALU.add))
            link(V.reciprocal(r4[7], r4[7]))
            dve.wait_ge(e_exp, 1)
            link(ts(r4[8], r4[1], 1.0, ALU.add))
            link(V.reciprocal(r4[8], r4[8]))
            link(tt(gw[:, 0, :], r4[8], r4[7], ALU.mult))
            link(tt(gw[:, 1, :], gw[:, 0, :], r4[1], ALU.mult))
            dve.wait_ge(psum_filled, filled("rank", 0))
            rk = bank_of("rank", 0)
            V.tensor_copy(x64, rk[:, 0:64].rearrange("p (t n) -> p t n", t=NT))
            V.tensor_copy(n16[0], rk[:, 64:80]).then_inc(dve_drained, 1)
            dve.wait_ge(*drained("rank", 0))
            link(ts(n16[1], n16[0], CAP + 0.5, ALU.is_gt))
            for k in range(2, -(-SEQ // CAP)):
                link(V.scalar_tensor_tensor(out=n16[1], in0=n16[0], scalar=CAP * k + 0.5, in1=n16[1], op0=ALU.is_gt, op1=ALU.add))
            link(V.tensor_copy(pre[0][:, 16:], n16[1]))
            for s, sh in enumerate((1, 2, 4, 8)):
                link(tt(pre[s + 1][:, 16:], pre[s][:, 16:], pre[s][:, 16 - sh:32 - sh], ALU.add))
            incl = pre[4][:, 16:]
            link(tt(n16[7], incl, n16[1], ALU.subtract))
            link(ts(n16[7], n16[7], NE - 1.0, ALU.add, float(CAP), ALU.mult))
            link(tt(n16[7], n16[7], base_id, ALU.subtract))
            link(ts(e64[4], x64, CAP - 0.5, ALU.is_gt))
            link(tt(e64[4], e64[4], ts4(n16[7]), ALU.mult))
            link(tt(e64[4], e64[4], ts4(base_id), ALU.add))
            link(tt(e64[4], e64[4], x64, ALU.add))
            for n in range(2):
                link(tt(e64[5], e64[4], e64[1 + n], ALU.mult))
                link(V.tensor_reduce(out=slot_f[:, n, :], in_=e64[5], axis=AX.X, op=ALU.add))
            V.tensor_copy(slot_i[:, :, :], slot_f).then_inc(slots_ready, 1)
            link(tt(o_lt, incl.unsqueeze(1).to_broadcast([P, N_OVER, NE]), o_k, ALU.is_lt))
            link(V.tensor_reduce(out=tile_row[:, 0:N_OVER], in_=o_lt, axis=AX.X, op=ALU.add))
            link(V.tensor_copy(tile_row[:, N_OVER:N_OVER + 1], incl[:, NE - 1:NE]))
            link(ts(tile_row[:, 0:N_OVER], tile_row[:, 0:N_OVER], NE - 1.0, ALU.min))
            V.tensor_copy(tile_i[:, 0:N_OVER + 1], tile_row[:, 0:N_OVER + 1]).then_inc(tiles_ready, 1)

            dve.sem_inc(hid_ready, 2)
            dve.sem_inc(zs_ready, 1)
            dve.sem_inc(y_dve, 1)
            dve.wait_ge(z_stored, 16 * NT)

            def rows_transposed(e, a):
                dve.wait_ge(xg_used, e + 1)
                V.tensor_copy(zsT[a][:, 0:4, :], bank[0][:, 0:4 * CAP].rearrange("p (k t) -> p k t", k=4))
                V.tensor_copy(zsT[a][:, 4:8, :], bank[1][:, 0:4 * CAP].rearrange("p (k t) -> p k t", k=4)).then_inc(zs_ready, 1)

            def expert(e, a):
                dve.wait_ge(silu_ready, e + 3)
                dve.wait_ge(gate_done, e + 1)
                tt(hid[a].rearrange("p k t -> p (k t)"), silu[a], bank[3 + 4 * a][:, 0:4 * CAP], ALU.mult).then_inc(hid_ready, 1)

            def left(e, a, n_st):
                dve.wait_ge(down_done, 2 * e + 1)
                if n_st is not None:
                    dve.wait_ge(y_stored[a], n_st)
                V.tensor_copy(ysb[a][:, 0:HALF], bank[4][0:CAP, :]).then_inc(y_dve, 1)

            rows_transposed(0, 0)
            expert(0, 0)
            rows_transposed(1, 1)
            left(0, 0, None)
            expert(1, 1)
            rows_transposed(2, 0)
            left(1, 1, None)
            with dve.Fori(1, NE // 2 - 1) as i:
                for a in range(2):
                    expert(2 * i + a, a)
                    rows_transposed(2 * i + a + 1, 1 - a)
                    left(2 * i + a, a, 16 * i)
            expert(NE - 2, 0)
            rows_transposed(NE - 1, 1)
            left(NE - 2, 0, 8 * (NE - 2))
            expert(NE - 1, 1)
            left(NE - 1, 1, 8 * (NE - 2))
            dve.wait_ge(tiles_ready, 1)
            n_over = dve.value_load(tile_i[0:1, N_OVER:N_OVER + 1], min_val=0, max_val=N_OVER)
            with dve.If(n_over > 0):
                with dve.Fori(0, n_over) as k:
                    dve.wait_ge(o_xT, k + 1)
                    V.tensor_copy(zsT[0][:, 0:4, :], bank[0][:, 0:4 * CAP].rearrange("p (k t) -> p k t", k=4))
                    V.tensor_copy(zsT[0][:, 4:8, :], bank[1][:, 0:4 * CAP].rearrange("p (k t) -> p k t", k=4)).then_inc(o_zs, 1)
                    dve.wait_ge(o_silu, k + 1)
                    dve.wait_ge(o_gate, k + 1)
                    tt(hid[0].rearrange("p k t -> p (k t)"), silu[0], bank[3][:, 0:4 * CAP], ALU.mult).then_inc(o_hid, 1)
                    dve.wait_ge(o_down, k + 2)
                    dve.wait_ge(y_stored[0], 8 * NE)
                    V.tensor_copy(ysb[0][:, 0:HALF], bank[4][0:CAP, :])
                    V.tensor_copy(ysb[0][:, HALF:D], bank[5][0:CAP, :]).then_inc(o_y, 1)
                dve.nop()
            with dve.Else():
                dve.nop()
            for t in range(NT):
                dve.wait_ge(back[t], 32)
                link(V.scalar_tensor_tensor(out=h[:, t, :], in0=yg1[t % 2], scalar=gw[:, 0, t:t + 1], in1=h[:, t, :], op0=ALU.mult, op1=ALU.add))
                V.scalar_tensor_tensor(out=h[:, t, :], in0=yg2[t % 2], scalar=gw[:, 1, t:t + 1], in1=h[:, t, :], op0=ALU.mult, op1=ALU.add).then_inc(combined, 1)
                dve.wait_ge(o_squared, t + 1)
                rstd(rs_z[:, t:t + 1], ss_o[:, t:t + 1])
                V.scalar_tensor_tensor(out=yg1[t % 2], in0=h[:, t, :], scalar=rs_z[:, t:t + 1], in1=gain_fin, op0=ALU.mult, op1=ALU.mult).then_inc(out_ready, 1)

        @block.tensor
        def _(pe):
            def claim(name, i):
                n = AT[name, i]
                assert ORDER[n][:2] == (name, i) and n == claimed[0]
                claimed[0] += 1
                if n >= BANKS:
                    pe.wait_ge(*drained(*ORDER[n - BANKS][:2]))
                return bank[n % BANKS]

            claimed = [0]

            def mm(o_, l_, r_, first, last):
                return nc.tensor.matmul(o_, lhsT=l_, rhs=r_, start=first, stop=last)

            def tr(o_, i_, p=P):
                return nc.tensor.transpose(o_, i_, ident[0:p, 0:p])

            def rows_to_columns(name, src, t):
                for n in range(2):
                    b = claim(name, 2 * t + n)
                    for k in range(4):
                        ins = tr(b[:, P * k:P * (k + 1)], src[:, t, P * (4 * n + k):P * (4 * n + k + 1)])
                    ins.then_inc(psum_filled, 1)

            def project(name, i, w, m, act_in, nk=KD):
                b = claim(name, i)
                for k in range(nk):
                    ins = mm(b[:, :], w[:, k, P * m:P * (m + 1)], act_in[:, k, :], k == 0, k == nk - 1)
                ins.then_inc(psum_filled, 1)

            def three(o_, l_, r_, at_l, at_r, first, last):
                mm(o_, l_[0][at_l], r_[0][at_r], first, False)
                mm(o_, l_[0][at_l], r_[1][at_r], False, False)
                return mm(o_, l_[1][at_l], r_[0][at_r], False, last)

            def project_split(name, i, w, m, act_in, nk=KD):
                b = claim(name, i)
                for k in range(nk):
                    ins = three(b[:, :], w, act_in, (slice(None), k, slice(P * m, P * (m + 1))), (slice(None), k), k == 0, k == nk - 1)
                ins.then_inc(psum_filled, 1)

            def weights_split(name):
                pe.wait_ge(weight_lo, 2 * SPLIT.index(name) + 2)

            pe.wait_ge(consts_ready, 1)
            for t in range(NT):
                pe.wait_ge(x_normed, t + 1)
                rows_to_columns("xT", h, t)
            pe.wait_ge(*loaded("v"))
            pe.wait_ge(*drained("xT", 7))
            for m in range(2):
                project("v", m, chunk("v", 8), m, uT)
            pe.wait_ge(lam_ready, 1)
            b = claim("lam", 0)
            for n in range(4):
                ins = tr(b[:, SSM_G * n:SSM_G * (n + 1)], lamq[:, n, :, :].rearrange("p x n -> p (x n)"), SSM_G)
            ins.then_inc(psum_filled, 1)
            pe.wait_ge(ssmb_loaded, 64)
            b = claim("cT", 0)
            for n in range(4):
                ins = tr(b[:, P * n:P * (n + 1)], cload[:, n, :])
            ins.then_inc(psum_filled, 1)
            for m in range(2, 4):
                project("v", m, chunk("v", 8), m, uT)
            pe.wait_ge(*loaded("z"))
            for m in range(4):
                project("zp", m, chunk("z", 8), m, uT)
            for t in range(MT):
                pe.wait_ge(mem_normed, t + 1)
                rows_to_columns("memT", mem_tok, t)
            pe.wait_ge(powers_ready, 1)
            for q in range(8):
                b = claim("bT", q)
                for n in range(4):
                    ins = tr(b[:, P * n:P * (n + 1)], bpow_m[:, 4 * q + n, :])
                ins.then_inc(psum_filled, 1)
            for q in range(8):
                b = claim("kern", q)
                for n in range(4):
                    gg = 4 * q + n
                    Bg, o_ = gc(Bb)[:, gg, :], b[0:SSM_C, P * n:P * (n + 1)]
                    mm(o_[:, 0:SSM_C], Bg, gc(Cy)[:, gg, :], True, True)
                    ins = mm(o_[:, SSM_C:P], Bg, cpow_m[:, gg, 0:P - SSM_C], True, True)
                ins.then_inc(psum_filled, 1)
            pe.wait_ge(*drained("v", 3))
            for l in range(LCH):
                b = claim("vl", l)
                for m in range(4):
                    ins = tr(b[0:NCH, P * m:P * (m + 1)], vT[:, m, :].rearrange("p (j l) -> p l j", l=LCH)[:, l, :])
                ins.then_inc(psum_filled, 1)
            pe.wait_ge(*drained("vl", 7))
            for q in range(4):
                b = claim("vch", q)
                for n in range(8):
                    ins = tr(b[:, NCH * n:NCH * (n + 1)], vj_m[:, 8 * q + n, :], NCH)
                ins.then_inc(psum_filled, 1)
            for q in range(4):
                b = claim("st", q)
                pe.wait_ge(*drained("vch", q))
                for n in range(8):
                    ins = mm(b[:, NCH * n:NCH * (n + 1)], bpow_m[:, 8 * q + n, :], vch[:, 8 * q + n, :], True, True)
                ins.then_inc(psum_filled, 1)
            pe.wait_ge(poolw_loaded, 16)
            for g_ in range(POOL_G):
                pe.wait_ge(pool_diff, g_ + 1)
                b = claim("mix", g_)
                mm(b[:, :], poolw[:, g_, :], zp[:, g_, PADT:], True, True).then_inc(psum_filled, 1)
            pe.wait_ge(*drained("memT", 3))
            for m in range(4):
                if m % 2 == 0:
                    pe.wait_ge(*loaded(f"k{m // 2}"))
                w = chunk(f"k{m // 2}", 8)
                b = claim("kk", m)
                for s in range(2):
                    c = 2 * (m % 2) + s
                    for k in range(KD):
                        ins = mm(b[:, MEM * s:MEM * (s + 1)], w[:, k, P * c:P * (c + 1)], memT[:, k, :], k == 0, k == KD - 1)
                ins.then_inc(psum_filled, 1)
            for n in range(4):
                if n % 2 == 0:
                    pe.wait_ge(*loaded(f"v{n // 2}"))
                w = chunk(f"v{n // 2}", 8)
                b = claim("vv", n)
                for k in range(KD):
                    ins = mm(b[:, :], memT[:, k, P * (n % 2):P * (n % 2 + 1)], w[:, k, :], k == 0, k == KD - 1)
                ins.then_inc(psum_filled, 1)
            pe.wait_ge(*loaded("toep"))
            pe.wait_ge(states_ready, 1)
            toep = ring[CH["toep"] % RAW][:, :].rearrange("p (g x) -> p g x", g=SSM_G)
            for q in range(8):
                b = claim("y", q)
                for n in range(4):
                    gg = 4 * q + n
                    mm(b[0:NCH, P * n:P * (n + 1)], vch[:, gg, :], toep[:, gg, :], True, False)
                    ins = mm(b[0:NCH, P * n:P * (n + 1)], hin[:, gg, 1, :], cpow_m[:, gg, :], False, True)
                ins.then_inc(psum_filled, 1)

            def gates(lo, hi):
                for m in range(lo, hi):
                    if m % 4 == 0:
                        weights_split(f"g{m // 4}")
                    project_split("gate", m, parts(f"g{m // 4}", 8), m % 4, (u_hi, u_lo))

            pe.wait_ge(u_split, KD)
            gates(0, 4)
            pe.wait_ge(*drained("y", 7))
            for m in range(4):
                b = claim("yT", m)
                for l in range(LCH):
                    ins = tr(b[:, NCH * l:NCH * (l + 1)], yj[:, m, l, :], NCH)
                ins.then_inc(psum_filled, 1)
            gates(4, 8)
            pe.wait_ge(*loaded("glu"))
            pe.wait_ge(gelu_ready, 4)
            for m in range(4):
                project("glu", m, chunk("glu", 4), m, ygT, 4)
            gates(8, 16)
            weights_split("bp")
            pe.wait_ge(yp_split, 4)
            for m in range(KD):
                project_split("bp", m, parts("bp", 4), m, (yp_hi, yp_lo), 4)
            weights_split("bs")
            pe.wait_ge(ys_split, 4)
            for m in range(KD):
                project_split("bs", m, parts("bs", 4), m, (ys_hi, ys_lo), 4)
            pe.wait_ge(merged_ready, KD)

            def by_rows(name, t, src, w):
                for n in range(2):
                    if t == 0:
                        weights_split(w[n])
                    b = claim(name, 2 * t + n)
                    for k in range(KD):
                        ins = three(b[:, :], src, parts(w[n], 8), (slice(None), k, slice(P * t, P * (t + 1))), (slice(None), k), k == 0, k == KD - 1)
                    ins.then_inc(psum_filled, 1)

            for t in range(NT):
                by_rows("wo1", t, (mg_hi, mg_lo), ("o0", "o1"))
                if t >= 1:
                    pe.wait_ge(h_normed, t)
                    rows_to_columns("hT", xn, t - 1)
            pe.wait_ge(h_normed, NT)
            rows_to_columns("hT", xn, NT - 1)
            pe.wait_ge(hn_split, 2 * NT)
            for m in range(8):
                if m % 4 == 0:
                    weights_split(f"q{m // 4}")
                project_split("q", m, parts(f"q{m // 4}", 8), m % 4, (hn_hi, hn_lo))
            pe.wait_ge(*drained("vv", 3))
            for hd in range(HEADS + 1):
                if hd < HEADS:
                    pe.wait_ge(*drained("q", 2 * hd + 1))
                    for n in range(2):
                        b = claim("sc", 2 * hd + n)
                        for s in range(2):
                            t = 2 * n + s
                            for k in range(2):
                                ins = mm(b[:, MEM * s:MEM * (s + 1)], qT[:, 2 * hd + k, P * t:P * (t + 1)], kT[:, 2 * hd + k, :], k == 0, k == 1)
                        ins.then_inc(psum_filled, 1)
                if hd >= 1:
                    o_ = hd - 1
                    pe.wait_ge(prob_ready, 2 * o_ + 2)
                    for n in range(2):
                        b = claim("pT", 2 * o_ + n)
                        for t in range(NT):
                            ins = tr(b[:, P * t:P * (t + 1)], prob[:, o_ % 2, t, P * n:P * (n + 1)])
                        ins.then_inc(psum_filled, 1)
                    pe.wait_ge(*drained("pT", 2 * o_ + 1))
                    for n in range(2):
                        b = claim("pv", 2 * o_ + n)
                        for k in range(MT):
                            ins = mm(b[:, :], vm[:, k, HD * o_ + P * n:HD * o_ + P * (n + 1)], probT[:, o_ % 2, k, :], k == 0, k == MT - 1)
                        ins.then_inc(psum_filled, 1)
            pe.wait_ge(o_split, KD)
            pe.wait_ge(router_loaded, 32)

            def route(t):
                b = claim("route", t)
                pe.wait_ge(*drained("zT", 2 * t + 1))
                for k in range(KD):
                    ins = mm(b[:, 0:20], zT[:, k, P * t:P * (t + 1)], rw[:, k, :], k == 0, k == KD - 1)
                ins.then_inc(psum_filled, 1)

            for t in range(NT):
                by_rows("wo2", t, (o_hi, o_lo), ("w0", "w1"))
                if t >= 2:
                    route(t - 2)
                if t >= 1:
                    pe.wait_ge(z_normed, t)
                    rows_to_columns("zT", xn, t - 1)
            route(NT - 2)
            pe.wait_ge(z_normed, NT)
            rows_to_columns("zT", xn, NT - 1)
            route(NT - 1)
            pe.wait_ge(mask_ready, 1)
            pe.wait_ge(masks_ready, 1)
            b = claim("rank", 0)
            mm(b[:, 0:64], before[:, :], e64[3].rearrange("p t n -> p (t n)"), True, False)
            mm(b[:, 0:64], ones[:, :], m_cum[:, 0:64], False, True)
            mm(b[:, 64:80], ones[:, :], m_cum[:, 64:80], True, True).then_inc(psum_filled, 1)
            pe.wait_ge(*drained("rank", 0))

            def transposes(e, a, n_g):
                pe.wait_ge(gathered[a], n_g)
                pe.wait_ge(zs_ready, e + 1)
                for k in range(KD):
                    ins = tr(bank[k // 4][:, CAP * (k % 4):CAP * (k % 4 + 1)], xg[a][:, P * k:P * (k + 1)], CAP)
                ins.then_inc(xg_used, 1)

            def up(a, s, b_, n_w, done):
                pe.wait_ge(slot_loaded[s], n_w)
                w = expert_chunk(s, 8)
                for m in range(4):
                    for k in range(KD):
                        ins = mm(b_[:, CAP * m:CAP * (m + 1)], w[:, k, P * m:P * (m + 1)], zsT[a][:, k, :], k == 0, k == KD - 1)
                ins.then_inc(done, 1)

            def expert(e, a, i, n_next):
                s0, s1, s2 = (expert_slot(a, c) for c in range(3))
                pe.wait_ge(zs_ready, e + 2)
                pe.wait_ge(silu_ready, e + 1)
                up(a, s0, bank[2 + 4 * a], front_loads[s0] + 16 * i + 16, up_done)
                pe.wait_ge(hid_ready, e + 1)
                up(a, s1, bank[3 + 4 * a], front_loads[s1] + 16 * i + 16, gate_done)
                if n_next is not None:
                    transposes(e + 1, 1 - a, n_next)
                pe.wait_ge(slot_loaded[s2], front_loads[s2] + 16 * i + 16)
                pe.wait_ge(hid_ready, e + 3)
                w = expert_chunk(s2, 4)
                for n, drained_by in ((0, y_dve), (1, y_act)):
                    pe.wait_ge(drained_by, e + 1)
                    for k in range(4):
                        ins = mm(bank[4 + n][0:CAP, :], hid[a][:, k, :], w[:, k, HALF * n:HALF * (n + 1)], k == 0, k == 3)
                    ins.then_inc(down_done, 1)

            transposes(0, 0, 16)
            with pe.Fori(0, NE // 2 - 1) as i:
                expert(2 * i, 0, i, 16 * i + 16)
                expert(2 * i + 1, 1, i, 16 * i + 32)
            last = NE // 2 - 1
            expert(NE - 2, 0, last, 16 * last + 16)
            expert(NE - 1, 1, last, None)
            pe.sem_inc(o_down, 1)
            pe.wait_ge(y_dve, NE + 1)
            pe.wait_ge(y_act, NE + 1)
            pe.wait_ge(tiles_ready, 1)
            n_over = pe.value_load(tile_i[0:1, N_OVER:N_OVER + 1], min_val=0, max_val=N_OVER)
            with pe.If(n_over > 0):
                with pe.Fori(0, n_over) as k:
                    pe.wait_ge(o_gath, 16 * k + 16)
                    for kk in range(KD):
                        ins = tr(bank[kk // 4][:, CAP * (kk % 4):CAP * (kk % 4 + 1)], xg[0][:, P * kk:P * (kk + 1)], CAP)
                    ins.then_inc(o_xT, 1)
                    pe.wait_ge(o_zs, k + 1)
                    pe.wait_ge(o_w, 48 * k + 48)
                    for c, done in ((0, o_up), (1, o_gate)):
                        w = expert_chunk(c, 8)
                        for m in range(4):
                            for kk in range(KD):
                                ins = mm(bank[2 + c][:, CAP * m:CAP * (m + 1)], w[:, kk, P * m:P * (m + 1)], zsT[0][:, kk, :], kk == 0, kk == KD - 1)
                        ins.then_inc(done, 1)
                    pe.wait_ge(o_hid, k + 1)
                    w = expert_chunk(2, 4)
                    for n in range(2):
                        for kk in range(4):
                            ins = mm(bank[4 + n][0:CAP, :], hid[0][:, kk, :], w[:, kk, HALF * n:HALF * (n + 1)], kk == 0, kk == 3)
                    ins.then_inc(o_down, 1)
                    pe.wait_ge(o_y, k + 1)
                pe.nop()
            with pe.Else():
                pe.nop()


_INS = ['x', 'mem', 'norm_mix', 'w_in', 'pool_w', 'pool_scale', 'ssm_a_re', 'ssm_a_im', 'ssm_log_dt', 'ssm_b_re', 'ssm_b_im', 'ssm_c_re', 'ssm_c_im', 'ssm_d', 'glu_w', 'glu_b', 'br_pool', 'br_ssm', 'w_out', 'norm_x', 'norm_mem', 'x_wq', 'x_wkv', 'x_wo', 'norm_ffn', 'router_g_w', 'router_g_b', 'router_e_w', 'router_e_b', 'exp_w1', 'exp_w3', 'exp_w2', 'norm_final']
_OUTS = [((1, SEQ, D), 'float32')]


def kernel(**inputs):
    import numpy as _np
    import concourse.bacc as _bacc
    from concourse import mybir as _mybir
    from concourse.bass_utils import run_bass_kernel_spmd as _run

    nc = _bacc.Bacc("TRN2", target_bir_lowering=False, num_devices=1)
    arrays, args = {}, []
    for name in _INS:
        a = _np.ascontiguousarray(inputs[name])
        arrays[f"in_{name}_dram"] = a
        args.append(nc.dram_tensor(f"in_{name}_dram", a.shape, _mybir.dt.from_np(a.dtype), kind="ExternalInput").ap())
    for i, (shape, dtype) in enumerate(_OUTS):
        dt = _mybir.dt.from_np(_np.dtype(dtype))
        args.append(nc.dram_tensor(f"out_{i}_dram", shape, dt, kind="ExternalOutput").ap())
    bass_hybrid_decoder_layer(nc, *args)
    r = _run(nc, [arrays], core_ids=[0])
    return r.results[0]["out_0_dram"]
```

```python
import math
from contextlib import ExitStack

import concourse.bass as bass
from concourse import mybir
from concourse.alu_op_type import AluOpType as ALU

P = 128
SEQ, D, MEM = 512, 1024, 256
NT, KD, MT = SEQ // P, D // P, MEM // P
HALF = 512
POOL_G, SSM_G, SSM_C, SSM_N = 4, 32, 16, 64
LCH = 8
NCH = SEQ // LCH
SUP = 8
HEADS, HD = 4, 256
NE, F = 16, 512
CAP = 96
N_OVER = (2 * SEQ) // CAP
N_TILES = NE + N_OVER
SLOTS = N_TILES * CAP
RING = 6
RAW = 3
PADT = 16
EPS = 1e-6
BANKS = 8


def bass_hybrid_decoder_layer(nc: bass.Bass, x, mem, norm_mix, w_in, pool_w, pool_scale, ssm_a_re, ssm_a_im,
                              ssm_log_dt, ssm_b_re, ssm_b_im, ssm_c_re, ssm_c_im, ssm_d, glu_w, glu_b,
                              br_pool, br_ssm, w_out, norm_x, norm_mem, x_wq, x_wkv, x_wo, norm_ffn,
                              router_g_w, router_g_b, router_e_w, router_e_b, exp_w1, exp_w3, exp_w2,
                              norm_final, out):
    f32, i32 = mybir.dt.float32, mybir.dt.int32
    ACT, AX = mybir.ActivationFunctionType, mybir.AxisListType

    ctx = ExitStack()
    with ctx:
        places = {}

        def sb(name, shape, dt=f32):
            places[name] = -(-nc.sbuf_base // 32) * 32
            return ctx.enter_context(nc.sbuf_tensor(name, shape, dt))

        def sem(name):
            return ctx.enter_context(nc.semaphore(name))

        ring = [sb(f"slot{i}", [P, 4096]) for i in range(RING)]
        hreg = sb("hreg", [P, 4096])
        ureg = sb("ureg", [P, 4096])
        greg = sb("greg", [P, 8192])
        kvreg = sb("kvreg", [P, 4096])
        areg = sb("areg", [P, 2048 + POOL_G * (PADT + SEQ)])
        zeros = areg[:, 0:4 * 7 * SSM_C]
        memreg = sb("memreg", [P, 2048])
        ident = sb("ident", [P, P])
        before = sb("before", [P, P])
        ones = sb("ones", [P, P])
        poolw = sb("poolw", [P, POOL_G, P])
        lam8 = sb("lam8", [P, 8, 2, SSM_G])
        cols = sb("cols", [P, 4 * KD + 4 * 3])
        cntinv = sb("cntinv", [P, POOL_G, PADT])
        rstat = sb("rstat", [P, 32])
        newton = sb("newton", [P, 8])
        soft = sb("soft", [P, 4, 4 * HEADS])

        f32r = mybir.dt.float32r

        def rounded(name, shape):
            return nc.alloc_sbuf_tensor_at(name + "_r", shape, f32r, offset=places[name])

        ring_r = [rounded(f"slot{i}", [P, 4096]) for i in range(RING)]
        hreg_r = rounded("hreg", [P, 4096])
        ureg_r = rounded("ureg", [P, 4096])
        greg_r = rounded("greg", [P, 8192])
        memreg_r = rounded("memreg", [P, 2048])
        areg_r = rounded("areg", [P, 2048 + POOL_G * (PADT + SEQ)])

        gain_mix, gain_x, gain_mem = (cols[:, KD * i:KD * (i + 1)] for i in range(3))
        gain_ffn_c = cols[:, 3 * KD + 12:4 * KD + 12]
        pscale, dskip, glub = (cols[:, 3 * KD + 4 * i:3 * KD + 4 * (i + 1)] for i in range(3))
        rmax, nmax, esum, rsum = (soft[:, i, :] for i in range(4))
        ss_x, rs_x = rstat[:, 0:4], rstat[:, 4:8]
        ss_m, rs_m = rstat[:, 8:10], rstat[:, 10:12]
        ss_h, rs_h = rstat[:, 12:16], rstat[:, 16:20]
        ss_z, rs_z = rstat[:, 20:24], rstat[:, 24:28]
        ss_o = rstat[:, 28:32]
        qscale = sb("qscale", [P, 2, NT])

        h = hreg[:, :].rearrange("p (t d) -> p t d", t=NT)
        cpow = hreg[:, :].rearrange("p (g k c) -> p g k c", g=SSM_G, k=LCH)
        cpow_m = hreg[:, :].rearrange("p (g m) -> p g m", g=SSM_G)
        msq = areg[:, 2048:4096].rearrange("p (t d) -> p t d", t=MT)
        yj = hreg[0:NCH, :].rearrange("p (m l c) -> p m l c", m=4, l=LCH)
        yj_g = hreg[0:NCH, :].rearrange("p (m l g c) -> p m g l c", m=4, l=LCH, c=SSM_C)
        uT = ureg[:, :].rearrange("p (k t) -> p k t", k=KD)
        qT, zT = uT, uT
        by_k = lambda a: a.rearrange("p (k t) -> p k t", t=SEQ)
        u_hi, u_lo = by_k(ring_r[5][:, :]), by_k(ureg_r[:, :])
        mg_hi, mg_lo = by_k(ureg_r[:, :]), by_k(ring_r[5][:, :])
        G_lo, G_hi = greg[:, 0:4096], greg[:, 4096:8192]
        bpow = G_lo.rearrange("p (g m c) -> p g m c", g=SSM_G, m=LCH)
        bpow_m = G_lo.rearrange("p (g m) -> p g m", g=SSM_G)
        W = G_lo.rearrange("p (g x s j) -> p g x s j", g=SSM_G, x=2, s=SUP)
        hin = G_lo.rearrange("p (g x q) -> p g x q", g=SSM_G, x=2)
        lamg = [greg[0:SSM_G, 64 * i:64 * (i + 1)] for i in range(24)]
        lamq = greg[0:SSM_G, 1536:2048].rearrange("p (q x n) -> p q x n", q=4, x=2)
        cload = greg[:, 2048:2560].rearrange("p (t n) -> p t n", t=4)
        gtmp = greg[:, 4096:6144]
        gtmp_k = gtmp.rearrange("p (g k c) -> p g k c", g=SSM_G, k=4)
        mem_tok = greg[:, 6144:8192].rearrange("p (t d) -> p t d", t=MT)
        kern_sb = greg[0:SSM_C, 4096:8192].rearrange("p (g x) -> p g x", g=SSM_G)
        vch = greg[:, 4096:6144].rearrange("p (g q) -> p g q", g=SSM_G)
        stmp = greg[:, 6144:8192]
        gT = greg[:, :].rearrange("p (k t) -> p k t", k=16)
        hnT, hn_hi, hn_lo = by_k(areg[:, 64:4160]), by_k(greg_r[:, 0:4096]), by_k(areg_r[:, 64:4160])
        oT, o_hi, o_lo = by_k(ring[5][:, :]), by_k(greg_r[:, 0:4096]), by_k(ring_r[5][:, :])
        xn = G_hi.rearrange("p (t d) -> p t d", t=NT)
        prob = G_hi[:, 0:2048].rearrange("p (b t m) -> p b t m", b=2, t=NT)
        probT = G_hi[:, 2048:4096].rearrange("p (b m t) -> p b m t", b=2, m=MT)
        B_s, B_w = kvreg[:, 0:512], kvreg[:, 512:1024]
        ptmp = kvreg[:, 0:2 * (PADT + SEQ)].rearrange("p (b t) -> p b t", b=2)
        o = 1088
        Bb, Bbw, Cy, Cw = (kvreg[:, o + 512 * i:o + 512 * (i + 1)] for i in range(4))
        pw = kvreg[:, o + 2048:o + 2560].rearrange("p (k x g) -> p k x g", k=LCH, x=2)
        lamL = kvreg[:, o + 2560:o + 2688].rearrange("p (q g) -> p q g", q=4)
        gc = lambda a: a.rearrange("p (g c) -> p g c", g=SSM_G)
        vj = kvreg[0:NCH, :].rearrange("p (g m c) -> p g m c", g=SSM_G, m=LCH)
        vj_m = kvreg[0:NCH, :].rearrange("p (g m) -> p g m", g=SSM_G)
        kT = kvreg[:, 0:2048].rearrange("p (k m) -> p k m", k=KD)
        vm = kvreg[:, 2048:4096].rearrange("p (t d) -> p t d", t=MT)
        vT = areg[:, 0:2048].rearrange("p (k t) -> p k t", k=4)
        zp = areg[:, 2048:].rearrange("p (k t) -> p k t", k=POOL_G)
        ypT, ysT = zp[:, :, PADT:], vT
        yp_hi, ys_hi = by_k(hreg_r[:, 0:2048]), by_k(hreg_r[:, 2048:4096])
        yp_lo, ys_lo = areg_r[:, 2048:].rearrange("p (k t) -> p k t", k=POOL_G)[:, :, PADT:], by_k(areg_r[:, 0:2048])
        memT, mem_hi, mem_lo = (r.rearrange("p (k t) -> p k t", k=KD) for r in (memreg[:, :], ring_r[5][:, 0:2048], memreg_r[:, :]))
        ygT = memreg[:, :].rearrange("p (k t) -> p k t", k=4)
        gain_ffn, gain_fin = memreg[:, 0:D], memreg[:, D:2 * D]

        rw = poolw[:, :, :].rearrange("p g d -> p (g d)")[:, 0:KD * 20].rearrange("p (k n) -> p k n", k=KD)
        rb = areg[:, 0:20]
        AR = areg
        def ar(at, n):
            return AR[:, at:at + n]
        logits = ar(32, 80).rearrange("p (t n) -> p t n", t=NT)
        lg, le = logits[:, :, 0:4], logits[:, :, 4:20]
        desc = ar(112, 4)
        r4 = [ar(120 + 4 * i, 4) for i in range(16)]
        q4 = [ar(200 + 16 * i, 16).rearrange("p (t n) -> p t n", t=NT) for i in range(10)]
        e64 = [ar(400 + 64 * i, 64).rearrange("p (t n) -> p t n", t=NT) for i in range(8)]
        x64 = ar(912, 64).rearrange("p (t n) -> p t n", t=NT)
        n16 = [ar(1000 + 16 * i, 16) for i in range(14)]
        m_cum = ar(1312, 80)
        o_k = ar(3100, N_OVER * NE).rearrange("p (k n) -> p k n", k=N_OVER)
        o_lt = ar(3500, N_OVER * NE).rearrange("p (k n) -> p k n", k=N_OVER)
        pre = [ar(1800 + 32 * i, 32) for i in range(5)]
        tile_row = ar(1290, N_OVER + 1)
        rank_f = ar(1980, 8).rearrange("p (s t) -> p s t", s=2)
        place = ar(2000, CAP)
        tok_f = ar(2100, NT)
        at_rank = ar(2112, 8 * CAP).rearrange("p (s t c) -> p s t c", s=2, t=NT)
        tok_of = ar(2112 + 8 * CAP, 128).rearrange("p (s t n) -> p s t n", s=2, t=NT)
        slot_f = ar(1260, 8).rearrange("p (s t) -> p s t", s=2)
        base_id = ar(1270, 16)
        tok_id = sb("tok_id", [P, NT], i32)
        place_i = sb("place_i", [P, CAP], i32)
        idx_first = sb("idx_first", [CAP, NE], i32)
        slot_i = sb("slot_i", [P, 2, NT], i32)
        tile_i = sb("tile_i", [P, N_OVER + 1], i32)
        idx_all = sb("idx_all", [CAP, N_TILES], i32)
        idx_one = sb("idx_one", [CAP, 1], i32)
        gw = sb("gw", [P, 2, NT])
        o = 0
        xg = [greg[0:CAP, D * a:D * (a + 1)] for a in range(2)]
        zsT = [greg[:, 2048 + 768 * a:2048 + 768 * a + KD * CAP].rearrange("p (k t) -> p k t", k=KD) for a in range(2)]
        silu = [greg[:, 3584 + 384 * a:3584 + 384 * a + 4 * CAP] for a in range(2)]
        hid = [greg[:, 4352 + 384 * a:4352 + 384 * a + 4 * CAP].rearrange("p (k t) -> p k t", k=4) for a in range(2)]
        hid_hi, hid_lo = ([greg_r[:, at_ + 384 * a:at_ + 384 * a + 4 * CAP].rearrange("p (k t) -> p k t", k=4) for a in range(2)]
                          for at_ in (7168, 4352))
        ysb = [greg[0:CAP, 5120 + D * a:5120 + D * (a + 1)] for a in range(2)]
        yg1, yg2 = ([r[:, 2048 * a + c * D:2048 * a + (c + 1) * D] for r in (kvreg, greg) for a in range(2)] for c in range(2))

        bank = [ctx.enter_context(nc.psum_tensor(f"bank{i}", [P, HALF], f32)) for i in range(BANKS)]

        kern_d = nc.dram_tensor("kern_d", [SSM_G, SSM_C, 15 * SSM_C], f32, kind="Internal").ap()
        z_d = nc.dram_tensor("z_d", [SEQ, D], f32, kind="Internal").ap()
        inv_d = nc.dram_tensor("inv_d", [SLOTS, 1], i32, kind="Internal").ap()
        y_d = nc.dram_tensor("y_d", [SLOTS, D], f32, kind="Internal").ap()

        x_loaded = [sem(f"x_loaded{t}") for t in range(NT)]
        mem_loaded, cols_loaded, ssm_loaded = sem("mem_loaded"), sem("cols_loaded"), sem("ssm_loaded")
        ssmb_loaded, poolw_loaded = sem("ssmb_loaded"), sem("poolw_loaded")
        slot_loaded = [sem(f"slot_loaded{s}") for s in range(RING)]
        toep_loaded, kern_stored, zero_stored = sem("toep_loaded"), sem("kern_stored"), sem("zero_stored")
        consts_ready, masks_ready, tok_ready, counts_ready, index_ready = (sem(n) for n in ("consts_ready", "masks_ready", "tok_ready", "counts_ready", "index_ready"))
        psum_filled, act_drained, dve_drained = sem("psum_filled"), sem("act_drained"), sem("dve_drained")
        dve_step, act_step, pool_step = sem("dve_step"), sem("act_step"), sem("pool_step")
        x_squared, mem_squared, x_normed, mem_normed = sem("x_squared"), sem("mem_squared"), sem("x_normed"), sem("mem_normed")
        decay_ready, lam_ready, sines_ready = sem("decay_ready"), sem("lam_ready"), sem("sines_ready")
        x_rstd, mem_rstd, o_rstd = sem("x_rstd"), sem("mem_rstd"), sem("o_rstd")
        angle_ready, powers_ready = sem("angle_ready"), sem("powers_ready")
        pool_diff, states_ready = sem("pool_diff"), sem("states_ready")
        weight_hi, kv_lo, weight_lo = sem("weight_hi"), sem("kv_lo"), sem("weight_lo")
        u_rounded, u_split, yp_rounded, yp_split, ys_rounded, ys_split = (sem(n) for n in ("u_rounded", "u_split", "yp_rounded", "yp_split", "ys_rounded", "ys_split"))
        mem_rounded, mem_split = sem("mem_rounded"), sem("mem_split")
        mg_exact, mg_rounded, hn_rounded, hn_split, o_rounded, o_split = (sem(n) for n in ("mg_exact", "mg_rounded", "hn_rounded", "hn_split", "o_rounded", "o_split"))
        gain_loaded = sem("gain_loaded")
        gelu_ready, ys_ready, merged_ready = sem("gelu_ready"), sem("ys_ready"), sem("merged_ready")
        h_loaded, h_squared, router_scaled = sem("h_loaded"), sem("h_squared"), sem("router_scaled")
        neg_max, exp_done, prob_ready = sem("neg_max"), sem("exp_done"), sem("prob_ready")
        gains_loaded, z_squared, z_normed, z_stored = sem("gains_loaded"), sem("z_squared"), sem("z_normed"), sem("z_stored")
        router_loaded, g_shift, g_exp, e_shift, e_exp = sem("router_loaded"), sem("g_shift"), sem("g_exp"), sem("e_shift"), sem("e_exp")
        mask_ready, slots_ready, tiles_ready, inv_zeroed, inv_stored, inv_loaded = sem("mask_ready"), sem("slots_ready"), sem("tiles_ready"), sem("inv_zeroed"), sem("inv_stored"), sem("inv_loaded")
        at_rank_ready, first_ready = sem("at_rank_ready"), sem("first_ready")
        idx_ready, pool_tick, rows_filled = sem("idx_ready"), sem("pool_tick"), sem("rows_filled")
        gathered = [sem(f"gathered{a}") for a in range(2)]
        xg_used, zs_ready, up_done, gate_done = sem("xg_used"), sem("zs_ready"), sem("up_done"), sem("gate_done")
        w2_hi, w2_lo, hid_exact, hid_rounded = (sem(n) for n in ("w2_hi", "w2_lo", "hid_exact", "hid_rounded"))
        silu_ready, hid_ready, down_done = sem("silu_ready"), sem("hid_ready"), sem("down_done")
        y_dve, y_act = sem("y_dve"), sem("y_act")
        y_stored = [sem(f"y_stored{a}") for a in range(2)]
        o_idx, o_gath, o_w, o_xT, o_zs, o_up, o_gate = (sem(n) for n in ("o_idx", "o_gath", "o_w", "o_xT", "o_zs", "o_up", "o_gate"))
        o_silu, o_hid, o_down, o_y, o_stored, all_stored = (sem(n) for n in ("o_silu", "o_hid", "o_down", "o_y", "o_stored", "all_stored"))
        back = [sem(f"back{t}") for t in range(NT)]
        combined, o_squared, out_ready = sem("combined"), sem("o_squared"), sem("out_ready")
        out_stored = [sem(f"out_stored{t}") for t in range(NT)]

        ORDER = []

        def jobs(name, n, engine):
            ORDER.extend((name, i, engine) for i in range(n))

        jobs("xT", 8, "dve")
        ORDER.extend(("v", i, "act") for i in range(2))
        jobs("lam", 1, "dve")
        jobs("cT", 1, "act")
        ORDER.extend(("v", i, "act") for i in range(2, 4))
        jobs("zp", 4, "act")
        jobs("memT", 4, "dve")
        jobs("bT", 8, "act")
        jobs("kern", 8, "act")
        jobs("vl", 8, "act")
        jobs("vch", 4, "act")
        jobs("st", 4, "act")
        jobs("mix", 4, "act")
        jobs("kk", 4, "act")
        jobs("vv", 4, "act")
        jobs("y", 8, "dve")
        ORDER.extend(("gate", i, "act") for i in range(4))
        jobs("yT", 4, "dve")
        ORDER.extend(("gate", i, "act") for i in range(4, 8))
        jobs("glu", 4, "act")
        ORDER.extend(("gate", i, "act") for i in range(8, 16))
        jobs("bp", 8, "dve")
        jobs("bs", 8, "dve")
        ROWS = [((0, 1), None), ((2, 3), 0), ((4, 6), 1), ((5,), None), ((7,), 2), ((), 3)]
        for banks_, t in ROWS:
            ORDER.extend(("wo1", i, "dve") for i in banks_)
            if t is not None:
                ORDER.extend(("hT", 2 * t + n, "dve") for n in range(2))
        Q_AHEAD = [(0, 1, 2), (3, 4), (5, 6), (7,)]
        for hd in range(HEADS + 1):
            if hd < HEADS:
                ORDER.extend(("q", m, "act") for m in Q_AHEAD[hd])
            if hd >= 1:
                ORDER.extend(("pT", 2 * (hd - 1) + n, "act") for n in range(2))
            if hd < HEADS:
                ORDER.extend(("sc", 2 * hd + n, "act") for n in range(2))
            if hd >= 1:
                ORDER.extend(("pv", 2 * (hd - 1) + n, "dve") for n in range(2))
        WO2 = [(0, 2, 1), (3,), (4, 5), (6, 7)]
        for t in range(NT):
            ORDER.extend(("wo2", i, "dve") for i in WO2[t])
            if t >= 2:
                ORDER.append(("route", t - 2, "dve"))
            if t >= 1:
                ORDER.extend(("zT", 2 * (t - 1) + n, "act") for n in range(2))
        ORDER.append(("route", NT - 2, "dve"))
        ORDER.extend(("zT", 6 + n, "act") for n in range(2))
        ORDER.append(("route", NT - 1, "dve"))
        jobs("rank", 1, "dve")
        jobs("index", 1, "dve")
        AT = {(n, i): k for k, (n, i, _) in enumerate(ORDER)}
        counts, at = {"act": 0, "dve": 0}, []
        for _, _, e in ORDER:
            counts[e] += 1
            at.append((e, counts[e]))

        def filled(name, i):
            return AT[name, i] + 1

        def drained(name, i):
            e, n = at[AT[name, i]]
            return (act_drained if e == "act" else dve_drained), n

        def bank_of(name, i):
            return bank[AT[name, i] % BANKS]

        wcol = lambda w, c: w[0, :, HALF * c:HALF * (c + 1)].rearrange("(k p) n -> p k n", p=P)
        FRONT = [("v", wcol(w_in, 1), ("v", 3)), ("z", wcol(w_in, 0), ("zp", 3)),
                 ("k0", wcol(x_wkv, 0), ("kk", 1)), ("k1", wcol(x_wkv, 1), ("kk", 3)),
                 ("v0", wcol(x_wkv, 2), ("vv", 1)), ("v1", wcol(x_wkv, 3), ("vv", 3)),
                 ("toep", None, ("y", 7)), ("g0", wcol(w_in, 2), ("gate", 3)), ("g1", wcol(w_in, 3), ("gate", 7)),
                 ("glu", glu_w[0].rearrange("(k p) n -> p k n", p=P), ("glu", 3)),
                 ("g2", wcol(w_in, 4), ("gate", 11)), ("g3", wcol(w_in, 5), ("gate", 15)),
                 ("bp", br_pool[0].rearrange("(k p) n -> p k n", p=P), ("bp", 7)),
                 ("bs", br_ssm[0].rearrange("(k p) n -> p k n", p=P), ("bs", 7)),
                 ("o0", wcol(w_out, 0), ("wo1", 6)), ("o1", wcol(w_out, 1), ("wo1", 7)),
                 ("q0", wcol(x_wq, 0), ("q", 3)), ("q1", wcol(x_wq, 1), ("q", 7)),
                 ("w0", wcol(x_wo, 0), ("wo2", 6)), ("w1", wcol(x_wo, 1), ("wo2", 7))]
        NF = len(FRONT)
        CH = {n: i for i, (n, _, _) in enumerate(FRONT)}
        front_loads = [16 * sum(1 for i in range(NF) if i % RAW == s and FRONT[i][0] != "toep") for s in range(RING)]

        def loaded(name):
            c = CH[name]
            if name == "toep":
                return toep_loaded, 16 * LCH
            return slot_loaded[c % RAW], 16 * sum(1 for i in range(c % RAW, c + 1, RAW) if FRONT[i][0] != "toep")

        def chunk(name, k, of=ring):
            return of[CH[name] % RAW][:, 0:(k * D if k == 4 and name != "glu" else k * HALF)].rearrange("p (k n) -> p k n", k=k)

        SPLIT = ["k0", "k1", "v0", "v1", "g0", "g1", "g2", "g3", "bp", "bs", "o0", "o1", "q0", "q1", "w0", "w1"]

        def hi_slot(name):
            return RAW + SPLIT.index(name) % 2

        def parts(name, k):
            return ring_r[hi_slot(name)][:, :].rearrange("p (k n) -> p k n", k=k), chunk(name, k, ring_r)

        def expert_slot(e, c):
            return 3 * e + c

        def expert_chunk(slot, k):
            return ring[slot][:, :].rearrange("p (k n) -> p k n", k=k)

        w13 = (exp_w1[0].rearrange("e (k p) f -> e p k f", p=P), exp_w3[0].rearrange("e (k p) f -> e p k f", p=P))
        w2v = exp_w2[0].rearrange("e (k p) n -> e p k n", p=P)
        block = ctx.enter_context(nc.Block())

        @block.sync
        def _(sp):
            for t in range(NT):
                sp.dma_start(h[:, t, :], x[0, P * t:P * (t + 1), :]).then_inc(x_loaded[t], 16)
            for c, (name, src, _) in enumerate(FRONT):
                if name == "k0":
                    sp.wait_ge(cols_loaded, 96)
                    sp.wait_ge(ssmb_loaded, 64)
                if name == "z":
                    sp.dma_start(mem_tok, mem[0].rearrange("(t p) d -> p t d", p=P)).then_inc(mem_loaded, 16)
                if c >= RAW:
                    sp.wait_ge(psum_filled, filled(*FRONT[c - RAW][2]))
                if name == "toep":
                    sp.wait_ge(kern_stored, 16)
                    sp.wait_ge(zero_stored, 16)
                    dst = ring[c % RAW][:, :].rearrange("p (g x) -> p g x", g=SSM_G)
                    for m in range(LCH):
                        sp.dma_start(dst[SSM_C * m:SSM_C * (m + 1), :, :],
                                     kern_d[:, :, SSM_C * m:SSM_C * m + P].rearrange("g c x -> c g x")).then_inc(toep_loaded, 16)
                    continue
                if name == "glu":
                    for lo in range(0, N_OVER * CAP, SEQ):
                        n = min(SEQ, N_OVER * CAP - lo)
                        sp.dma_start(y_d[NE * CAP + lo:NE * CAP + lo + n, :], x[0, 0:n, :]).then_inc(rows_filled, 16)
                k = src.shape[1]
                dst = ring[c % RAW][:, 0:k * src.shape[2]].rearrange("p (k n) -> p k n", k=k)
                sp.dma_start(dst, src).then_inc(slot_loaded[c % RAW], 16)

            def load_expert(e, a, used, order=(0, 1, 2)):
                for c in order:
                    if used:
                        sp.wait_ge(*used[c])
                    s = expert_slot(a, c)
                    src = (w13[c] if c < 2 else w2v)[bass.ds(e, 1)].rearrange("e p k n -> p (e k) n")
                    sp.dma_start(expert_chunk(s, 8 if c < 2 else 4), src).then_inc(slot_loaded[s], 16)

            load_expert(0, 0, [(psum_filled, filled(*job)) for job in (("wo2", 6), ("wo2", 7), ("q", 7))], (2, 0, 1))
            load_expert(1, 1, [(psum_filled, filled("wo2", 7))] * 3)
            with sp.Fori(1, NE // 2) as i:
                for a in range(2):
                    load_expert(2 * i + a, a, [(up_done, 2 * i + a - 1), (gate_done, 4 * i + 2 * a - 2),
                                               (down_done, 4 * i + 2 * a - 2)])
            sp.wait_ge(tiles_ready, 1)
            n_over = sp.value_load(tile_i[0:1, N_OVER:N_OVER + 1], min_val=0, max_val=N_OVER)
            with sp.If(n_over > 0):
                with sp.Fori(0, n_over) as k:
                    ex = sp.value_load(tile_i[0:1, bass.ds(k, 1)], min_val=0, max_val=NE - 1)
                    sp.wait_ge(down_done, 2 * NE)
                    sp.wait_ge(o_down, k + 1)
                    for c in range(3):
                        src = (w13[c] if c < 2 else w2v)[bass.ds(ex, 1)].rearrange("e p k n -> p (e k) n")
                        sp.dma_start(expert_chunk(c, 8 if c < 2 else 4), src).then_inc(o_w, 16)
                sp.nop()
            with sp.Else():
                sp.nop()

            for t in range(NT):
                sp.wait_ge(out_ready, t + 1)
                sp.dma_start(out[0, P * t:P * (t + 1), :], yg1[t]).then_inc(out_stored[t], 16)
            for t in range(NT):
                sp.wait_ge(out_stored[t], 16)

        @block.gpsimd
        def _(pool):
            pool.memset(ident[:, :], 0.0).then_inc(pool_step, 1)
            pool.memset(before[:, :], 1.0).then_inc(pool_step, 1)
            pool.memset(ones[:, :], 1.0).then_inc(pool_step, 1)
            pool.wait_ge(pool_step, 3)
            pool.affine_select(out=ident[:, :], in_=ident[:, :], compare_op=ALU.not_equal, fill=1.0, base=0,
                               pattern=[[-1, P]], channel_multiplier=1).then_inc(consts_ready, 1)
            column = lambda a: a.rearrange("a (k p) -> p (a k)", p=P)
            pool.dma_start(gain_mix, column(norm_mix), allow_slow_non_contiguous=True).then_inc(gain_loaded, 16)
            for dst, src in ((gain_x, norm_x), (gain_mem, norm_mem), (pscale, pool_scale),
                             (dskip, ssm_d), (glub, glu_b), (gain_ffn_c, norm_ffn)):
                pool.dma_start(dst, column(src), allow_slow_non_contiguous=True).then_inc(cols_loaded, 16)
            pool.affine_select(out=before[:, :], in_=before[:, :], compare_op=ALU.is_gt, fill=0.0, base=0,
                               pattern=[[1, P]], channel_multiplier=-1).then_inc(masks_ready, 1)
            pool.dma_start(poolw[:, :, :], pool_w[0].rearrange("g c d -> c g d")).then_inc(poolw_loaded, 16)
            pool.iota(tok_id[:, :], pattern=[[P, NT]], base=0, channel_multiplier=1).then_inc(tok_ready, 1)
            pool.iota(place_i[:, :], pattern=[[1, CAP]], base=0, channel_multiplier=0).then_inc(tok_ready, 1)
            pool.memset(zeros, 0.0).then_inc(pool_step, 1)
            pool.wait_ge(pool_step, 4)
            pool.dma_start(kern_d.rearrange("g c x -> (g c) x")[:, 0:7 * SSM_C].rearrange("(p r) x -> p r x", p=P),
                           zeros.rearrange("p (r x) -> p r x", r=4)).then_inc(zero_stored, 16)
            pool.dma_start(inv_d.rearrange("(p r) o -> p (r o)", p=CAP), zeros[0:CAP, 0:N_TILES].bitcast(i32)).then_inc(inv_zeroed, 16)
            for gi in range(POOL_G):
                w = 2 << gi
                for c in range(w - 1):
                    pool.memset(cntinv[:, gi, c:c + 1], 1.0 / (c + 1))
                ins = pool.memset(cntinv[:, gi, w - 1:], 1.0 / w)
            ins.then_inc(counts_ready, 1)
            def kv_weights_lo(name):
                for c in range(2):
                    half = slice(2048 * c, 2048 * (c + 1))
                    s_ = CH[name] % RAW
                    pool.wait_ge(weight_hi, 2 * SPLIT.index(name) + c + 1)
                    pool.tensor_tensor(out=ring_r[s_][:, half], in0=ring[s_][:, half], in1=ring_r[hi_slot(name)][:, half],
                                       op=ALU.subtract).then_inc(kv_lo, 1)

            kv_weights_lo("k0")
            kv_weights_lo("k1")
            for c in range(2):
                pool.wait_ge(mem_rounded, c + 1)
                pool.tensor_tensor(out=mem_lo[:, 4 * c:4 * c + 4, :], in0=memT[:, 4 * c:4 * c + 4, :], in1=mem_hi[:, 4 * c:4 * c + 4, :],
                                   op=ALU.subtract).then_inc(mem_split, 1)
            kv_weights_lo("v0")
            kv_weights_lo("v1")
            pool.wait_ge(psum_filled, filled("mix", 3))
            pool.dma_start(rw[:, :, 0:4], router_g_w[0].rearrange("(k p) n -> p k n", p=P)).then_inc(router_loaded, 16)
            pool.dma_start(rw[:, :, 4:20], router_e_w[0].rearrange("(k p) g n -> p k (g n)", p=P)).then_inc(router_loaded, 16)
            pool.wait_ge(psum_filled, filled("bs", 7))
            pool.dma_start(h, x[0].rearrange("(t p) d -> p t d", p=P)).then_inc(h_loaded, 16)
            pool.wait_ge(ys_ready, 4)
            pool.dma_start(gain_ffn, norm_ffn.partition_broadcast(P).rearrange("p a d -> p (a d)")).then_inc(gains_loaded, 16)
            pool.dma_start(gain_fin, norm_final.partition_broadcast(P)).then_inc(gains_loaded, 16)
            pool.wait_ge(psum_filled, filled("q", 7))
            pool.dma_start(rb[:, 0:4], router_g_b.partition_broadcast(P).rearrange("p a n -> p (a n)")).then_inc(gains_loaded, 16)
            pool.dma_start(rb[:, 4:20], router_e_b.partition_broadcast(P).rearrange("p a g n -> p (a g n)")).then_inc(gains_loaded, 16)
            for c in range(4):
                pool.memset(desc[:, c:c + 1], 4.0 - c)
            for c in range(NE):
                ins = pool.memset(base_id[:, c:c + 1], float(CAP * c))
            pool.memset(m_cum[:, 0:16], 0.0)
            for k in range(N_OVER):
                pool.memset(o_k[:, k, :], k + 0.5)
            for q in range(5):
                ins = pool.memset(pre[q][:, 0:16], 0.0)
            ins.then_inc(index_ready, 1)
            for t in range(NT):
                pool.wait_ge(z_normed, t + 1)
                pool.dma_start(z_d[P * t:P * (t + 1), :], xn[:, t, :]).then_inc(z_stored, 16)
            pool.wait_ge(z_stored, 16 * NT)
            pool.wait_ge(first_ready, 1)

            def gather(e, a):
                pool.tensor_copy(idx_one[:, :], idx_first[:, bass.ds(e, 1)] if not isinstance(e, int) else idx_first[:, e:e + 1]).then_inc(idx_ready, 1)
                pool.wait_ge(idx_ready, e + 1)
                pool.sem_inc(pool_tick, 1)
                pool.indirect_dma_start(out=xg[a], out_offset=None, in_=z_d,
                                        in_offset=bass.IndirectOffsetOnAxis(ap=idx_one[:, :], axis=0)).then_inc(gathered[a], 16)
            gather(0, 0)
            pool.wait_ge(gathered[0], 16)
            gather(1, 1)
            pool.wait_ge(gathered[1], 16)
            pool.wait_ge(slots_ready, 1)
            pool.wait_ge(inv_zeroed, 16)
            for s in range(2):
                for t in range(NT):
                    pool.indirect_dma_start(out=inv_d, out_offset=bass.IndirectOffsetOnAxis(ap=slot_i[:, s, t:t + 1], axis=0),
                                            in_=tok_id[:, t:t + 1], in_offset=None).then_inc(inv_stored, 16)
            pool.wait_ge(inv_stored, 16 * 2 * NT)
            pool.dma_start(idx_all[:, :], inv_d.rearrange("(e p) o -> p (e o)", p=CAP), allow_slow_non_contiguous=True).then_inc(inv_loaded, 16)
            pool.wait_ge(inv_loaded, 16)
            with pool.Fori(1, NE // 2) as i:
                for a in range(2):
                    pool.wait_ge(xg_used, 2 * i + a - 1)
                    gather(2 * i + a, a)
                    pool.wait_ge(gathered[a], 16 * i + 16)
            pool.wait_ge(tiles_ready, 1)
            n_over = pool.value_load(tile_i[0:1, N_OVER:N_OVER + 1], min_val=0, max_val=N_OVER)
            with pool.If(n_over > 0):
                with pool.Fori(0, n_over) as k:
                    pool.wait_ge(xg_used, NE)
                    pool.wait_ge(o_down, k + 1)
                    pool.tensor_copy(idx_one[:, :], idx_all[:, bass.ds(k + NE, 1)]).then_inc(o_idx, 1)
                    pool.wait_ge(o_idx, k + 1)
                    pool.sem_inc(pool_tick, 1)
                    pool.indirect_dma_start(out=xg[0], out_offset=None, in_=z_d,
                                            in_offset=bass.IndirectOffsetOnAxis(ap=idx_one[:, :], axis=0)).then_inc(o_gath, 16)
                    pool.wait_ge(o_gath, 16 * k + 16)
                pool.nop()
            with pool.Else():
                pool.nop()
            pool.wait_ge(all_stored, 1)
            pool.wait_ge(rows_filled, 32)
            for t in range(NT):
                pool.indirect_dma_start(out=yg1[t], out_offset=None, in_=y_d,
                                        in_offset=bass.IndirectOffsetOnAxis(ap=slot_i[:, 0, t:t + 1], axis=0)).then_inc(back[t], 16)
                pool.indirect_dma_start(out=yg2[t], out_offset=None, in_=y_d,
                                        in_offset=bass.IndirectOffsetOnAxis(ap=slot_i[:, 1, t:t + 1], axis=0)).then_inc(back[t], 16)

        @block.scalar
        def _(act):
            g = lamg
            act.dma_start(g[0], ssm_a_re[0]).then_inc(ssm_loaded, 16)
            act.dma_start(g[1], ssm_a_im[0]).then_inc(ssm_loaded, 16)
            act.dma_start(g[2][:, 0:1], ssm_log_dt.rearrange("a g -> g a"), allow_slow_non_contiguous=True).then_inc(ssm_loaded, 16)
            steps = [0]

            def link(ins):
                steps[0] += 1
                ins.then_inc(act_step, 1)
                act.wait_ge(act_step, steps[0])

            for t in range(NT):
                act.wait_ge(x_loaded[t], 16)
                if t:
                    act.wait_ge(x_squared, t)
                act.activation(ureg[:, 0:D], h[:, t, :], ACT.Square, scale=1 / 32, accum_out=ss_x[:, t:t + 1]).then_inc(x_squared, 1)
            act.wait_ge(ssm_loaded, 48)
            link(act.activation(g[2][:, 1:2], g[2][:, 0:1], ACT.Exp))
            act.activation(g[3], g[0], ACT.Exp, scale=g[2][:, 1:2]).then_inc(decay_ready, 1)
            for t in range(NT):
                act.wait_ge(x_rstd, t // 2 + 1)
                act.activation(h[:, t, :], h[:, t, :], ACT.Copy, scale=rs_x[:, t:t + 1]).then_inc(x_normed, 1)
            act.dma_start(cload[:, :, 0:64], ssm_c_re[0].rearrange("(t g) c n -> (g c) t n", t=4)).then_inc(ssmb_loaded, 16)
            act.dma_start(cload[:, :, 64:128], ssm_c_im[0].rearrange("(t g) c n -> (g c) t n", t=4)).then_inc(ssmb_loaded, 16)
            act.dma_start(gc(B_s)[0:64], ssm_b_re[0].rearrange("g n c -> n g c")).then_inc(ssmb_loaded, 16)
            act.dma_start(gc(B_s)[64:128], ssm_b_im[0].rearrange("g n c -> n g c")).then_inc(ssmb_loaded, 16)
            act.wait_ge(angle_ready, 2)
            act.activation(g[6], g[4], ACT.Sin)
            act.activation(g[7], g[5], ACT.Sin, scale=0.5).then_inc(sines_ready, 1)

            act.wait_ge(zero_stored, 16)
            act.wait_ge(inv_zeroed, 16)
            def v_drained(lo, hi):
                for m in range(lo, hi):
                    act.wait_ge(psum_filled, filled("v", m))
                    act.activation(vT[:, m, :], bank_of("v", m)[:, :], ACT.Copy).then_inc(act_drained, 1)

            v_drained(0, 2)
            act.wait_ge(psum_filled, filled("cT", 0))
            b = bank_of("cT", 0)
            act.activation(Cy[0:64], b[0:64, :], ACT.Copy)
            act.activation(Cy[64:128], b[64:128, :], ACT.Copy, scale=-1.0)
            act.activation(Cw[0:64], b[64:128, :], ACT.Copy, scale=-1.0)
            act.activation(Cw[64:128], b[0:64, :], ACT.Copy, scale=-1.0).then_inc(act_drained, 1)
            v_drained(2, 4)
            act.wait_ge(mem_loaded, 16)
            for t in range(MT):
                act.activation(msq[:, t, :], mem_tok[:, t, :], ACT.Square, scale=1 / 32, accum_out=ss_m[:, t:t + 1]).then_inc(mem_squared, 1)
            act.wait_ge(mem_squared, MT)
            def round_weights(name):
                j = SPLIT.index(name)
                act.wait_ge(*loaded(name))
                if j >= 2:
                    act.wait_ge(psum_filled, filled(*FRONT[CH[SPLIT[j - 2]]][2]))
                for c in range(2):
                    half = slice(2048 * c, 2048 * (c + 1))
                    act.activation(ring_r[hi_slot(name)][:, half], ring[CH[name] % RAW][:, half], ACT.Copy).then_inc(weight_hi, 1)

            round_weights("k0")
            for m in range(4):
                if m == 2:
                    round_weights("k1")
                act.wait_ge(psum_filled, filled("zp", m))
                act.activation(zp[:, m, PADT:], bank_of("zp", m)[:, :], ACT.Copy).then_inc(act_drained, 1)
            for c in range(2):
                act.wait_ge(*drained("memT", 2 + c))
                act.activation(mem_hi[:, 4 * c:4 * c + 4, :], memT[:, 4 * c:4 * c + 4, :], ACT.Copy).then_inc(mem_rounded, 1)
            for q in range(8):
                act.wait_ge(psum_filled, filled("bT", q))
                act.activation(bpow_m[:, 4 * q:4 * q + 4, :], bank_of("bT", q)[:, :].rearrange("p (g m) -> p g m", g=4),
                               ACT.Copy).then_inc(act_drained, 1)
            for q in range(8):
                act.wait_ge(psum_filled, filled("kern", q))
                act.activation(kern_sb[:, 4 * q:4 * q + 4, :], bank_of("kern", q)[0:SSM_C, :].rearrange("p (g m) -> p g m", g=4),
                               ACT.Copy).then_inc(act_drained, 1)
            act.wait_ge(*drained("kern", 7))
            act.dma_start(kern_d[:, :, 7 * SSM_C:].rearrange("g c x -> c g x"), kern_sb).then_inc(kern_stored, 16)
            act.wait_ge(pool_diff, POOL_G)
            for l in range(LCH):
                act.wait_ge(psum_filled, filled("vl", l))
                act.activation(vj[:, :, LCH - 1 - l, :], bank_of("vl", l)[0:NCH, :].rearrange("p (g c) -> p g c", g=SSM_G),
                               ACT.Copy).then_inc(act_drained, 1)
            act.wait_ge(kern_stored, 16)
            for q in range(4):
                act.wait_ge(psum_filled, filled("vch", q))
                act.activation(vch[:, 8 * q:8 * q + 8, :], bank_of("vch", q)[:, :].rearrange("p (g q) -> p g q", g=8),
                               ACT.Copy).then_inc(act_drained, 1)
            for q in range(4):
                act.wait_ge(psum_filled, filled("st", q))
                b = bank_of("st", q)[:, :].rearrange("p (g q) -> p g q", g=8)
                gs = slice(8 * q, 8 * q + 8)
                act.activation(hin[:, gs, 0, :], b, ACT.Copy)
                act.activation(hin[0:64, gs, 1, :], b[64:128], ACT.Copy, scale=-1.0)
                act.activation(hin[64:128, gs, 1, :], b[0:64], ACT.Copy).then_inc(act_drained, 1)
            act.wait_ge(cols_loaded, 96)
            for g_ in range(4):
                act.wait_ge(psum_filled, filled("mix", g_))
                act.activation(ypT[:, g_, :], bank_of("mix", g_)[:, :], ACT.Copy, scale=pscale[:, g_:g_ + 1]).then_inc(act_drained, 1)
            for m in range(4):
                if m == 2:
                    round_weights("v0")
                act.wait_ge(psum_filled, filled("kk", m))
                act.activation(kT[:, 2 * m:2 * m + 2, :], bank_of("kk", m)[:, :].rearrange("p (k m) -> p k m", k=2),
                               ACT.Copy).then_inc(act_drained, 1)
            round_weights("v1")
            for n in range(4):
                if n == 2:
                    round_weights("g0")
                act.wait_ge(psum_filled, filled("vv", n))
                act.activation(vm[:, n % 2, HALF * (n // 2):HALF * (n // 2 + 1)], bank_of("vv", n)[:, :],
                               ACT.Copy).then_inc(act_drained, 1)

            for k in range(KD):
                act.activation(u_hi[:, k, :], uT[:, k, :], ACT.Copy).then_inc(u_rounded, 1)
            round_weights("g1")

            def gates(lo, hi):
                for m in range(lo, hi):
                    act.wait_ge(psum_filled, filled("gate", m))
                    act.activation(gT[:, m, :], bank_of("gate", m)[:, :], ACT.Sigmoid).then_inc(act_drained, 1)

            gates(0, 5)
            for m in range(4):
                act.wait_ge(*drained("yT", m))
                act.activation(ygT[:, m, :], vT[:, m, :], ACT.Gelu_apprx_tanh).then_inc(gelu_ready, 1)
            gates(5, 6)
            round_weights("g2")
            gates(6, 8)
            for m in range(4):
                act.activation(yp_hi[:, m, :], ypT[:, m, :], ACT.Copy).then_inc(yp_rounded, 1)
            for m in range(4):
                act.wait_ge(psum_filled, filled("glu", m))
                act.activation(vT[:, m, :], bank_of("glu", m)[:, :], ACT.Sigmoid, bias=glub[:, m:m + 1]).then_inc(act_drained, 1)
            for m in range(4):
                act.wait_ge(ys_ready, m + 1)
                act.activation(ys_hi[:, m, :], ysT[:, m, :], ACT.Copy).then_inc(ys_rounded, 1)
            gates(8, 10)
            round_weights("g3")
            gates(10, 13)
            round_weights("bp")
            gates(13, 16)
            round_weights("bs")
            round_weights("o0")
            for m in range(KD):
                act.wait_ge(mg_exact, m + 1)
                act.activation(mg_hi[:, m, :], gT[:, m, :], ACT.Copy).then_inc(mg_rounded, 1)
            round_weights("o1")

            def round_hn(t):
                for n in range(2):
                    act.wait_ge(*drained("hT", 2 * t + n))
                    act.activation(hn_hi[:, 4 * n:4 * n + 4, P * t:P * (t + 1)], hnT[:, 4 * n:4 * n + 4, P * t:P * (t + 1)],
                                   ACT.Copy).then_inc(hn_rounded, 1)

            for t in range(NT):
                round_hn(t)
                if t == 1:
                    round_weights("q0")
            for t in range(NT):
                act.wait_ge(*drained("wo1", 2 * t + 1))
                act.activation(xn[:, t, :], h[:, t, :], ACT.Square, scale=1 / 32, accum_out=ss_h[:, t:t + 1]).then_inc(h_squared, 1)
            round_weights("q1")
            def probs(hd):
                for n in range(2):
                    act.wait_ge(neg_max, 2 * hd + n + 1)
                    if hd >= 2 and n == 0:
                        act.wait_ge(psum_filled, filled("pT", 2 * hd - 3))
                    b = bank_of("sc", 2 * hd + n)[:, :].rearrange("p (t m) -> p t m", t=2)
                    for s in range(2):
                        t = 2 * n + s
                        ins = act.activation(prob[:, hd % 2, t, :], b[:, s, :], ACT.Exp, scale=qscale[:, 0, t:t + 1],
                                             bias=nmax[:, 4 * hd + t:4 * hd + t + 1], accum_out=esum[:, 4 * hd + t:4 * hd + t + 1])
                    ins.then_inc(act_drained, 1)

            def round_o(hd):
                for n in range(2):
                    act.wait_ge(*drained("pv", 2 * hd + n))
                    act.activation(o_hi[:, 2 * hd + n, :], oT[:, 2 * hd + n, :], ACT.Copy).then_inc(o_rounded, 1)

            for hd in range(HEADS + 1):
                if hd < HEADS:
                    for m in Q_AHEAD[hd]:
                        act.wait_ge(psum_filled, filled("q", m))
                        act.activation(qT[:, m, :], bank_of("q", m)[:, :], ACT.Copy).then_inc(act_drained, 1)
                if hd >= 1:
                    for n in range(2):
                        act.wait_ge(psum_filled, filled("pT", 2 * (hd - 1) + n))
                        act.activation(probT[:, (hd - 1) % 2, n, :], bank_of("pT", 2 * (hd - 1) + n)[:, :], ACT.Copy).then_inc(act_drained, 1)
                if hd < HEADS:
                    probs(hd)
                if hd == 1:
                    round_weights("w0")
                if hd == 3:
                    round_o(0)
                    round_o(1)
                if hd == 4:
                    round_o(2)
            round_o(HEADS - 1)
            round_weights("w1")

            def z_transposed(t):
                for n in range(2):
                    act.wait_ge(psum_filled, filled("zT", 2 * t + n))
                    act.activation(zT[:, 4 * n:4 * n + 4, P * t:P * (t + 1)],
                                   bank_of("zT", 2 * t + n)[:, :].rearrange("p (k t) -> p k t", k=4), ACT.Copy).then_inc(act_drained, 1)

            for t in range(NT):
                act.wait_ge(*drained("wo2", 2 * t + 1))
                if t == 0:
                    act.wait_ge(psum_filled, filled("pv", 7))
                act.activation(xn[:, t, :], h[:, t, :], ACT.Square, scale=1 / 32, accum_out=ss_z[:, t:t + 1]).then_inc(z_squared, 1)
                if t >= 1:
                    z_transposed(t - 1)
            z_transposed(NT - 1)
            act.wait_ge(g_shift, 1)
            act.activation(q4[0], q4[1], ACT.Exp).then_inc(g_exp, 1)
            act.wait_ge(e_shift, 1)
            act.activation(r4[1], r4[2], ACT.Exp).then_inc(e_exp, 1)

            act.sem_inc(silu_ready, 2)
            act.sem_inc(y_act, 1)

            act.wait_ge(psum_filled, filled("route", NT - 1))

            def expert(e, a, i, n_st):
                act.wait_ge(slot_loaded[expert_slot(a, 2)], front_loads[expert_slot(a, 2)] + 16 * i + 16)
                if not isinstance(e, int) or e > 0:
                    act.wait_ge(down_done, 2 * e)
                for c in range(2):
                    half = slice(2048 * c, 2048 * (c + 1))
                    act.activation(ureg_r[:, half], ring[expert_slot(a, 2)][:, half], ACT.Copy).then_inc(w2_hi, 1)
                act.wait_ge(up_done, e + 1)
                act.wait_ge(hid_ready, e + 1)
                act.activation(silu[a], bank[2 + 4 * a][:, 0:4 * CAP], ACT.Silu).then_inc(silu_ready, 1)
                act.wait_ge(down_done, 2 * e + 2)
                if n_st is not None:
                    act.wait_ge(y_stored[a], n_st)
                act.activation(ysb[a][:, HALF:D], bank[5][0:CAP, :], ACT.Copy).then_inc(y_act, 1)
                act.wait_ge(y_act, e + 2)
                act.wait_ge(y_dve, e + 2)
                act.dma_start(y_d[bass.ds(e * CAP, CAP), :], ysb[a]).then_inc(y_stored[a], 16)

            expert(0, 0, 0, None)
            expert(1, 1, 0, None)
            with act.Fori(1, NE // 2) as i:
                for a in range(2):
                    expert(2 * i + a, a, i, 16 * i)
            act.wait_ge(y_stored[0], 8 * NE)
            act.wait_ge(y_stored[1], 8 * NE)
            act.wait_ge(tiles_ready, 1)
            n_over = act.value_load(tile_i[0:1, N_OVER:N_OVER + 1], min_val=0, max_val=N_OVER)
            with act.If(n_over > 0):
                act.wait_ge(rows_filled, 32)
                with act.Fori(0, n_over) as k:
                    act.wait_ge(o_up, k + 1)
                    act.activation(silu[0], bank[2][:, 0:4 * CAP], ACT.Silu).then_inc(o_silu, 1)
                    act.wait_ge(o_y, k + 1)
                    act.dma_start(y_d[bass.ds((k + NE) * CAP, CAP), :], ysb[0]).then_inc(o_stored, 16)
                    act.wait_ge(o_stored, 16 * k + 16)
                act.nop()
            with act.Else():
                act.nop()
            act.sem_inc(all_stored, 1)
            for t in range(NT):
                act.wait_ge(combined, t + 1)
                if t:
                    act.wait_ge(o_squared, t)
                act.activation(ureg[:, 0:D], h[:, t, :], ACT.Square, scale=1 / 32, accum_out=ss_o[:, t:t + 1]).then_inc(o_squared, 1)

        @block.vector
        def _(dve):
            V = nc.vector
            steps = [0]

            def link(ins):
                steps[0] += 1
                ins.then_inc(dve_step, 1)
                dve.wait_ge(dve_step, steps[0])

            def tt(o_, a, b, op):
                return V.tensor_tensor(out=o_, in0=a, in1=b, op=op)

            def ts(o_, a, s1, op0, s2=None, op1=None):
                if op1 is None:
                    return V.tensor_scalar(o_, a, s1, None, op0)
                return V.tensor_scalar(o_, a, s1, s2, op0, op1)

            def rstd(o_, ss, done=None):
                n = ss.shape[1]
                v, t_ = newton[:, 0:n], newton[:, 4:4 + n]
                link(ts(v, ss, EPS, ALU.add))
                link(ts(t_.bitcast(i32), v.bitcast(i32), 1, ALU.logical_shift_right))
                link(ts(o_.bitcast(i32), t_.bitcast(i32), -1.0, ALU.mult, float(0x5F3759DF), ALU.add))
                for r in range(3):
                    link(tt(t_, o_, o_, ALU.mult))
                    link(V.scalar_tensor_tensor(out=t_, in0=t_, scalar=-0.5, in1=v, op0=ALU.mult, op1=ALU.mult))
                    ins = V.scalar_tensor_tensor(out=o_, in0=t_, scalar=1.5, in1=o_, op0=ALU.add, op1=ALU.mult)
                    if r == 2 and done is not None:
                        ins.then_inc(done, 1)
                    else:
                        link(ins)

            for q in range(2):
                dve.wait_ge(x_squared, 2 * q + 2)
                rstd(rs_x[:, 2 * q:2 * q + 2], ss_x[:, 2 * q:2 * q + 2], x_rstd)
            dve.wait_ge(gain_loaded, 16)

            def transposed(name, i, dst, gain):
                dve.wait_ge(psum_filled, filled(name, i))
                tt(dst, bank_of(name, i)[:, :].rearrange("p (k t) -> p k t", k=4), gain.unsqueeze(2).to_broadcast([P, 4, P]),
                   ALU.mult).then_inc(dve_drained, 1)

            for i in range(8):
                t, n = i // 2, i % 2
                transposed("xT", i, uT[:, 4 * n:4 * n + 4, P * t:P * (t + 1)], gain_mix[:, 4 * n:4 * n + 4])
            g = lamg
            TWO_PI = 2 * math.pi
            c1 = 6.28125
            c2 = float(int((TWO_PI - c1) * 2 ** 22)) / 2 ** 22
            c3 = TWO_PI - c1 - c2
            MAGIC = 1.5 * 2.0 ** 23
            dve.wait_ge(decay_ready, 1)
            link(ts(g[8], g[1], g[2][:, 1:2], ALU.mult))
            link(ts(g[9], g[8], 1 / TWO_PI, ALU.mult, MAGIC, ALU.add))
            link(ts(g[9], g[9], MAGIC, ALU.subtract))
            for c in (c1, c2, c3):
                link(V.scalar_tensor_tensor(out=g[8], in0=g[9], scalar=-c, in1=g[8], op0=ALU.mult, op1=ALU.add))
            ts(g[4], g[8], 3.1415925, ALU.min, -3.1415925, ALU.max).then_inc(angle_ready, 1)
            ts(g[5], g[8], 3.1415925, ALU.min, -3.1415925, ALU.max).then_inc(angle_ready, 1)
            dve.wait_ge(sines_ready, 1)
            link(tt(g[10], g[7], g[7], ALU.mult))
            link(ts(g[10], g[10], -2.0, ALU.mult, 1.0, ALU.add))
            link(tt(g[11], g[3], g[10], ALU.mult))
            link(tt(g[12], g[3], g[6], ALU.mult))
            link(tt(g[13], g[0], g[0], ALU.mult))
            link(tt(g[14], g[1], g[1], ALU.mult))
            link(tt(g[13], g[13], g[14], ALU.add))
            link(V.reciprocal(g[13], g[13]))
            link(ts(g[15], g[11], 1.0, ALU.subtract))
            link(tt(g[16], g[15], g[0], ALU.mult))
            link(tt(g[17], g[12], g[1], ALU.mult))
            link(tt(g[16], g[16], g[17], ALU.add))
            link(tt(g[18], g[12], g[0], ALU.mult))
            link(tt(g[19], g[15], g[1], ALU.mult))
            link(tt(g[18], g[18], g[19], ALU.subtract))
            link(tt(g[16], g[16], g[13], ALU.mult))
            link(tt(g[18], g[18], g[13], ALU.mult))
            for n, s in enumerate((11, 12, 16, 18)):
                ins = V.tensor_copy(lamq[:, n, :, :], g[s].unsqueeze(1).to_broadcast([SSM_G, 2, SSM_N]))
            ins.then_inc(lam_ready, 1)

            dve.wait_ge(psum_filled, filled("lam", 0))
            V.tensor_copy(lamL, bank_of("lam", 0)[:, 0:4 * SSM_G].rearrange("p (q g) -> p q g", q=4)).then_inc(dve_drained, 1)
            dve.wait_ge(*drained("lam", 0))
            LR, LI, FR, FI = (lamL[:, n, :] for n in range(4))
            over_c = lambda a: a.unsqueeze(2).to_broadcast([P, SSM_G, SSM_C])
            dve.wait_ge(ssmb_loaded, 64)

            def swapped(dst, src):
                link(ts(dst[0:64], src[64:128], -1.0, ALU.mult))
                link(V.tensor_copy(dst[64:128], src[0:64]))

            swapped(B_w, B_s)
            t1 = gtmp[:, 0:512]
            link(tt(gc(Bb), gc(B_s), over_c(FR), ALU.mult))
            link(tt(gc(t1), gc(B_w), over_c(FI), ALU.mult))
            link(tt(Bb, Bb, t1, ALU.add))
            swapped(Bbw, Bb)

            def powers(dst, base_r, base_i, tmp_at):
                link(V.tensor_copy(dst[:, 0, 0, :], base_r))
                link(V.tensor_copy(dst[:, 0, 1, :], base_i))
                n = 1
                while n < 8:
                    lo = dst[:, 0:n]
                    br = dst[:, n - 1, 0, :].unsqueeze(1).to_broadcast([P, n, SSM_G])
                    bi = dst[:, n - 1, 1, :].unsqueeze(1).to_broadcast([P, n, SSM_G])
                    tmp = tmp_at[:, 0:n * SSM_G].rearrange("p (k g) -> p k g", k=n)
                    hi = dst[:, n:2 * n]
                    link(tt(hi[:, :, 0, :], lo[:, :, 0, :], br, ALU.mult))
                    link(tt(tmp, lo[:, :, 1, :], bi, ALU.mult))
                    link(tt(hi[:, :, 0, :], hi[:, :, 0, :], tmp, ALU.subtract))
                    link(tt(hi[:, :, 1, :], lo[:, :, 0, :], bi, ALU.mult))
                    link(tt(tmp, lo[:, :, 1, :], br, ALU.mult))
                    link(tt(hi[:, :, 1, :], hi[:, :, 1, :], tmp, ALU.add))
                    n *= 2

            powers(pw, LR, LI, gtmp[:, 512:640])
            dve.wait_ge(*drained("cT", 0))
            link(V.tensor_copy(bpow[:, :, 0, :], gc(Bb)))

            def scaled(dst, a, b, lo, n):
                four = [P, SSM_G, n, SSM_C]
                bc = lambda v: gc(v).unsqueeze(2).to_broadcast(four)
                pr, pi = (pw[:, lo:lo + n, x_, :].rearrange("p k g -> p g k").unsqueeze(3).to_broadcast(four) for x_ in range(2))
                tmp = gtmp_k[:, :, 0:n, :]
                link(tt(dst, bc(a), pr, ALU.mult))
                link(tt(tmp, bc(b), pi, ALU.mult))
                return tt(dst, dst, tmp, ALU.add)

            link(scaled(bpow[:, :, 1:5, :], Bb, Bbw, 0, 4))
            link(scaled(bpow[:, :, 5:8, :], Bb, Bbw, 4, 3))
            link(scaled(cpow[:, :, 0:4, :], Cy, Cw, 0, 4))
            scaled(cpow[:, :, 4:8, :], Cy, Cw, 4, 4).then_inc(powers_ready, 1)
            powers(lam8, pw[:, 7, 0, :], pw[:, 7, 1, :], B_s)

            dve.wait_ge(mem_squared, MT)
            rstd(rs_m, ss_m, mem_rstd)
            dve.wait_ge(mem_rstd, 1)
            for t in range(MT):
                ts(mem_tok[:, t, :], mem_tok[:, t, :], rs_m[:, t:t + 1], ALU.mult).then_inc(mem_normed, 1)
            for i in range(4):
                t, n = i // 2, i % 2
                transposed("memT", i, memT[:, 4 * n:4 * n + 4, P * t:P * (t + 1)], gain_mem[:, 4 * n:4 * n + 4])

            for b in range(2):
                link(V.memset(ptmp[:, b, 0:PADT], 0.0))
            link(V.memset(zp[:, :, 0:PADT], 0.0))
            dve.wait_ge(counts_ready, 1)
            for gi in range(POOL_G):
                dve.wait_ge(*drained("zp", gi))
                src, w = zp[:, gi, :], 1
                for s in range(gi + 1):
                    dst = ptmp[:, s % 2, :]
                    link(tt(dst[:, PADT:], src[:, PADT:], src[:, PADT - w:PADT + SEQ - w], ALU.add))
                    src, w = dst, 2 * w
                link(V.scalar_tensor_tensor(out=zp[:, gi, 2 * PADT:], in0=src[:, 2 * PADT:], scalar=1.0 / w,
                                            in1=zp[:, gi, 2 * PADT:], op0=ALU.mult, op1=ALU.subtract))
                link(tt(src[:, PADT:2 * PADT], src[:, PADT:2 * PADT], cntinv[:, gi, :], ALU.mult))
                ins = tt(zp[:, gi, PADT:2 * PADT], src[:, PADT:2 * PADT], zp[:, gi, PADT:2 * PADT], ALU.subtract)
                ins.then_inc(pool_diff, 1)
                dve.wait_ge(pool_diff, gi + 1)

            def lo_of(lo, exact, hi):
                return tt(lo, exact, hi, ALU.subtract)

            def weights_lo(name):
                j = SPLIT.index(name)
                for c in range(2):
                    half = slice(2048 * c, 2048 * (c + 1))
                    s_ = CH[name] % RAW
                    dve.wait_ge(weight_hi, 2 * j + c + 1)
                    lo_of(ring_r[s_][:, half], ring[s_][:, half], ring_r[hi_slot(name)][:, half]).then_inc(weight_lo, 1)

            dve.wait_ge(*drained("st", 3))
            A1 = stmp[:, 0:512].rearrange("p (g x s) -> p g x s", g=SSM_G, x=2)
            A2 = stmp[:, 512:1024].rearrange("p (g x s) -> p g x s", g=SSM_G, x=2)
            S = stmp[:, 1024:1536].rearrange("p (g x s) -> p g x s", g=SSM_G, x=2)
            l8r, l8i = lam8[:, 0, 0, :], lam8[:, 0, 1, :]
            gxs = [P, SSM_G, 2, SUP]
            for j in range(1, SUP):
                old, new = W[:, :, :, :, j - 1], W[:, :, :, :, j]
                link(tt(A1, old, l8r.unsqueeze(2).unsqueeze(3).to_broadcast(gxs), ALU.mult))
                im = l8i.unsqueeze(2).to_broadcast([P, SSM_G, SUP])
                link(tt(A2[:, :, 0, :], old[:, :, 1, :], im, ALU.mult))
                link(V.scalar_tensor_tensor(out=A2[:, :, 1, :], in0=old[:, :, 0, :], scalar=-1.0, in1=im, op0=ALU.mult, op1=ALU.mult))
                link(tt(A1, A1, A2, ALU.add))
                link(tt(new, new, A1, ALU.add))
            link(V.memset(S[:, :, :, 0], 0.0))
            l64r, l64i = lam8[:, 7, 0, :], lam8[:, 7, 1, :]
            for s in range(SUP - 1):
                old, new = S[:, :, :, s], S[:, :, :, s + 1]
                link(tt(A1[:, :, :, 0], old, l64r.unsqueeze(2).to_broadcast([P, SSM_G, 2]), ALU.mult))
                link(tt(A2[:, :, 0, 0], old[:, :, 1], l64i, ALU.mult))
                link(V.scalar_tensor_tensor(out=A2[:, :, 1, 0], in0=old[:, :, 0], scalar=-1.0, in1=l64i, op0=ALU.mult, op1=ALU.mult))
                link(tt(A1[:, :, :, 0], A1[:, :, :, 0], A2[:, :, :, 0], ALU.add))
                link(tt(new, A1[:, :, :, 0], W[:, :, :, s, SUP - 1], ALU.add))
            Hn = W[:, :, 1, :, :]
            link(V.tensor_copy(Hn[:, :, :, 0], S[:, :, 0, :]))
            for j in range(1, SUP):
                pr, pi = (lam8[:, j - 1, x_, :].unsqueeze(2).to_broadcast([P, SSM_G, SUP]) for x_ in range(2))
                B1, B2 = A1[:, :, 0, :], A2[:, :, 0, :]
                link(tt(B1, S[:, :, 0, :], pr, ALU.mult))
                link(tt(B2, S[:, :, 1, :], pi, ALU.mult))
                link(tt(B1, B1, B2, ALU.add))
                ins = tt(Hn[:, :, :, j], B1, W[:, :, 0, :, j - 1], ALU.add)
                if j < SUP - 1:
                    link(ins)
            ins.then_inc(states_ready, 1)
            weights_lo("g0")
            for k in range(KD):
                dve.wait_ge(u_rounded, k + 1)
                lo_of(u_lo[:, k, :], uT[:, k, :], u_hi[:, k, :]).then_inc(u_split, 1)
            for q in range(8):
                dve.wait_ge(psum_filled, filled("y", q | 1))
                n = q % 2
                V.tensor_copy(yj_g[:, q // 2, 4 * n:4 * n + 4, :, :],
                              bank_of("y", q)[0:NCH, :].rearrange("p (g l c) -> p g l c", g=4, l=LCH)).then_inc(dve_drained, 1)
            weights_lo("g1")
            jl = lambda a: a.rearrange("p (j l) -> p l j", l=LCH)
            for m in range(4):
                dve.wait_ge(psum_filled, filled("yT", m))
                V.scalar_tensor_tensor(out=jl(vT[:, m, :]), in0=jl(vT[:, m, :]), scalar=dskip[:, m:m + 1],
                                       in1=bank_of("yT", m)[:, :].rearrange("p (l j) -> p l j", l=LCH),
                                       op0=ALU.mult, op1=ALU.add).then_inc(dve_drained, 1)
            weights_lo("g2")
            for m in range(4):
                dve.wait_ge(yp_rounded, m + 1)
                lo_of(yp_lo[:, m, :], ypT[:, m, :], yp_hi[:, m, :]).then_inc(yp_split, 1)
            for m in range(4):
                dve.wait_ge(*drained("glu", m))
                tt(ysT[:, m, :], vT[:, m, :], ygT[:, m, :], ALU.mult).then_inc(ys_ready, 1)
            for m in range(4):
                dve.wait_ge(ys_rounded, m + 1)
                lo_of(ys_lo[:, m, :], ysT[:, m, :], ys_hi[:, m, :]).then_inc(ys_split, 1)
            weights_lo("g3")
            weights_lo("bp")
            dve.wait_ge(*drained("gate", 15))
            for m in range(KD):
                dve.wait_ge(psum_filled, filled("bp", m))
                tt(gT[:, m, :], gT[:, m, :], bank_of("bp", m)[:, :], ALU.mult).then_inc(dve_drained, 1)
                if m == 1:
                    weights_lo("bs")
            for m in range(KD + 1):
                if m < KD:
                    dve.wait_ge(psum_filled, filled("bs", m))
                    tt(gT[:, KD + m, :], gT[:, KD + m, :], bank_of("bs", m)[:, :], ALU.mult).then_inc(dve_drained, 1)
                    dve.wait_ge(*drained("bs", m))
                    tt(gT[:, m, :], gT[:, m, :], gT[:, KD + m, :], ALU.add).then_inc(mg_exact, 1)
                    if m == 1:
                        weights_lo("o0")
                if m >= 1:
                    dve.wait_ge(mg_rounded, m)
                    lo_of(mg_lo[:, m - 1, :], gT[:, m - 1, :], mg_hi[:, m - 1, :]).then_inc(merged_ready, 1)
            weights_lo("o1")
            dve.wait_ge(h_loaded, 16)

            def h_transposed(t):
                for n in range(2):
                    transposed("hT", 2 * t + n, hnT[:, 4 * n:4 * n + 4, P * t:P * (t + 1)], gain_x[:, 4 * n:4 * n + 4])

            def residual(name, i):
                dve.wait_ge(psum_filled, filled(name, i))
                hs = h[:, i // 2, HALF * (i % 2):HALF * (i % 2 + 1)]
                tt(hs, hs, bank_of(name, i)[:, :], ALU.add).then_inc(dve_drained, 1)

            def hn_remainder(t):
                for n in range(2):
                    at_ = (slice(None), slice(4 * n, 4 * n + 4), slice(P * t, P * (t + 1)))
                    dve.wait_ge(hn_rounded, 2 * t + n + 1)
                    lo_of(hn_lo[at_], hnT[at_], hn_hi[at_]).then_inc(hn_split, 1)

            for banks_, t in ROWS:
                for i in banks_:
                    residual("wo1", i)
                if t is not None:
                    h_transposed(t)
                if t == 1:
                    hn_remainder(0)
                    hn_remainder(1)
                    weights_lo("q0")
            hn_remainder(2)
            hn_remainder(3)
            dve.wait_ge(h_squared, NT)
            rstd(rs_h, ss_h)
            link(ts(qscale[:, 0, :], rs_h, HD ** -0.5, ALU.mult))
            link(ts(qscale[:, 1, :], rs_h, -HD ** -0.5, ALU.mult))
            weights_lo("q1")
            dve.wait_ge(router_loaded, 32)
            tt(rw, rw, gain_ffn_c.unsqueeze(2).to_broadcast([P, KD, 20]), ALU.mult).then_inc(router_scaled, 1)
            def maxima(hd):
                for n in range(2):
                    dve.wait_ge(psum_filled, filled("sc", 2 * hd + n))
                    at_ = 4 * hd + 2 * n
                    link(V.tensor_reduce(out=rmax[:, at_:at_ + 2], in_=bank_of("sc", 2 * hd + n)[:, :].rearrange("p (t m) -> p t m", t=2),
                                         axis=AX.X, op=ALU.max))
                    tt(nmax[:, at_:at_ + 2], rmax[:, at_:at_ + 2], qscale[:, 1, 2 * n:2 * n + 2], ALU.mult).then_inc(neg_max, 1)

            def divide(hd):
                for n in range(2):
                    dve.wait_ge(*drained("sc", 2 * hd + n))
                    at_ = 4 * hd + 2 * n
                    link(V.reciprocal(rsum[:, at_:at_ + 2], esum[:, at_:at_ + 2]))
                    for s in range(2):
                        t = 2 * n + s
                        ins = ts(prob[:, hd % 2, t, :], prob[:, hd % 2, t, :], rsum[:, at_ + s:at_ + s + 1], ALU.mult)
                    ins.then_inc(prob_ready, 1)

            def o_remainder(hd):
                for n in range(2):
                    dve.wait_ge(o_rounded, 2 * hd + n + 1)
                    lo_of(o_lo[:, 2 * hd + n, :], oT[:, 2 * hd + n, :], o_hi[:, 2 * hd + n, :]).then_inc(o_split, 1)

            for hd in range(HEADS + 1):
                if hd < HEADS:
                    maxima(hd)
                if hd == HEADS:
                    o_remainder(2)
                if hd >= 1:
                    for n in range(2):
                        dve.wait_ge(psum_filled, filled("pv", 2 * (hd - 1) + n))
                        V.tensor_copy(oT[:, 2 * (hd - 1) + n, :], bank_of("pv", 2 * (hd - 1) + n)[:, :]).then_inc(dve_drained, 1)
                if hd < HEADS:
                    divide(hd)
                if hd == 1:
                    weights_lo("w0")
                if hd == 3:
                    o_remainder(0)
                    o_remainder(1)
            o_remainder(HEADS - 1)
            weights_lo("w1")
            dve.wait_ge(gains_loaded, 64)

            def logits_of(t):
                dve.wait_ge(psum_filled, filled("route", t))
                V.scalar_tensor_tensor(out=logits[:, t, :], in0=bank_of("route", t)[:, 0:20], scalar=rs_z[:, t:t + 1], in1=rb,
                                       op0=ALU.mult, op1=ALU.add).then_inc(dve_drained, 1)

            for t in range(NT):
                for i in WO2[t]:
                    residual("wo2", i)
                dve.wait_ge(z_squared, t + 1)
                rstd(rs_z[:, t:t + 1], ss_z[:, t:t + 1])
                V.scalar_tensor_tensor(out=xn[:, t, :], in0=h[:, t, :], scalar=rs_z[:, t:t + 1], in1=gain_ffn,
                                       op0=ALU.mult, op1=ALU.mult).then_inc(z_normed, 1)
                if t >= 2:
                    logits_of(t - 2)
            logits_of(NT - 2)

            t4 = lambda a: a.unsqueeze(2).to_broadcast([P, NT, 4])
            n4 = lambda a: a.unsqueeze(1).to_broadcast([P, NT, 4])
            ts4 = lambda a: a.unsqueeze(1).to_broadcast([P, NT, 16])
            dve.wait_ge(index_ready, 1)
            dve.wait_ge(tok_ready, 2)
            V.tensor_copy(place, place_i[:, :])
            link(V.tensor_copy(tok_f, tok_id[:, :]))
            logits_of(NT - 1)
            dve.wait_ge(*drained("route", NT - 1))

            def first_max(mask, top, src, t_a, t_b):
                link(V.tensor_reduce(out=top, in_=src, axis=AX.X, op=ALU.max))
                link(tt(t_a, src, t4(top), ALU.is_equal))
                link(tt(t_a, t_a, n4(desc), ALU.mult))
                link(V.tensor_reduce(out=t_b, in_=t_a, axis=AX.X, op=ALU.max))
                link(tt(mask, t_a, t4(t_b), ALU.is_equal))

            gmask, esel, top1, top2, e2 = q4[2], q4[3], q4[4], q4[5], q4[6]
            first_max(gmask, r4[3], lg, q4[7], r4[4])
            tt(q4[1], lg, t4(r4[3]), ALU.subtract).then_inc(g_shift, 1)
            le4 = le.rearrange("p t (g e) -> p t g e", g=4)
            link(tt(e64[0].rearrange("p t (g e) -> p t g e", g=4), le4, gmask.unsqueeze(3).to_broadcast([P, NT, 4, 4]), ALU.mult))
            link(V.tensor_reduce(out=esel, in_=e64[0].rearrange("p t (g e) -> p t e g", g=4), axis=AX.X, op=ALU.add))
            first_max(top1, r4[5], esel, q4[7], r4[4])
            link(ts(q4[8], top1, -1.0, ALU.mult, 1.0, ALU.add))
            link(tt(e2, esel, q4[8], ALU.mult))
            link(ts(q4[9], top1, -3.0e38, ALU.mult))
            link(tt(e2, e2, q4[9], ALU.add))
            first_max(top2, r4[6], e2, q4[7], r4[4])
            tt(r4[2], r4[6], r4[5], ALU.subtract).then_inc(e_shift, 1)
            for n, tm in ((1, top1), (2, top2)):
                link(tt(e64[n].rearrange("p t (g e) -> p t g e", g=4), gmask.unsqueeze(3).to_broadcast([P, NT, 4, 4]),
                        tm.unsqueeze(2).to_broadcast([P, NT, 4, 4]), ALU.mult))
            link(tt(e64[3], e64[1], e64[2], ALU.add))
            mc = m_cum.rearrange("p (t n) -> p t n", t=5)
            link(V.tensor_copy(mc[:, 1, :], e64[3][:, 0, :]))
            for t in range(1, NT):
                ins = tt(mc[:, t + 1, :], mc[:, t, :], e64[3][:, t, :], ALU.add)
                if t < NT - 1:
                    link(ins)
            ins.then_inc(mask_ready, 1)
            dve.wait_ge(g_exp, 1)
            link(V.tensor_reduce(out=r4[7], in_=q4[0], axis=AX.X, op=ALU.add))
            link(V.reciprocal(r4[7], r4[7]))
            dve.wait_ge(e_exp, 1)
            link(ts(r4[8], r4[1], 1.0, ALU.add))
            link(V.reciprocal(r4[8], r4[8]))
            link(tt(gw[:, 0, :], r4[8], r4[7], ALU.mult))
            link(tt(gw[:, 1, :], gw[:, 0, :], r4[1], ALU.mult))
            for n in range(2):
                ins = tt(tok_of[:, n, :, :], e64[1 + n], tok_f.unsqueeze(2).to_broadcast([P, NT, 16]), ALU.mult)
            dve.wait_ge(psum_filled, filled("rank", 0))
            rk = bank_of("rank", 0)
            V.tensor_copy(x64, rk[:, 0:64].rearrange("p (t n) -> p t n", t=NT))
            V.tensor_copy(n16[0], rk[:, 64:80]).then_inc(dve_drained, 1)
            dve.wait_ge(*drained("rank", 0))
            for n in range(2):
                ins = tt(e64[6 + n], x64, e64[1 + n], ALU.mult)
            link(ins)
            for n in range(2):
                ins = V.tensor_reduce(out=rank_f[:, n, :], in_=e64[6 + n], axis=AX.X, op=ALU.add)
            link(ins)
            for n in range(2):
                for t in range(NT):
                    ins = ts(at_rank[:, n, t, :], place, rank_f[:, n, t:t + 1], ALU.is_equal)
            ins.then_inc(at_rank_ready, 1)
            dve.wait_ge(psum_filled, filled("index", 0))
            V.tensor_copy(idx_first[:, :], bank_of("index", 0)[0:CAP, 0:NE]).then_inc(dve_drained, 1)
            dve.wait_ge(*drained("index", 0))
            dve.sem_inc(first_ready, 1)
            link(ts(n16[1], n16[0], CAP + 0.5, ALU.is_gt))
            for k in range(2, -(-SEQ // CAP)):
                link(V.scalar_tensor_tensor(out=n16[1], in0=n16[0], scalar=CAP * k + 0.5, in1=n16[1], op0=ALU.is_gt, op1=ALU.add))
            link(V.tensor_copy(pre[0][:, 16:], n16[1]))
            for s, sh in enumerate((1, 2, 4, 8)):
                link(tt(pre[s + 1][:, 16:], pre[s][:, 16:], pre[s][:, 16 - sh:32 - sh], ALU.add))
            incl = pre[4][:, 16:]
            link(tt(n16[7], incl, n16[1], ALU.subtract))
            link(ts(n16[7], n16[7], NE - 1.0, ALU.add, float(CAP), ALU.mult))
            link(tt(n16[7], n16[7], base_id, ALU.subtract))
            link(ts(e64[4], x64, CAP - 0.5, ALU.is_gt))
            link(tt(e64[4], e64[4], ts4(n16[7]), ALU.mult))
            link(tt(e64[4], e64[4], ts4(base_id), ALU.add))
            link(tt(e64[4], e64[4], x64, ALU.add))
            for n in range(2):
                link(tt(e64[5], e64[4], e64[1 + n], ALU.mult))
                link(V.tensor_reduce(out=slot_f[:, n, :], in_=e64[5], axis=AX.X, op=ALU.add))
            V.tensor_copy(slot_i[:, :, :], slot_f).then_inc(slots_ready, 1)
            link(tt(o_lt, incl.unsqueeze(1).to_broadcast([P, N_OVER, NE]), o_k, ALU.is_lt))
            link(V.tensor_reduce(out=tile_row[:, 0:N_OVER], in_=o_lt, axis=AX.X, op=ALU.add))
            link(V.tensor_copy(tile_row[:, N_OVER:N_OVER + 1], incl[:, NE - 1:NE]))
            link(ts(tile_row[:, 0:N_OVER], tile_row[:, 0:N_OVER], NE - 1.0, ALU.min))
            V.tensor_copy(tile_i[:, 0:N_OVER + 1], tile_row[:, 0:N_OVER + 1]).then_inc(tiles_ready, 1)

            dve.sem_inc(hid_ready, 2)
            dve.sem_inc(zs_ready, 1)
            dve.sem_inc(y_dve, 1)
            dve.wait_ge(z_stored, 16 * NT)

            def rows_transposed(e, a):
                dve.wait_ge(xg_used, e + 1)
                V.tensor_copy(zsT[a][:, 0:4, :], bank[0][:, 0:4 * CAP].rearrange("p (k t) -> p k t", k=4))
                V.tensor_copy(zsT[a][:, 4:8, :], bank[1][:, 0:4 * CAP].rearrange("p (k t) -> p k t", k=4)).then_inc(zs_ready, 1)

            def expert(e, a):
                for c in range(2):
                    half = slice(2048 * c, 2048 * (c + 1))
                    s_ = expert_slot(a, 2)
                    dve.wait_ge(w2_hi, 2 * e + c + 1)
                    lo_of(ring_r[s_][:, half], ring[s_][:, half], ureg_r[:, half]).then_inc(w2_lo, 1)
                dve.wait_ge(silu_ready, e + 3)
                for c, (k0, k1) in enumerate(((0, 3), (3, 4))):
                    dve.wait_ge(gate_done, 2 * e + c + 1)
                    part = slice(k0 * CAP, k1 * CAP)
                    b = bank[3 + 4 * a][:, part] if c == 0 else bank[2 + 4 * a][:, 4 * CAP:5 * CAP]
                    tt(hid[a][:, k0:k1, :].rearrange("p k t -> p (k t)"), silu[a][:, part], b, ALU.mult).then_inc(hid_exact, 1)
                    dve.wait_ge(hid_exact, 2 * e + c + 1)
                    V.tensor_copy(hid_hi[a][:, k0:k1, :], hid[a][:, k0:k1, :]).then_inc(hid_rounded, 1)
                    dve.wait_ge(hid_rounded, 2 * e + c + 1)
                    ins = lo_of(hid_lo[a][:, k0:k1, :], hid[a][:, k0:k1, :], hid_hi[a][:, k0:k1, :])
                ins.then_inc(hid_ready, 1)

            def left(e, a, n_st):
                dve.wait_ge(down_done, 2 * e + 1)
                if n_st is not None:
                    dve.wait_ge(y_stored[a], n_st)
                V.tensor_copy(ysb[a][:, 0:HALF], bank[4][0:CAP, :]).then_inc(y_dve, 1)

            rows_transposed(0, 0)
            expert(0, 0)
            rows_transposed(1, 1)
            left(0, 0, None)
            expert(1, 1)
            rows_transposed(2, 0)
            left(1, 1, None)
            with dve.Fori(1, NE // 2 - 1) as i:
                for a in range(2):
                    expert(2 * i + a, a)
                    rows_transposed(2 * i + a + 1, 1 - a)
                    left(2 * i + a, a, 16 * i)
            expert(NE - 2, 0)
            rows_transposed(NE - 1, 1)
            left(NE - 2, 0, 8 * (NE - 2))
            expert(NE - 1, 1)
            left(NE - 1, 1, 8 * (NE - 2))
            dve.wait_ge(tiles_ready, 1)
            n_over = dve.value_load(tile_i[0:1, N_OVER:N_OVER + 1], min_val=0, max_val=N_OVER)
            with dve.If(n_over > 0):
                with dve.Fori(0, n_over) as k:
                    dve.wait_ge(o_xT, k + 1)
                    V.tensor_copy(zsT[0][:, 0:4, :], bank[0][:, 0:4 * CAP].rearrange("p (k t) -> p k t", k=4))
                    V.tensor_copy(zsT[0][:, 4:8, :], bank[1][:, 0:4 * CAP].rearrange("p (k t) -> p k t", k=4)).then_inc(o_zs, 1)
                    dve.wait_ge(o_silu, k + 1)
                    dve.wait_ge(o_gate, k + 1)
                    tt(hid[0].rearrange("p k t -> p (k t)"), silu[0], bank[3][:, 0:4 * CAP], ALU.mult).then_inc(o_hid, 1)
                    dve.wait_ge(o_down, k + 2)
                    dve.wait_ge(y_stored[0], 8 * NE)
                    V.tensor_copy(ysb[0][:, 0:HALF], bank[4][0:CAP, :])
                    V.tensor_copy(ysb[0][:, HALF:D], bank[5][0:CAP, :]).then_inc(o_y, 1)
                dve.nop()
            with dve.Else():
                dve.nop()
            for q in range(2):
                for t in (2 * q, 2 * q + 1):
                    dve.wait_ge(back[t], 32)
                    link(V.scalar_tensor_tensor(out=h[:, t, :], in0=yg1[t], scalar=gw[:, 0, t:t + 1], in1=h[:, t, :], op0=ALU.mult, op1=ALU.add))
                    V.scalar_tensor_tensor(out=h[:, t, :], in0=yg2[t], scalar=gw[:, 1, t:t + 1], in1=h[:, t, :], op0=ALU.mult, op1=ALU.add).then_inc(combined, 1)
                dve.wait_ge(o_squared, 2 * q + 2)
                rstd(rs_z[:, 2 * q:2 * q + 2], ss_o[:, 2 * q:2 * q + 2], o_rstd)
                dve.wait_ge(o_rstd, q + 1)
                for t in (2 * q, 2 * q + 1):
                    V.scalar_tensor_tensor(out=yg1[t], in0=h[:, t, :], scalar=rs_z[:, t:t + 1], in1=gain_fin, op0=ALU.mult, op1=ALU.mult).then_inc(out_ready, 1)

        @block.tensor
        def _(pe):
            def claim(name, i):
                n = AT[name, i]
                assert ORDER[n][:2] == (name, i) and n == claimed[0]
                claimed[0] += 1
                if n >= BANKS:
                    pe.wait_ge(*drained(*ORDER[n - BANKS][:2]))
                return bank[n % BANKS]

            claimed = [0]

            def mm(o_, l_, r_, first, last):
                return nc.tensor.matmul(o_, lhsT=l_, rhs=r_, start=first, stop=last)

            def tr(o_, i_, p=P):
                return nc.tensor.transpose(o_, i_, ident[0:p, 0:p])

            def rows_to_columns(name, src, t):
                for n in range(2):
                    b = claim(name, 2 * t + n)
                    for k in range(4):
                        ins = tr(b[:, P * k:P * (k + 1)], src[:, t, P * (4 * n + k):P * (4 * n + k + 1)])
                    ins.then_inc(psum_filled, 1)

            def project(name, i, w, m, act_in, nk=KD):
                b = claim(name, i)
                for k in range(nk):
                    ins = mm(b[:, :], w[:, k, P * m:P * (m + 1)], act_in[:, k, :], k == 0, k == nk - 1)
                ins.then_inc(psum_filled, 1)

            def three(o_, l_, r_, at_l, at_r, first, last):
                mm(o_, l_[0][at_l], r_[0][at_r], first, False)
                mm(o_, l_[0][at_l], r_[1][at_r], False, False)
                return mm(o_, l_[1][at_l], r_[0][at_r], False, last)

            def project_split(name, i, w, m, act_in, nk=KD):
                b = claim(name, i)
                for k in range(nk):
                    ins = three(b[:, :], w, act_in, (slice(None), k, slice(P * m, P * (m + 1))), (slice(None), k), k == 0, k == nk - 1)
                ins.then_inc(psum_filled, 1)

            def weights_split(name):
                j = SPLIT.index(name)
                if j < 4:
                    pe.wait_ge(kv_lo, 2 * j + 2)
                else:
                    pe.wait_ge(weight_lo, 2 * j - 6)

            pe.wait_ge(consts_ready, 1)
            for t in range(NT):
                pe.wait_ge(x_normed, t + 1)
                rows_to_columns("xT", h, t)
            pe.wait_ge(*loaded("v"))
            pe.wait_ge(*drained("xT", 7))
            for m in range(2):
                project("v", m, chunk("v", 8), m, uT)
            pe.wait_ge(lam_ready, 1)
            b = claim("lam", 0)
            for n in range(4):
                ins = tr(b[:, SSM_G * n:SSM_G * (n + 1)], lamq[:, n, :, :].rearrange("p x n -> p (x n)"), SSM_G)
            ins.then_inc(psum_filled, 1)
            pe.wait_ge(ssmb_loaded, 64)
            b = claim("cT", 0)
            for n in range(4):
                ins = tr(b[:, P * n:P * (n + 1)], cload[:, n, :])
            ins.then_inc(psum_filled, 1)
            for m in range(2, 4):
                project("v", m, chunk("v", 8), m, uT)
            pe.wait_ge(*loaded("z"))
            for m in range(4):
                project("zp", m, chunk("z", 8), m, uT)
            for t in range(MT):
                pe.wait_ge(mem_normed, t + 1)
                rows_to_columns("memT", mem_tok, t)
            pe.wait_ge(powers_ready, 1)
            for q in range(8):
                b = claim("bT", q)
                for n in range(4):
                    ins = tr(b[:, P * n:P * (n + 1)], bpow_m[:, 4 * q + n, :])
                ins.then_inc(psum_filled, 1)
            for q in range(8):
                b = claim("kern", q)
                for n in range(4):
                    gg = 4 * q + n
                    Bg, o_ = gc(Bb)[:, gg, :], b[0:SSM_C, P * n:P * (n + 1)]
                    mm(o_[:, 0:SSM_C], Bg, gc(Cy)[:, gg, :], True, True)
                    ins = mm(o_[:, SSM_C:P], Bg, cpow_m[:, gg, 0:P - SSM_C], True, True)
                ins.then_inc(psum_filled, 1)
            pe.wait_ge(*drained("v", 3))
            for l in range(LCH):
                b = claim("vl", l)
                for m in range(4):
                    ins = tr(b[0:NCH, P * m:P * (m + 1)], vT[:, m, :].rearrange("p (j l) -> p l j", l=LCH)[:, l, :])
                ins.then_inc(psum_filled, 1)
            pe.wait_ge(*drained("vl", 7))
            for q in range(4):
                b = claim("vch", q)
                for n in range(8):
                    ins = tr(b[:, NCH * n:NCH * (n + 1)], vj_m[:, 8 * q + n, :], NCH)
                ins.then_inc(psum_filled, 1)
            for q in range(4):
                b = claim("st", q)
                pe.wait_ge(*drained("vch", q))
                for n in range(8):
                    ins = mm(b[:, NCH * n:NCH * (n + 1)], bpow_m[:, 8 * q + n, :], vch[:, 8 * q + n, :], True, True)
                ins.then_inc(psum_filled, 1)
            pe.wait_ge(poolw_loaded, 16)
            for g_ in range(POOL_G):
                pe.wait_ge(pool_diff, g_ + 1)
                b = claim("mix", g_)
                mm(b[:, :], poolw[:, g_, :], zp[:, g_, PADT:], True, True).then_inc(psum_filled, 1)
            pe.wait_ge(mem_split, 2)
            for m in range(4):
                if m % 2 == 0:
                    weights_split(f"k{m // 2}")
                w = parts(f"k{m // 2}", 8)
                b = claim("kk", m)
                for s in range(2):
                    c = 2 * (m % 2) + s
                    for k in range(KD):
                        ins = three(b[:, MEM * s:MEM * (s + 1)], w, (mem_hi, mem_lo), (slice(None), k, slice(P * c, P * (c + 1))),
                                    (slice(None), k), k == 0, k == KD - 1)
                ins.then_inc(psum_filled, 1)
            for n in range(4):
                if n % 2 == 0:
                    weights_split(f"v{n // 2}")
                b = claim("vv", n)
                for k in range(KD):
                    ins = three(b[:, :], (mem_hi, mem_lo), parts(f"v{n // 2}", 8), (slice(None), k, slice(P * (n % 2), P * (n % 2 + 1))),
                                (slice(None), k), k == 0, k == KD - 1)
                ins.then_inc(psum_filled, 1)
            pe.wait_ge(*loaded("toep"))
            pe.wait_ge(states_ready, 1)
            toep = ring[CH["toep"] % RAW][:, :].rearrange("p (g x) -> p g x", g=SSM_G)
            for q in range(8):
                b = claim("y", q)
                for n in range(4):
                    gg = 4 * q + n
                    mm(b[0:NCH, P * n:P * (n + 1)], vch[:, gg, :], toep[:, gg, :], True, False)
                    ins = mm(b[0:NCH, P * n:P * (n + 1)], hin[:, gg, 1, :], cpow_m[:, gg, :], False, True)
                ins.then_inc(psum_filled, 1)

            def gates(lo, hi):
                for m in range(lo, hi):
                    if m % 4 == 0:
                        weights_split(f"g{m // 4}")
                    project_split("gate", m, parts(f"g{m // 4}", 8), m % 4, (u_hi, u_lo))

            pe.wait_ge(u_split, KD)
            gates(0, 4)
            pe.wait_ge(*drained("y", 7))
            for m in range(4):
                b = claim("yT", m)
                for l in range(LCH):
                    ins = tr(b[:, NCH * l:NCH * (l + 1)], yj[:, m, l, :], NCH)
                ins.then_inc(psum_filled, 1)
            gates(4, 8)
            pe.wait_ge(*loaded("glu"))
            pe.wait_ge(gelu_ready, 4)
            for m in range(4):
                project("glu", m, chunk("glu", 4), m, ygT, 4)
            gates(8, 16)
            weights_split("bp")
            pe.wait_ge(yp_split, 4)
            for m in range(KD):
                project_split("bp", m, parts("bp", 4), m, (yp_hi, yp_lo), 4)
            weights_split("bs")
            pe.wait_ge(ys_split, 4)
            for m in range(KD):
                project_split("bs", m, parts("bs", 4), m, (ys_hi, ys_lo), 4)
            pe.wait_ge(merged_ready, KD)

            def by_rows(name, i, src, w):
                t, n = i // 2, i % 2
                if t == 0:
                    weights_split(w[n])
                b = claim(name, i)
                for k in range(KD):
                    ins = three(b[:, :], src, parts(w[n], 8), (slice(None), k, slice(P * t, P * (t + 1))), (slice(None), k), k == 0, k == KD - 1)
                ins.then_inc(psum_filled, 1)

            for banks_, t in ROWS:
                for i in banks_:
                    by_rows("wo1", i, (mg_hi, mg_lo), ("o0", "o1"))
                if t is not None:
                    pe.wait_ge(*drained("wo1", 2 * t + 1))
                    rows_to_columns("hT", h, t)
            pe.wait_ge(hn_split, 2 * NT)
            pe.wait_ge(*drained("vv", 3))
            for hd in range(HEADS + 1):
                o_ = hd - 1
                if hd < HEADS:
                    for m in Q_AHEAD[hd]:
                        if m % 4 == 0:
                            weights_split(f"q{m // 4}")
                        project_split("q", m, parts(f"q{m // 4}", 8), m % 4, (hn_hi, hn_lo))
                if hd >= 1:
                    pe.wait_ge(prob_ready, 2 * o_ + 2)
                    for n in range(2):
                        b = claim("pT", 2 * o_ + n)
                        for t in range(NT):
                            ins = tr(b[:, P * t:P * (t + 1)], prob[:, o_ % 2, t, P * n:P * (n + 1)])
                        ins.then_inc(psum_filled, 1)
                if hd < HEADS:
                    pe.wait_ge(*drained("q", 2 * hd + 1))
                    for n in range(2):
                        b = claim("sc", 2 * hd + n)
                        for s in range(2):
                            t = 2 * n + s
                            for k in range(2):
                                ins = mm(b[:, MEM * s:MEM * (s + 1)], qT[:, 2 * hd + k, P * t:P * (t + 1)], kT[:, 2 * hd + k, :], k == 0, k == 1)
                        ins.then_inc(psum_filled, 1)
                if hd >= 1:
                    pe.wait_ge(*drained("pT", 2 * o_ + 1))
                    for n in range(2):
                        b = claim("pv", 2 * o_ + n)
                        for k in range(MT):
                            ins = mm(b[:, :], vm[:, k, HD * o_ + P * n:HD * o_ + P * (n + 1)], probT[:, o_ % 2, k, :], k == 0, k == MT - 1)
                        ins.then_inc(psum_filled, 1)
            pe.wait_ge(o_split, KD)

            def route(t):
                b = claim("route", t)
                if t == 0:
                    pe.wait_ge(router_scaled, 1)
                pe.wait_ge(*drained("zT", 2 * t + 1))
                for k in range(KD):
                    ins = mm(b[:, 0:20], zT[:, k, P * t:P * (t + 1)], rw[:, k, :], k == 0, k == KD - 1)
                ins.then_inc(psum_filled, 1)

            for t in range(NT):
                for i in WO2[t]:
                    by_rows("wo2", i, (o_hi, o_lo), ("w0", "w1"))
                if t >= 2:
                    route(t - 2)
                if t >= 1:
                    pe.wait_ge(*drained("wo2", 2 * t - 1))
                    rows_to_columns("zT", h, t - 1)
            route(NT - 2)
            pe.wait_ge(*drained("wo2", 2 * NT - 1))
            rows_to_columns("zT", h, NT - 1)
            route(NT - 1)
            pe.wait_ge(mask_ready, 1)
            pe.wait_ge(masks_ready, 1)
            b = claim("rank", 0)
            mm(b[:, 0:64], before[:, :], e64[3].rearrange("p t n -> p (t n)"), True, False)
            mm(b[:, 0:64], ones[:, :], m_cum[:, 0:64], False, True)
            mm(b[:, 64:80], ones[:, :], m_cum[:, 64:80], True, True).then_inc(psum_filled, 1)
            pe.wait_ge(at_rank_ready, 1)
            b = claim("index", 0)
            for n in range(2):
                for t in range(NT):
                    ins = mm(b[0:CAP, 0:NE], at_rank[:, n, t, :], tok_of[:, n, t, :], n + t == 0, n + t == NT)
            ins.then_inc(psum_filled, 1)
            pe.wait_ge(*drained("rank", 0))
            pe.wait_ge(*drained("index", 0))

            def transposes(e, a, n_g):
                pe.wait_ge(gathered[a], n_g)
                pe.wait_ge(zs_ready, e + 1)
                for k in range(KD):
                    ins = tr(bank[k // 4][:, CAP * (k % 4):CAP * (k % 4 + 1)], xg[a][:, P * k:P * (k + 1)], CAP)
                ins.then_inc(xg_used, 1)

            def up(a, s, b_, n_w, ms, done):
                pe.wait_ge(slot_loaded[s], n_w)
                w = expert_chunk(s, 8)
                for n, m in enumerate(ms):
                    for k in range(KD):
                        ins = mm(b_[:, CAP * n:CAP * (n + 1)], w[:, k, P * m:P * (m + 1)], zsT[a][:, k, :], k == 0, k == KD - 1)
                ins.then_inc(done, 1)

            def expert(e, a, i, n_next):
                s0, s1, s2 = (expert_slot(a, c) for c in range(3))
                pe.wait_ge(zs_ready, e + 2)
                pe.wait_ge(silu_ready, e + 1)
                up(a, s0, bank[2 + 4 * a], front_loads[s0] + 16 * i + 16, range(4), up_done)
                pe.wait_ge(hid_ready, e + 1)
                up(a, s1, bank[3 + 4 * a], front_loads[s1] + 16 * i + 16, range(3), gate_done)
                pe.wait_ge(silu_ready, e + 3)
                up(a, s1, bank[2 + 4 * a][:, 4 * CAP:5 * CAP], front_loads[s1] + 16 * i + 16, (3,), gate_done)
                if n_next is not None:
                    transposes(e + 1, 1 - a, n_next)
                pe.wait_ge(w2_lo, 2 * e + 2)
                pe.wait_ge(hid_ready, e + 3)
                w = [r.rearrange("p (k n) -> p k n", k=4) for r in (ureg_r[:, :], ring_r[s2][:, :])]
                for n, drained_by in ((0, y_dve), (1, y_act)):
                    pe.wait_ge(drained_by, e + 1)
                    for k in range(4):
                        ins = three(bank[4 + n][0:CAP, :], (hid_hi[a], hid_lo[a]), w, (slice(None), k),
                                    (slice(None), k, slice(HALF * n, HALF * (n + 1))), k == 0, k == 3)
                    ins.then_inc(down_done, 1)

            transposes(0, 0, 16)
            with pe.Fori(0, NE // 2 - 1) as i:
                expert(2 * i, 0, i, 16 * i + 16)
                expert(2 * i + 1, 1, i, 16 * i + 32)
            last = NE // 2 - 1
            expert(NE - 2, 0, last, 16 * last + 16)
            expert(NE - 1, 1, last, None)
            pe.sem_inc(o_down, 1)
            pe.wait_ge(y_dve, NE + 1)
            pe.wait_ge(y_act, NE + 1)
            pe.wait_ge(tiles_ready, 1)
            n_over = pe.value_load(tile_i[0:1, N_OVER:N_OVER + 1], min_val=0, max_val=N_OVER)
            with pe.If(n_over > 0):
                with pe.Fori(0, n_over) as k:
                    pe.wait_ge(o_gath, 16 * k + 16)
                    for kk in range(KD):
                        ins = tr(bank[kk // 4][:, CAP * (kk % 4):CAP * (kk % 4 + 1)], xg[0][:, P * kk:P * (kk + 1)], CAP)
                    ins.then_inc(o_xT, 1)
                    pe.wait_ge(o_zs, k + 1)
                    pe.wait_ge(o_w, 48 * k + 48)
                    for c, done in ((0, o_up), (1, o_gate)):
                        w = expert_chunk(c, 8)
                        for m in range(4):
                            for kk in range(KD):
                                ins = mm(bank[2 + c][:, CAP * m:CAP * (m + 1)], w[:, kk, P * m:P * (m + 1)], zsT[0][:, kk, :], kk == 0, kk == KD - 1)
                        ins.then_inc(done, 1)
                    pe.wait_ge(o_hid, k + 1)
                    w = expert_chunk(2, 4)
                    for n in range(2):
                        for kk in range(4):
                            ins = mm(bank[4 + n][0:CAP, :], hid[0][:, kk, :], w[:, kk, HALF * n:HALF * (n + 1)], kk == 0, kk == 3)
                    ins.then_inc(o_down, 1)
                    pe.wait_ge(o_y, k + 1)
                pe.nop()
            with pe.Else():
                pe.nop()


_INS = ['x', 'mem', 'norm_mix', 'w_in', 'pool_w', 'pool_scale', 'ssm_a_re', 'ssm_a_im', 'ssm_log_dt', 'ssm_b_re', 'ssm_b_im', 'ssm_c_re', 'ssm_c_im', 'ssm_d', 'glu_w', 'glu_b', 'br_pool', 'br_ssm', 'w_out', 'norm_x', 'norm_mem', 'x_wq', 'x_wkv', 'x_wo', 'norm_ffn', 'router_g_w', 'router_g_b', 'router_e_w', 'router_e_b', 'exp_w1', 'exp_w3', 'exp_w2', 'norm_final']
_OUTS = [((1, SEQ, D), 'float32')]


def kernel(**inputs):
    import numpy as _np
    import concourse.bacc as _bacc
    from concourse import mybir as _mybir
    from concourse.bass_utils import run_bass_kernel_spmd as _run

    nc = _bacc.Bacc("TRN2", target_bir_lowering=False, num_devices=1)
    arrays, args = {}, []
    for name in _INS:
        a = _np.ascontiguousarray(inputs[name])
        arrays[f"in_{name}_dram"] = a
        args.append(nc.dram_tensor(f"in_{name}_dram", a.shape, _mybir.dt.from_np(a.dtype), kind="ExternalInput").ap())
    for i, (shape, dtype) in enumerate(_OUTS):
        dt = _mybir.dt.from_np(_np.dtype(dtype))
        args.append(nc.dram_tensor(f"out_{i}_dram", shape, dt, kind="ExternalOutput").ap())
    bass_hybrid_decoder_layer(nc, *args)
    r = _run(nc, [arrays], core_ids=[0])
    return r.results[0]["out_0_dram"]
```
